# Optimizing a Trainium2 kernel written in Bass

```python
import math
import numpy as np
import jax
import jax.numpy as jnp
from jax import lax
import jax, jax.numpy as jnp

D_MODEL = 1024
BATCH = 1
SEQ = 1024
DEPTH = 1

GRID_W = 64
CTX_LEN = 256

RWKV_WIDTH = 512
RWKV_HEAD = 64
RWKV_HEADS = RWKV_WIDTH // RWKV_HEAD
DECAY_LORA = 32
AAA_LORA = 32
GATE_LORA = 96
DIFF_WIDTH = D_MODEL - RWKV_WIDTH
DIFF_HEAD = 64
DIFF_HEADS = DIFF_WIDTH // (2 * DIFF_HEAD)
D_FF = 2816
CONV_W = 3
Q_BLOCK = 128
ROPE_THETA = 10000.0
NORM_EPS = 1e-6
LN_X_EPS = 64e-5
SUBLN_EPS = 1e-5
ATTN_SCALE = DIFF_HEAD ** -0.5

RWKV_SPLITS = (RWKV_WIDTH, 2 * RWKV_WIDTH, 3 * RWKV_WIDTH,
               3 * RWKV_WIDTH + DECAY_LORA, 3 * RWKV_WIDTH + DECAY_LORA + AAA_LORA)
RWKV_COLS = 3 * RWKV_WIDTH + DECAY_LORA + AAA_LORA + GATE_LORA
DIFF_QK = DIFF_HEADS * 2 * DIFF_HEAD
DIFF_V = DIFF_HEADS * 2 * DIFF_HEAD
IN_COLS = RWKV_COLS + 2 * DIFF_QK + DIFF_V


def rmsnorm(x, g, eps=NORM_EPS):
    xf = x.astype(jnp.float32)
    y = xf * lax.rsqrt(jnp.mean(xf * xf, axis=-1, keepdims=True) + eps)
    return (y * g.astype(jnp.float32)).astype(x.dtype)

def modulate(h, shift, scale):
    return h * (1.0 + scale) + shift

def adaln(cond, w_mod, b_mod):
    return jax.nn.silu(cond) @ w_mod + b_mod

def dwconv(x, w):
    return lax.conv_general_dilated(
        x, w[:, None, :].astype(x.dtype), window_strides=(1,),
        padding=((CONV_W // 2, CONV_W // 2),),
        dimension_numbers=('NWC', 'WIO', 'NWC'),
        feature_group_count=x.shape[-1])

def axial_rope(rows):
    n_pair = DIFF_HEAD // 4
    row = jnp.repeat(jnp.arange(rows, dtype=jnp.float32), GRID_W)
    col = jnp.tile(jnp.arange(GRID_W, dtype=jnp.float32), rows)
    inv = ROPE_THETA ** (-jnp.arange(n_pair, dtype=jnp.float32) / n_pair)
    ang = jnp.concatenate([row[:, None] * inv, col[:, None] * inv], axis=-1)
    return jnp.cos(ang), jnp.sin(ang)

def apply_rope(x, cos, sin):
    half = DIFF_HEAD // 2
    x1, x2 = x[..., :half], x[..., half:]
    return jnp.concatenate([x1 * cos - x2 * sin, x1 * sin + x2 * cos], axis=-1).astype(x.dtype)

def rwkv_prepare(rw, p):
    B, T, _ = rw.shape
    heads = lambda t: t.reshape(B, T, RWKV_HEADS, RWKV_HEAD)
    r, k, v, wl, al, gl = jnp.split(rw, RWKV_SPLITS, axis=-1)
    kk = heads(k * p['k_k']).astype(jnp.float32)
    kk = kk / jnp.maximum(jnp.linalg.norm(kk, axis=-1, keepdims=True), 1e-12)
    w_lat = jnp.tanh(wl)
    dirs = []
    for w0, w2, a0, a2 in ((p['w0_fwd'], p['w2_fwd'], p['a0_fwd'], p['a2_fwd']),
                           (p['w0_bwd'], p['w2_bwd'], p['a0_bwd'], p['a2_bwd'])):
        w = -jax.nn.softplus(-(w0 + w_lat @ w2).astype(jnp.float32)) - 0.5
        decay = jnp.exp(-jnp.exp(w))
        a = jax.nn.sigmoid((a0 + al @ a2).astype(jnp.float32))
        k_dir = k * (1.0 + (a - 1.0) * p['k_a'])
        dirs.append((heads(decay), heads(k_dir), heads(a)))
    return heads(r), heads(v), kk, gl, dirs

def rwkv_scan(r, decay, k, v, kk, a, s0, reverse):
    tm = lambda t: jnp.swapaxes(t, 0, 1)

    def step(S, inp):
        r_t, w_t, k_t, v_t, kk_t, b_t = inp
        sa = jnp.einsum('bhvk,bhk->bhv', S, kk_t)
        S = (S * w_t[:, :, None, :] - sa[..., None] * b_t[:, :, None, :]
             + v_t[..., None] * k_t[:, :, None, :])
        return S, jnp.einsum('bhvk,bhk->bhv', S, r_t)

    s_fin, ys = lax.scan(step, s0, (tm(r), tm(decay), tm(k), tm(v), tm(kk), tm(kk * a)),
                         reverse=reverse)
    return tm(ys), s_fin

def rwkv_output(y, r, v, k_bonus, gl, p):
    B, T = y.shape[:2]
    mu = jnp.mean(y, axis=-1, keepdims=True)
    var = jnp.mean(jnp.square(y - mu), axis=-1, keepdims=True)
    yn = ((y - mu) * lax.rsqrt(var + LN_X_EPS)).reshape(B, T, RWKV_WIDTH) * p['ln_x_w'] + p['ln_x_b']
    bonus = (jnp.sum(r * k_bonus * p['r_k'], axis=-1, keepdims=True) * v).reshape(B, T, RWKV_WIDTH)
    g = jax.nn.sigmoid(gl) @ p['g2']
    return ((yn + bonus) * g).astype(r.dtype)

def rwkv_mixer(rw, rw_c, p, need_ctx):
    r, v, kk, gl, dirs = rwkv_prepare(rw, p)
    r_c, v_c, kk_c, gl_c, dirs_c = rwkv_prepare(rw_c, p)
    s0 = jnp.zeros((rw.shape[0], RWKV_HEADS, RWKV_HEAD, RWKV_HEAD), jnp.float32)
    ys, ys_c = [], []
    for d, reverse in enumerate((False, True)):
        dec_c, k_c, a_c = dirs_c[d]
        yd_c, s_ctx = rwkv_scan(r_c, dec_c, k_c, v_c, kk_c, a_c, s0, reverse)
        dec, k_d, a_d = dirs[d]
        yd, _ = rwkv_scan(r, dec, k_d, v, kk, a_d, s_ctx, reverse)
        ys.append(yd)
        ys_c.append(yd_c)
    out = rwkv_output(ys[0] + ys[1], r, v, 0.5 * (dirs[0][1] + dirs[1][1]), gl, p)
    out_c = (rwkv_output(ys_c[0] + ys_c[1], r_c, v_c, 0.5 * (dirs_c[0][1] + dirs_c[1][1]), gl_c, p)
             if need_ctx else None)
    return out, out_c

def diff_split(dq):
    B, T, _ = dq.shape
    q, k, v = jnp.split(dq, (DIFF_QK, 2 * DIFF_QK), axis=-1)
    qk = lambda t: t.reshape(B, T, DIFF_HEADS, 2, DIFF_HEAD).transpose(0, 2, 3, 1, 4)
    return qk(q), qk(k), v.reshape(B, T, DIFF_HEADS, 2 * DIFF_HEAD).transpose(0, 2, 1, 3)

def diff_attention(q, k_all, v_all, lam):
    s = jnp.einsum('bhmqd,bhmkd->bhmqk', q, k_all).astype(jnp.float32) * ATTN_SCALE
    pr = jax.nn.softmax(s, axis=-1)
    a = pr[:, :, 0] - lam * pr[:, :, 1]
    return jnp.einsum('bhqk,bhke->bhqe', a.astype(v_all.dtype), v_all)

def diff_post(o, p, lam_init):
    B, H, T, e = o.shape
    o = rmsnorm(o, p['subln_w'], SUBLN_EPS) * (1.0 - lam_init)
    return o.transpose(0, 2, 1, 3).reshape(B, T, H * e)

def diff_mixer(dq, dq_c, p, lam_init, cos, sin, need_ctx):
    q, k, v = diff_split(dq)
    q_c, k_c, v_c = diff_split(dq_c)
    q, k = apply_rope(q, cos, sin), apply_rope(k, cos, sin)
    f32 = lambda t: t.astype(jnp.float32)
    lam = (jnp.exp(jnp.sum(f32(p['lam_q1']) * f32(p['lam_k1'])))
           - jnp.exp(jnp.sum(f32(p['lam_q2']) * f32(p['lam_k2']))) + lam_init)
    k_all = jnp.concatenate([k_c, k], axis=3)
    v_all = jnp.concatenate([v_c, v], axis=2)
    B, H, _, T, d = q.shape
    nb = T // Q_BLOCK
    qb = q.reshape(B, H, 2, nb, Q_BLOCK, d).transpose(3, 0, 1, 2, 4, 5)
    o = lax.map(lambda qq: diff_attention(qq, k_all, v_all, lam), qb)
    o = o.transpose(1, 2, 0, 3, 4).reshape(B, H, T, 2 * d)
    out = diff_post(o, p, lam_init)
    out_c = diff_post(diff_attention(q_c, k_c, v_c, lam), p, lam_init) if need_ctx else None
    return out, out_c

def token_mixer(h, h_c, p, lam_init, cos, sin, need_ctx):
    parts = h @ p['w_in']
    parts_c = h_c @ p['w_in']
    rw = dwconv(parts[..., :RWKV_COLS], p['rwkv_conv'])
    rw_c = dwconv(parts_c[..., :RWKV_COLS], p['rwkv_conv'])
    y_r, y_r_c = rwkv_mixer(rw, rw_c, p, need_ctx)
    y_d, y_d_c = diff_mixer(parts[..., RWKV_COLS:], parts_c[..., RWKV_COLS:], p, lam_init,
                            cos, sin, need_ctx)
    out = jnp.concatenate([y_r, y_d], axis=-1) @ p['w_out']
    out_c = jnp.concatenate([y_r_c, y_d_c], axis=-1) @ p['w_out'] if need_ctx else None
    return out, out_c

def conv_ffn(h, p):
    u = dwconv(h @ p['w_up'], p['ffn_conv']) + p['ffn_conv_b']
    val, gate = jnp.split(u, 2, axis=-1)
    return (val * jax.nn.silu(gate)) @ p['w_down']

def first_inputs(seed: int = 0) -> dict:
    key = jax.random.key(seed)
    keys = jax.random.split(key, 36)
    L, D, Rw = DEPTH, D_MODEL, RWKV_WIDTH

    def nrm(i, shape, s):
        return s * jax.random.normal(keys[i], shape, jnp.float32)

    def uni(i, shape, lo, hi):
        return jax.random.uniform(keys[i], shape, jnp.float32, lo, hi)

    conv_base = jnp.array([0.25, 0.5, 0.25], jnp.float32)[None, :, None]
    return {
        'x': nrm(0, (BATCH, SEQ, D), 1.0),
        'c': nrm(1, (BATCH, D), 1.0),
        'ctx': nrm(2, (BATCH, CTX_LEN, D), 1.0),
        'c_ctx': nrm(3, (D,), 1.0),
        'w_mod': nrm(4, (L, D, 6 * D), 0.5 * D ** -0.5),
        'b_mod': nrm(5, (L, 6 * D), 0.02),
        'g_pre_mix': 1.0 + nrm(6, (L, D), 0.05),
        'g_post_mix': 1.0 + nrm(7, (L, D), 0.05),
        'g_pre_ffn': 1.0 + nrm(8, (L, D), 0.05),
        'g_post_ffn': 1.0 + nrm(9, (L, D), 0.05),
        'w_in': nrm(10, (L, D, IN_COLS), D ** -0.5),
        'rwkv_conv': conv_base + nrm(11, (L, CONV_W, RWKV_COLS), 0.1),
        'w0_fwd': uni(12, (L, Rw), -6.5, -1.5),
        'w2_fwd': nrm(13, (L, DECAY_LORA, Rw), 0.1),
        'a0_fwd': nrm(14, (L, Rw), 0.1),
        'a2_fwd': nrm(15, (L, AAA_LORA, Rw), 0.1),
        'w0_bwd': uni(16, (L, Rw), -6.5, -1.5),
        'w2_bwd': nrm(17, (L, DECAY_LORA, Rw), 0.1),
        'a0_bwd': nrm(18, (L, Rw), 0.1),
        'a2_bwd': nrm(19, (L, AAA_LORA, Rw), 0.1),
        'g2': nrm(20, (L, GATE_LORA, Rw), GATE_LORA ** -0.5),
        'k_k': 0.85 + nrm(21, (L, Rw), 0.05),
        'k_a': 1.0 + nrm(22, (L, Rw), 0.05),
        'r_k': nrm(23, (L, RWKV_HEADS, RWKV_HEAD), 0.1),
        'ln_x_w': 1.0 + nrm(24, (L, Rw), 0.05),
        'ln_x_b': nrm(25, (L, Rw), 0.02),
        'lam_q1': nrm(26, (L, DIFF_HEAD), 0.1),
        'lam_k1': nrm(27, (L, DIFF_HEAD), 0.1),
        'lam_q2': nrm(28, (L, DIFF_HEAD), 0.1),
        'lam_k2': nrm(29, (L, DIFF_HEAD), 0.1),
        'subln_w': 1.0 + nrm(30, (L, 2 * DIFF_HEAD), 0.05),
        'w_out': nrm(31, (L, D, D), D ** -0.5),
        'w_up': nrm(32, (L, D, 2 * D_FF), D ** -0.5),
        'ffn_conv': conv_base + nrm(33, (L, CONV_W, 2 * D_FF), 0.1),
        'ffn_conv_b': nrm(34, (L, 2 * D_FF), 0.02),
        'w_down': nrm(35, (L, D_FF, D), D_FF ** -0.5),
    }

def first_block(x, c, ctx, c_ctx, w_mod, b_mod, g_pre_mix, g_post_mix, g_pre_ffn, g_post_ffn,
              w_in, rwkv_conv, w0_fwd, w2_fwd, a0_fwd, a2_fwd, w0_bwd, w2_bwd, a0_bwd, a2_bwd,
              g2, k_k, k_a, r_k, ln_x_w, ln_x_b, lam_q1, lam_k1, lam_q2, lam_k2, subln_w,
              w_out, w_up, ffn_conv, ffn_conv_b, w_down):
    n_tok = x.shape[1]
    ROWS = n_tok // GRID_W
    cos, sin = axial_rope(ROWS)
    for l in range(DEPTH):
        p = dict(g_pre_mix=g_pre_mix[l], g_post_mix=g_post_mix[l], g_pre_ffn=g_pre_ffn[l],
                 g_post_ffn=g_post_ffn[l], w_in=w_in[l], rwkv_conv=rwkv_conv[l],
                 w0_fwd=w0_fwd[l], w2_fwd=w2_fwd[l], a0_fwd=a0_fwd[l], a2_fwd=a2_fwd[l],
                 w0_bwd=w0_bwd[l], w2_bwd=w2_bwd[l], a0_bwd=a0_bwd[l], a2_bwd=a2_bwd[l],
                 g2=g2[l], k_k=k_k[l], k_a=k_a[l], r_k=r_k[l], ln_x_w=ln_x_w[l], ln_x_b=ln_x_b[l],
                 lam_q1=lam_q1[l], lam_k1=lam_k1[l], lam_q2=lam_q2[l], lam_k2=lam_k2[l],
                 subln_w=subln_w[l], w_out=w_out[l], w_up=w_up[l], ffn_conv=ffn_conv[l],
                 ffn_conv_b=ffn_conv_b[l], w_down=w_down[l])
        lam_init = 0.8 - 0.6 * math.exp(-0.3 * l)
        need_ctx = l + 1 < DEPTH
        mod = adaln(c, w_mod[l], b_mod[l])[:, None, :]
        mod_c = adaln(c_ctx[None, :], w_mod[l], b_mod[l])[:, None, :]
        sh1, sc1, gt1, sh2, sc2, gt2 = jnp.split(mod, 6, axis=-1)
        sh1c, sc1c, gt1c, sh2c, sc2c, gt2c = jnp.split(mod_c, 6, axis=-1)
        h = modulate(rmsnorm(x, p['g_pre_mix']), sh1, sc1)
        h_c = modulate(rmsnorm(ctx, p['g_pre_mix']), sh1c, sc1c)
        y, y_c = token_mixer(h, h_c, p, lam_init, cos, sin, need_ctx)
        x = x + gt1 * rmsnorm(y, p['g_post_mix'])
        h = modulate(rmsnorm(x, p['g_pre_ffn']), sh2, sc2)
        x = x + gt2 * rmsnorm(conv_ffn(h, p), p['g_post_ffn'])
        if need_ctx:
            ctx = ctx + gt1c * rmsnorm(y_c, p['g_post_mix'])
            h_c = modulate(rmsnorm(ctx, p['g_pre_ffn']), sh2c, sc2c)
            ctx = ctx + gt2c * rmsnorm(conv_ffn(h_c, p), p['g_post_ffn'])
    return x


DEPTH_2 = 2

N_META = 16
N_MIXERS = 2
N_CONV_LAYERS = (DEPTH_2 + 1) // 2
N_GLA_LAYERS = DEPTH_2 // 2
DN_ALPHA = (2 * DEPTH_2) ** 0.25
DN_BETA = (8 * DEPTH_2) ** -0.25
LN_EPS = 1e-5
RMS_EPS = 1e-6
CONV_CH = D_MODEL
CONV_TAPS = 31
CONV_IN = 3 * CONV_CH
GLA_HEADS = 4
GLA_DK = D_MODEL // 2
GLA_DV = D_MODEL
GLA_HK = GLA_DK // GLA_HEADS
GLA_HV = GLA_DV // GLA_HEADS
GLA_GATE_RANK = 16
GLA_TAU = 16.0
GLA_CHUNK = 64
GLA_IN = 2 * GLA_DK + 2 * GLA_DV + GLA_GATE_RANK


def layer_norm(x, g, b):
    xf = x.astype(jnp.float32)
    mu = jnp.mean(xf, axis=-1, keepdims=True)
    xc = xf - mu
    var = jnp.mean(xc * xc, axis=-1, keepdims=True)
    y = xc * lax.rsqrt(var + LN_EPS) * g.astype(jnp.float32) + b.astype(jnp.float32)
    return y.astype(x.dtype)

def conformer_mixer(h, w_in, b_in, w_dw, b_dw, norm_g, norm_b, w_out, b_out):
    u = h @ w_in + b_in
    a, ga, z = jnp.split(u, 3, axis=-1)
    glu = a * jax.nn.sigmoid(ga)
    c = lax.conv_general_dilated(
        glu, w_dw[:, None, :].astype(glu.dtype), window_strides=(1,),
        padding=[(CONV_TAPS - 1, 0)], dimension_numbers=('NWC', 'WIO', 'NWC'),
        feature_group_count=CONV_CH) + b_dw
    c = jax.nn.silu(layer_norm(c, norm_g, norm_b))
    return (c * jax.nn.silu(z)) @ w_out + b_out

def _gla_chunk_step(S, inp):
    qc, kc, vc, gc = inp
    bc = jnp.cumsum(gc, axis=1)
    o_inter = jnp.einsum('bthd,bhde->bthe', qc * jnp.exp(bc), S)
    causal = jnp.tril(jnp.ones((GLA_CHUNK, GLA_CHUNK), dtype=bool))
    diff = bc[:, :, None] - bc[:, None, :]
    decay = jnp.exp(jnp.where(causal[None, :, :, None, None], diff, -jnp.inf))
    att = jnp.einsum('bthd,bshd,btshd->bhts', qc, kc, decay)
    o_intra = jnp.einsum('bhts,bshe->bthe', att, vc)
    b_last = bc[:, -1]
    S_new = jnp.exp(b_last)[..., None] * S + jnp.einsum(
        'bshd,bshe->bhde', kc * jnp.exp(b_last[:, None] - bc), vc)
    return S_new, o_inter + o_intra

def gla_mixer(h, w_in, w_a2, b_a, norm_g, w_out):
    B, L, _ = h.shape
    u = h @ w_in
    q, k, v, r, a1 = jnp.split(
        u, [GLA_DK, 2 * GLA_DK, 2 * GLA_DK + GLA_DV, 2 * GLA_DK + 2 * GLA_DV], axis=-1)
    glog = jax.nn.log_sigmoid((a1 @ w_a2 + b_a).astype(jnp.float32)) / GLA_TAU
    pad = GLA_CHUNK - N_META
    n_chunks = (L + pad) // GLA_CHUNK

    def prep(t, hd):
        t = jnp.pad(t.astype(jnp.float32), ((0, 0), (pad, 0), (0, 0)))
        return t.reshape(B, n_chunks, GLA_CHUNK, GLA_HEADS, hd).transpose(1, 0, 2, 3, 4)

    qs = prep(q, GLA_HK) * (GLA_HK ** -0.5)
    ks = prep(k, GLA_HK)
    vs = prep(v, GLA_HV)
    gs = prep(glog, GLA_HK)
    S0 = jnp.zeros((B, GLA_HEADS, GLA_HK, GLA_HV), jnp.float32)
    _, o = lax.scan(_gla_chunk_step, S0, (qs, ks, vs, gs))
    o = o.transpose(1, 0, 2, 3, 4).reshape(B, n_chunks * GLA_CHUNK, GLA_HEADS, GLA_HV)[:, pad:]
    o = o * lax.rsqrt(jnp.mean(o * o, axis=-1, keepdims=True) + RMS_EPS) * norm_g.astype(jnp.float32)
    o = o.reshape(B, L, GLA_DV).astype(h.dtype)
    return (o * jax.nn.silu(r)) @ w_out

def second_inputs(seed: int = 0) -> dict:
    key = jax.random.key(seed)
    ks = jax.random.split(key, 20)
    nrm = jax.random.normal
    f32 = jnp.float32
    Lc, Lg = N_CONV_LAYERS, N_GLA_LAYERS
    return {
        "x": nrm(ks[0], (BATCH, SEQ, D_MODEL), f32),
        "meta": nrm(ks[1], (N_META, D_MODEL), f32),
        "conv_w_in": nrm(ks[2], (Lc, D_MODEL, CONV_IN), f32) * D_MODEL ** -0.5,
        "conv_b_in": nrm(ks[3], (Lc, CONV_IN), f32) * 0.02,
        "conv_w_dw": nrm(ks[4], (Lc, CONV_TAPS, CONV_CH), f32) * CONV_TAPS ** -0.5,
        "conv_b_dw": nrm(ks[5], (Lc, CONV_CH), f32) * 0.02,
        "conv_norm_g": 1.0 + 0.02 * nrm(ks[6], (Lc, CONV_CH), f32),
        "conv_norm_b": nrm(ks[7], (Lc, CONV_CH), f32) * 0.02,
        "conv_w_out": nrm(ks[8], (Lc, CONV_CH, D_MODEL), f32) * (CONV_CH ** -0.5 * DN_BETA),
        "conv_b_out": nrm(ks[9], (Lc, D_MODEL), f32) * 0.02,
        "gla_w_in": nrm(ks[10], (Lg, D_MODEL, GLA_IN), f32) * D_MODEL ** -0.5,
        "gla_w_a2": nrm(ks[11], (Lg, GLA_GATE_RANK, GLA_DK), f32) * GLA_GATE_RANK ** -0.5,
        "gla_b_a": nrm(ks[12], (Lg, GLA_DK), f32) * 0.02,
        "gla_norm_g": 1.0 + 0.02 * nrm(ks[13], (Lg, GLA_HV), f32),
        "gla_w_out": nrm(ks[14], (Lg, GLA_DV, D_MODEL), f32) * (GLA_DV ** -0.5 * DN_BETA),
        "post_ln_g": 1.0 + 0.02 * nrm(ks[15], (DEPTH_2, D_MODEL), f32),
        "post_ln_b": nrm(ks[16], (DEPTH_2, D_MODEL), f32) * 0.02,
    }

def second_block(x, meta, conv_w_in, conv_b_in, conv_w_dw, conv_b_dw, conv_norm_g, conv_norm_b,
              conv_w_out, conv_b_out, gla_w_in, gla_w_a2, gla_b_a, gla_norm_g, gla_w_out,
              post_ln_g, post_ln_b):
    B = x.shape[0]
    h = jnp.concatenate(
        [jnp.broadcast_to(meta[None].astype(x.dtype), (B, N_META, D_MODEL)), x], axis=1)
    for i in range(DEPTH_2):
        j = i // N_MIXERS
        if i % N_MIXERS == 0:
            y = conformer_mixer(h, conv_w_in[j], conv_b_in[j], conv_w_dw[j], conv_b_dw[j],
                                conv_norm_g[j], conv_norm_b[j], conv_w_out[j], conv_b_out[j])
        else:
            y = gla_mixer(h, gla_w_in[j], gla_w_a2[j], gla_b_a[j], gla_norm_g[j], gla_w_out[j])
        h = layer_norm(DN_ALPHA * h + y, post_ln_g[i], post_ln_b[i])
    return h[:, N_META:]


def setup_inputs(seed=0):
    out = dict(first_inputs(seed))
    for name, value in second_inputs(seed + 1).items():
        if name != "x":
            out[name + "_2"] = value
    return out


def reference(
    x, c, ctx, c_ctx, w_mod, b_mod, g_pre_mix, g_post_mix, g_pre_ffn, g_post_ffn, w_in,
    rwkv_conv, w0_fwd, w2_fwd, a0_fwd, a2_fwd, w0_bwd, w2_bwd, a0_bwd, a2_bwd, g2, k_k, k_a,
    r_k, ln_x_w, ln_x_b, lam_q1, lam_k1, lam_q2, lam_k2, subln_w, w_out, w_up, ffn_conv,
    ffn_conv_b, w_down, meta_2, conv_w_in_2, conv_b_in_2, conv_w_dw_2, conv_b_dw_2,
    conv_norm_g_2, conv_norm_b_2, conv_w_out_2, conv_b_out_2, gla_w_in_2, gla_w_a2_2, gla_b_a_2,
    gla_norm_g_2, gla_w_out_2, post_ln_g_2, post_ln_b_2,
):
    x = first_block(
        x, c, ctx, c_ctx, w_mod, b_mod, g_pre_mix, g_post_mix, g_pre_ffn, g_post_ffn, w_in,
        rwkv_conv, w0_fwd, w2_fwd, a0_fwd, a2_fwd, w0_bwd, w2_bwd, a0_bwd, a2_bwd, g2, k_k, k_a,
        r_k, ln_x_w, ln_x_b, lam_q1, lam_k1, lam_q2, lam_k2, subln_w, w_out, w_up, ffn_conv,
        ffn_conv_b, w_down,
    )
    return second_block(
        x, meta_2, conv_w_in_2, conv_b_in_2, conv_w_dw_2, conv_b_dw_2, conv_norm_g_2,
        conv_norm_b_2, conv_w_out_2, conv_b_out_2, gla_w_in_2, gla_w_a2_2, gla_b_a_2,
        gla_norm_g_2, gla_w_out_2, post_ln_g_2, post_ln_b_2,
    )


_drawn_inputs = setup_inputs


def setup_inputs(seed=0):
    import zlib

    import numpy as np

    out = dict(_drawn_inputs(seed))
    spreads = {}
    factors = {'g_pre_mix': 2.872,
     'g_post_mix': 3.077,
     'g_pre_ffn': 2.941,
     'g_post_ffn': 3.453,
     'w2_fwd': 7.788,
     'a0_fwd': 8.0,
     'w2_bwd': 8.0,
     'a0_bwd': 8.0,
     'ln_x_w': 5.985,
     'ln_x_b': 8.0,
     'lam_k1': 3.397,
     'lam_q2': 8.0,
     'subln_w': 4.074,
     'ffn_conv_b': 4.678,
     'conv_b_in_2': 8.0,
     'conv_b_dw_2': 8.0,
     'conv_norm_g_2': 8.0,
     'conv_norm_b_2': 8.0,
     'conv_b_out_2': 3.739,
     'gla_b_a_2': 8.0,
     'gla_norm_g_2': 8.0}
    for name, (base, spread) in spreads.items():
        noise = np.random.default_rng([zlib.crc32(name.encode()), seed]).standard_normal(out[name].shape)
        drawn = base * np.exp(spread * noise) if base else spread * noise
        out[name] = jnp.asarray(drawn.astype(out[name].dtype))
    for name, factor in factors.items():
        out[name] = (out[name] * factor).astype(out[name].dtype)
    return out
```

```python
from contextlib import ExitStack

from concourse import mybir

F32 = mybir.dt.float32
F32R = mybir.dt.float32r
I32 = mybir.dt.int32
ALU = mybir.AluOpType
ACT = mybir.ActivationFunctionType
AX = mybir.AxisListType

P = 128
BANK = 512
D = 1024
KD = D // P
SEQ, CTX, META = 1024, 256, 16
RW, HEAD = 512, 64
LORA, GATE = 32, 96
DIFF = 512
RWKV_COLS = 3 * RW + 2 * LORA + GATE
FF = 2816
KF = FF // P
NT = SEQ // P
NC = CTX // P
ALL = CTX + SEQ
DECAY = 0.6065306597126334
LAM_INIT = 0.8 - 0.6
L2 = META + SEQ
DN_ALPHA = 4 ** 0.25
TAPS = 31
GK, GV = 128, 256
GH = 4
LEVELS = (1, 2, 4, 8, 16, 32, 64)
SLOT = KD * 512


class Core:

    NAMES = ("pe", "dve", "act", "pool", "sp")

    def __init__(self, nc, ctx):
        self.nc, self.ctx = nc, ctx
        self.queue = {e: [] for e in self.NAMES}
        self.done = {e: ctx.enter_context(nc.semaphore(f"done_{e}")) for e in self.NAMES}
        self.count = {e: 0 for e in self.NAMES}
        self.waited = {e: {} for e in self.NAMES}
        self.held = {e: [] for e in self.NAMES}
        self.dma_count = {}
        self.dma_sems = {}

    def last(self, eng):
        return (self.done[eng], self.count[eng]) if self.count[eng] else None

    def waits(self, eng, after):
        need = []
        for item in after:
            if item is None:
                continue
            if isinstance(item, list):
                need += self.waits(eng, item)
                continue
            sem, value = item
            if self.waited[eng].get(id(sem), 0) < value:
                self.waited[eng][id(sem)] = value
                need.append((sem, value))
        return need

    def put(self, eng, step, *after, signal=True, loose=False):
        own = [] if (loose or eng == "pe") else [self.last(eng)]
        need = self.waits(eng, [*after, *own, *self.held[eng]])
        self.held[eng] = []
        if signal:
            self.count[eng] += 1
        self.queue[eng].append((need, step, (self.done[eng], 1) if signal else None))
        return (self.done[eng], self.count[eng]) if signal else None

    def dma(self, eng, name, out, in_, *after):
        if name not in self.dma_sems:
            self.dma_sems[name] = self.ctx.enter_context(self.nc.semaphore(f"dma_{name}"))
            self.dma_count[name] = 0
        self.dma_count[name] += 16
        sem = self.dma_sems[name]
        need = self.waits(eng, [*after, *(self.held[eng] if eng != "sp" else [])])
        self.queue[eng].append((need, lambda e: e.dma_start(out, in_), (sem, 16)))
        return (sem, self.dma_count[name])

    def everything(self):
        return [self.last(e) for e in ("pe", "dve", "act", "pool")]

    def new_phase(self):
        for e in ("pe", "dve", "act", "pool"):
            self.held[e] = self.held[e] + self.everything()

    def emit(self):
        tail = [(self.dma_sems[n], v) for n, v in self.dma_count.items()]
        block = self.ctx.enter_context(self.nc.Block())

        def run(name, eng):
            for need, step, inc in self.queue[name]:
                for sem, value in need:
                    eng.wait_ge(sem, value)
                made = step(eng)
                if inc:
                    made.then_inc(*inc)

        block.tensor(lambda eng: run("pe", eng))
        block.vector(lambda eng: run("dve", eng))
        block.scalar(lambda eng: run("act", eng))
        block.gpsimd(lambda eng: run("pool", eng))

        @block.sync
        def _(eng):
            run("sp", eng)
            for sem, value in tail:
                eng.wait_ge(sem, value)


class Ring:

    def __init__(self, slots):
        self.slots, self.readers, self.at = slots, [[] for _ in slots], -1

    def take(self):
        self.at = (self.at + 1) % len(self.slots)
        return self.at, self.slots[self.at], list(self.readers[self.at])

    def read(self, index, *counts):
        self.readers[index] = list(counts)


class Arena:

    def __init__(self, tensor, cols):
        self.t, self.at, self.cols = tensor, 0, cols

    def take(self, n, **shape):
        n0, self.at = self.at, self.at + n
        assert self.at <= self.cols, (self.at, self.cols)
        return self.view(n0, n, **shape)

    def view(self, at, n, **shape):
        v = self.t[:, at:at + n]
        if shape:
            names = list(shape)
            v = v.rearrange("p (" + " ".join(names) + " rest) -> p " + " ".join(names) + " rest", **shape)
        return v


class Kernel:
    def __init__(self, nc, io, ctx):
        self.nc, self.io = nc, io
        self.c = Core(nc, ctx)
        self.ctx = ctx
        cols = 53200
        self.sb = Arena(ctx.enter_context(nc.sbuf_tensor("sbuf_all", [P, cols], F32)), cols)
        self.ps = ctx.enter_context(nc.psum_tensor("psum_all", [P, 8 * BANK], F32))
        self.banks(8)

    def banks(self, n, first=0):
        self.bank = Ring([self.ps[:, (first + i) * BANK:(first + i + 1) * BANK] for i in range(n)])
        for i in range(n):
            self.bank.readers[i] = self.c.everything()

    def mm(self, out, lhsT, rhs, start, stop, *after, signal=False):
        return self.c.put("pe", lambda e: e.matmul(out, lhsT, rhs, start=start, stop=stop, skip_group_check=True),
                          *after, signal=signal)

    def turn(self, out, in_, ident, *after, signal=False):
        return self.c.put("pe", lambda e: e.transpose(out, in_, ident), *after, signal=signal)

    def act(self, out, in_, func, *after, scale=1.0, bias=0.0, accum=None, loose=False):
        kw = {} if accum is None else {"accum_out": accum}
        return self.c.put("act", lambda e: e.activation(out, in_, func, bias=bias, scale=scale, **kw), *after,
                          loose=loose)

    def copy(self, eng, out, in_, *after, loose=False):
        if eng == "act":
            return self.act(out, in_, ACT.Copy, *after, loose=loose)
        return self.c.put(eng, lambda e: e.tensor_copy(out, in_), *after, loose=loose)

    def tt(self, out, a, b, op, *after, eng="dve", loose=False):
        return self.c.put(eng, lambda e: e.tensor_tensor(out, a, b, op), *after, loose=loose)

    def ts(self, out, a, s1, s2, op0, op1, *after, eng="dve", loose=False):
        if s2 is None:
            return self.c.put(eng, lambda e: e.tensor_scalar(out, a, s1, None, op0), *after, loose=loose)
        return self.c.put(eng, lambda e: e.tensor_scalar(out, a, s1, s2, op0, op1), *after, loose=loose)

    def stt(self, out, a, s, b, op0, op1, *after, loose=False):
        return self.c.put("dve", lambda e: e.scalar_tensor_tensor(out, a, s, b, op0, op1), *after, loose=loose)

    def recip(self, out, a, *after):
        return self.c.put("dve", lambda e: e.reciprocal(out, a), *after)

    def fill(self, ap, value, *after, eng="pool"):
        return self.c.put(eng, lambda e: e.memset(ap, value), *after)

    def constants(self):
        c, sb = self.c, self.sb
        self.ident = sb.take(P)
        self.ones = sb.take(P)
        self.zero = sb.view(42000, P)
        self.fill(self.zero, 0.0)
        ready = self.fill(self.ones, 1.0)

        def select(out, in_, pattern, base, mult, op, fill=0.0):
            return c.put("pool", lambda e: e.affine_select(out=out, in_=in_, pattern=pattern, compare_op=op,
                                                           fill=fill, base=base, channel_multiplier=mult))

        select(self.ident, self.zero, [[-1, P]], 0, 1, ALU.not_equal, 1.0)
        self.before_at = sb.at
        self.before, self.upto = sb.take(P), sb.take(P)
        self.later_at = sb.at
        self.later, self.from_ = sb.take(P), sb.take(P)
        select(self.before, self.ones, [[1, P]], 0, -1, ALU.is_gt)
        select(self.upto, self.ones, [[1, P]], 0, -1, ALU.is_ge)
        select(self.later, self.ones, [[-1, P]], 0, 1, ALU.is_gt)
        select(self.from_, self.ones, [[-1, P]], 0, 1, ALU.is_ge)
        self.level = {"upper": sb.take(P * 7, m=7), "lower": sb.take(P * 7, m=7)}
        same = {1: self.ident}
        spare = sb.view(42200, P * 7, m=7)
        for i, m in enumerate(LEVELS):
            n = 2 * m
            s = spare[:, i, :]
            if n == P:
                self.copy("pool", s, self.ones)
            else:
                v = s.rearrange("p (b j) -> p b j", j=n)
                one = self.ones.rearrange("p (b j) -> p b j", j=n)
                select(v, one, [[-n, P // n], [0, n]], 0, 1, ALU.is_ge)
                select(v, v, [[n, P // n], [0, n]], n - 1, -1, ALU.is_ge)
            same[n] = s
        for i, m in enumerate(LEVELS):
            for side, order in (("upper", self.before), ("lower", self.later)):
                out = self.level[side][:, i, :]
                self.tt(out, same[2 * m], same[m], ALU.subtract, eng="pool")
                ready = self.tt(out, out, order, ALU.mult, eng="pool")
        self.heads = sb.take(P)
        ready = self.copy("pool", self.heads, same[64])
        self.consts_ready = [ready]

        cols, rows = {}, []

        def vec(name, ap, n, width=P):
            rows.append((name, ap, n, width))

        io = self.io
        lines = lambda ap: ap.rearrange("(r f) -> r f", f=P)
        for name in ("g_pre_mix", "g_pre_ffn", "g_post_mix", "g_post_ffn"):
            vec(name, lines(io[name][0]), KD)
        vec("c", lines(io["c"][0]), KD)
        vec("c_ctx", lines(io["c_ctx"]), KD)
        vec("b_mod", lines(io["b_mod"][0]), 48)
        rows.append(None)
        for name in ("w0_fwd", "w0_bwd", "a0_fwd", "a0_bwd", "k_k", "k_a"):
            vec(name, lines(io[name][0]), 4)
        vec("r_k", io["r_k"][0].rearrange("h f -> (h f)").rearrange("(r f) -> r f", f=P), 4)
        for t in range(3):
            vec(f"rconv{t}", lines(io["rwkv_conv"][0, t, 0:3 * RW]), 12)
            vec(f"lconv{t}", io["rwkv_conv"][0, t:t + 1, 3 * RW:3 * RW + 2 * LORA], 1, 2 * LORA)
            vec(f"gconv{t}", io["rwkv_conv"][0, t:t + 1, 3 * RW + 2 * LORA:RWKV_COLS], 1, GATE)
        vec("subln_w", io["subln_w"], 1)
        for name in ("lam_q1", "lam_q2", "lam_k1", "lam_k2"):
            vec(name, io[name], 1, HEAD)
        rows.append(None)
        for t in range(2):
            vec(f"fconv{t}", lines(io["ffn_conv"][0, t]), 44)
        rows.append(None)
        vec("fconv2", lines(io["ffn_conv"][0, 2]), 44)
        vec("ffn_conv_b", lines(io["ffn_conv_b"][0]), 44)
        rows.append(None)
        dw = io["conv_w_dw_2"][0].rearrange("t (r f) -> (t r) f", f=P)
        vec("dw_a", dw[0:124], 124)
        rows.append(None)
        vec("dw_b", dw[124:248], 124)
        rows.append(None)
        vec("conv_b_in", lines(io["conv_b_in_2"][0]), 24)
        vec("conv_b_dw", lines(io["conv_b_dw_2"][0]), 8)
        vec("conv_norm_g", lines(io["conv_norm_g_2"][0]), 8)
        vec("conv_norm_b", lines(io["conv_norm_b_2"][0]), 8)
        vec("gla_b_a", lines(io["gla_b_a_2"][0]), 4)
        vec("gla_norm_g", lines(io["gla_norm_g_2"][0]), 2)
        rows.append(None)

        total = sum(r[2] for r in rows if r)
        self.par = sb.take(total)
        stage = Ring([sb.view(40000 + i * P, P) for i in range(7)])
        cleared = [self.fill(sb.view(40000, 7 * P), 0.0, eng="dve")]
        at = group = 0
        batch = []
        self.col, self.par_at = {}, {}
        for r in rows:
            if r is not None:
                batch.append(r)
                continue
            i, buf, _ = stage.take()
            n, loads = 0, []
            for name, ap, k, width in batch:
                loads = [c.dma("sp" if group % 2 == 0 else "act", f"params{group}", buf[n:n + k, 0:width], ap, cleared)]
                self.col[name] = self.par[:, at + n:at + n + k]
                self.par_at[name] = (self.par, at + n)
                n += k
            bi, bank, free = self.bank.take()
            t = self.turn(bank[:, 0:n], buf[0:n, :], self.ident[0:n, 0:n], loads[-1], self.consts_ready, free, signal=True)
            done = self.copy("dve", self.par[:, at:at + n], bank[:, 0:n], t)
            self.bank.read(bi, done)
            at += n
            group += 1
            batch = []
        self.par_ready = done

    def open_weights(self, slots=3):
        self.w_at = self.sb.at
        self.w_slots = slots
        self.sb.take(slots * SLOT)
        self.weights = Ring([self.sb.view(self.w_at + i * SLOT, SLOT) for i in range(slots)])
        self.w_queue = []

    def load_block(self, parts):
        i, slot, free = self.weights.take()
        got = None
        for view, src in parts(slot):
            got = self.c.dma("sp", f"w{i}", view, src, free)
        return i, slot, got

    def w_block(self, w, c0, n, k0=0, k=KD):
        def parts(slot):
            view = slot[:, 0:k * n].rearrange("p (k n) -> p k n", n=n)
            yield view, w[k0 * P:(k0 + k) * P, c0:c0 + n].rearrange("(k p) n -> p k n", p=P)
        i, slot, got = self.load_block(parts)
        return i, slot[:, 0:k * n].rearrange("p (k n) -> p k n", n=n), got

    def modulation(self):
        c = self.c
        sc = self.sb.take(16).rearrange("p (k two) -> p k two", two=2)
        self.mod = self.sb.take(48)
        self.modc = self.sb.take(16)
        a = self.act(sc[:, :, 0], self.col["c"], ACT.Silu, self.par_ready)
        a = self.act(sc[:, :, 1], self.col["c_ctx"], ACT.Silu)
        self.silu_c, self.silu_ready = sc, a
        self.mod_blocks(range(4))
        self.gs1, self.gs1c = self.sb.take(KD), self.sb.take(KD)
        self.stt(self.gs1, self.mod[:, 8:16], 1.0, self.col["g_pre_mix"], ALU.add, ALU.mult)
        self.mod_ready = self.stt(self.gs1c, self.modc[:, 8:16], 1.0, self.col["g_pre_mix"], ALU.add, ALU.mult)

    def mod_blocks(self, blocks):
        for b in blocks:
            wi, w, got = self.w_block(self.io["w_mod"][0], b * 512, 512)
            bi, bank, free = self.bank.take()
            for j in range(4):
                for k in range(KD):
                    t = self.mm(bank[:, 2 * j:2 * j + 2], w[:, k, j * P:(j + 1) * P], self.silu_c[:, k, :],
                                k == 0, k == KD - 1, got, free, self.silu_ready, signal=(j == 3 and k == KD - 1))
            self.weights.read(wi, t)
            two = bank[:, 0:8].rearrange("p (j two) -> p j two", two=2)
            bm = self.col["b_mod"][:, 4 * b:4 * b + 4]
            done = self.tt(self.mod[:, 4 * b:4 * b + 4], two[:, :, 0], bm, ALU.add, t)
            if b < 4:
                done = self.tt(self.modc[:, 4 * b:4 * b + 4], two[:, :, 1], bm, ALU.add, t)
            self.bank.read(bi, done)
        return done

    def rstd(self, out, ssq, n, eps, *after):
        t = self.ts(out, ssq, 1.0 / n, eps, ALU.mult, ALU.add, *after)
        t = self.act(out, out, ACT.Sqrt, t)
        return self.recip(out, out, t)

    def turn_rows(self, rows, tiles, emit, after, kt=KD):
        for j in range(kt):
            bi, bank, free = self.bank.take()
            for n, i in enumerate(tiles):
                t = self.turn(bank[:, n * P:(n + 1) * P], rows(i)[:, j * P:(j + 1) * P], self.ident,
                              after, free, self.consts_ready, signal=(n == len(tiles) - 1))
            self.bank.read(bi, emit(j, bank[:, 0:len(tiles) * P], t))
        return t

    def first_norm(self):
        c, sb = self.c, self.sb
        self.hT_at = sb.at
        self.hT = sb.take(KD * ALL, k=KD)
        mark = sb.at
        raw = sb.take(4 * 4 * D).rearrange("p (g i d) -> p g i d", g=4, i=4)[:, 0:3]
        sb.at -= 4 * D
        stat = sb.take(10)
        junk = sb.take(D)
        x = self.io["x"][0].rearrange("(i p) d -> p i d", p=P)
        cx = self.io["ctx"][0].rearrange("(i p) d -> p i d", p=P)
        groups = [(cx, 0, 2, 0), (x, 0, 4, CTX), (x, 4, 4, CTX + 512)]
        got = [c.dma("act", f"rows{g}", raw[:, g, 0:n, :], src[:, i0:i0 + n, :]) for g, (src, i0, n, _) in enumerate(groups)]
        s = 0
        for g, (_, _, n, _) in enumerate(groups):
            for i in range(n):
                sq = self.act(junk, raw[:, g, i, :], ACT.Square, got[g], accum=stat[:, s:s + 1])
                s += 1
        r = self.rstd(stat, stat, D, 1e-6, sq)
        s = 0
        for g, (_, _, n, col) in enumerate(groups):
            for i in range(n):
                t = self.ts(raw[:, g, i, :], raw[:, g, i, :], stat[:, s:s + 1], None, ALU.mult, ALU.bypass, r, loose=True)
                s += 1
            scale, shift = (self.gs1c, self.modc) if g == 0 else (self.gs1, self.mod)

            def emit(j, bank, t, col=col, n=n, scale=scale, shift=shift):
                out = self.hT[:, j, col:col + n * P]
                if j % 2:
                    return self.act(out, bank, ACT.Identity, t, self.mod_ready, scale=scale[:, j:j + 1],
                                    bias=shift[:, j:j + 1], loose=True)
                return self.ts(out, bank, scale[:, j:j + 1], shift[:, j:j + 1], ALU.mult, ALU.add, t,
                               self.mod_ready, loose=True)

            last = self.turn_rows(lambda i, g=g: raw[:, g, i, :], range(n), emit, t)
        sb.at = mark
        self.hT_ready = [c.last("act"), c.last("dve")]
        return last

    def dense(self, w, c0, n, rhs, spans, emit, after, kt=KD):
        wi, wt, got = self.w_block(w, c0, n, k=kt)
        for j in range((n + P - 1) // P):
            m = min(P, n - j * P)
            self.product(lambda k: wt[:, k, j * P:j * P + m], rhs, spans, kt, m, [got, after],
                         lambda s, bank, t: emit(j, s, bank, t))
        self.weights.read(wi, self.c.last("pe"))

    def product(self, lhs, rhs, spans, kt, m, after, emit):
        for s, (a, b) in enumerate(spans):
            bi, bank, free = self.bank.take()
            for k in range(kt):
                t = self.mm(bank[0:m, 0:b - a], lhs(k), rhs(k, a, b), k == 0, k == kt - 1, after, free,
                            signal=(k == kt - 1))
            self.bank.read(bi, emit(s, bank[0:m, 0:b - a], t))

    def attention(self):
        c, sb, io = self.c, self.sb, self.io
        self.yd_at = sb.at
        self.ydT = sb.take(4 * SEQ, h=4)
        q, k = sb.take(4 * SEQ, h=4), sb.take(4 * ALL, h=4)
        v = sb.take(10 * DIFF, i=10)
        rope_at = sb.at
        cos, sin, turn = sb.take(SEQ), sb.take(SEQ), sb.take(P)
        tmp = [sb.take(BANK), sb.take(BANK)]
        c.new_phase()
        tables = [c.dma("act", "rope", t, io[n]) for n, t in (("rope_cos", cos), ("rope_sin", sin), ("rope_turn", turn))]
        hT = lambda k_, a, b: self.hT[:, k_, a:b]
        ready = self.hT_ready
        turn_ring = Ring(tmp)

        def moved(dst):
            return lambda j, s, bank, t: self.copy("act" if s % 2 else "dve", dst(j, s), bank, t, loose=True)

        def rope(x, first):
            for h in range(4):
                for a in (0, 512):
                    xs = x[:, h, first + a:first + a + 512]
                    bi, bank, free = self.bank.take()
                    t = self.mm(bank, turn, xs, True, True, c.last("act"), c.last("dve"), free, tables[-1], signal=True)
                    ti, rot, _ = turn_ring.take()
                    t1 = self.tt(rot, bank, sin[:, a:a + 512], ALU.mult, t)
                    self.bank.read(bi, t1)
                    self.tt(xs, xs, cos[:, a:a + 512], ALU.mult, t)
                    self.tt(xs, xs, rot, ALU.add)

        self.dense(io["w_in"][0], RWKV_COLS, DIFF, lambda k_, a, b: self.hT[:, k_, CTX + a:CTX + b],
                   [(0, 512), (512, 1024)], moved(lambda j, s: q[:, j, s * 512:(s + 1) * 512]), ready)
        spans = [(0, 512), (512, 1024), (1024, 1280)]
        self.dense(io["w_in"][0], RWKV_COLS + DIFF, DIFF, hT, spans,
                   moved(lambda j, s: k[:, j, spans[s][0]:spans[s][1]]), ready)
        rope(q, 0)
        rope(k, CTX)
        wi, wv, got = self.w_block(io["w_in"][0], RWKV_COLS + 2 * DIFF, DIFF)
        for i in range(10):
            bi, bank, free = self.bank.take()
            for kk in range(KD):
                t = self.mm(bank, self.hT[:, kk, i * P:(i + 1) * P], wv[:, kk, :], kk == 0, kk == KD - 1,
                            got, free, ready, signal=(kk == KD - 1))
            self.bank.read(bi, self.copy("act" if i % 2 else "dve", v[:, i, :], bank, t, loose=True))
        self.weights.read(wi, c.last("pe"))

        c.new_phase()
        sb.at = rope_at
        lam = sb.take(8)
        lq, lk = self.col["lam_q1"], self.col["lam_k1"]
        prod = lam[:, 0:2]
        qcols = self.par_slice("lam_q1", 2)
        kcols = self.par_slice("lam_k1", 2)
        t = self.tt(prod, qcols, kcols, ALU.mult)
        bi, bank, free = self.bank.take()
        t = self.mm(bank[:, 0:2], self.ones, prod, True, True, t, free, signal=True)
        t = self.act(lam[:, 2:4], bank[:, 0:2], ACT.Exp, t)
        self.bank.read(bi, t)
        neg_lam = lam[:, 4:5]
        self.tt(neg_lam, lam[:, 3:4], lam[:, 2:3], ALU.subtract, t)
        lam_ready = self.ts(neg_lam, neg_lam, -LAM_INIT, None, ALU.add, ALU.bypass)

        pbuf = [[sb.take(ALL) for m in range(2)] for _ in range(2)]
        pT = [sb.take(ALL) for _ in range(2)]
        oh = [sb.take(P) for _ in range(2)]
        stats = sb.take(16)
        self.banks(2, first=6)
        scores = [self.ps[:, 0:ALL], self.ps[:, 3 * BANK:3 * BANK + ALL]]
        score_free = [c.everything(), c.everything()]
        kv_ready = c.everything()
        scale = HEAD ** -0.5
        p_free = [None, None]
        pT_free = [None, None]
        o_free = [None, None]
        yd_t = []
        work = [(h, i) for h in range(4) for i in range(NT)]

        def score(n):
            h, i = work[n]
            ts = []
            for m in range(2):
                for a, b in spans:
                    t = self.mm(scores[m][:, a:b], q[m * HEAD:(m + 1) * HEAD, h, i * P:(i + 1) * P],
                                k[m * HEAD:(m + 1) * HEAD, h, a:b], True, True, kv_ready, score_free[m], signal=(b == ALL))
                ts.append(t)
            return ts

        score_t = score(0)
        for n, (h, i) in enumerate(work):
            par = n % 2
            s_ = stats[:, 8 * par:8 * par + 8]
            p0, p1 = pbuf[par]
            for m in range(2):
                t = c.put("dve", lambda e, o=s_[:, m:m + 1], x=scores[m]: e.tensor_reduce(o, x, AX.X, ALU.max),
                          score_t[m], p_free[par])
                t = self.ts(s_[:, m:m + 1], s_[:, m:m + 1], -scale, None, ALU.mult, ALU.bypass)
                t = self.act(pbuf[par][m], scores[m], ACT.Exp, t, p_free[par], scale=scale, bias=s_[:, m:m + 1],
                             accum=s_[:, 2 + m:3 + m], loose=True)
                score_free[m] = t
            if n + 1 < len(work):
                score_t = score(n + 1)
            t = self.recip(s_[:, 2:4], s_[:, 2:4], t)
            self.tt(s_[:, 3:4], s_[:, 3:4], neg_lam, ALU.mult, lam_ready)
            self.ts(p0, p0, s_[:, 2:3], None, ALU.mult, ALU.bypass)
            a_t = self.stt(p0, p1, s_[:, 3:4], p0, ALU.mult, ALU.add)
            for g in range(0, 10, 4):
                w = min(4, 10 - g)
                bi, bank, free = self.bank.take()
                for kk in range(w):
                    t = self.turn(bank[:, kk * P:(kk + 1) * P], p0[:, (g + kk) * P:(g + kk + 1) * P], self.ident,
                                  a_t, free, signal=(kk == w - 1))
                t = self.copy("act" if g == 4 else "dve", pT[par][:, g * P:(g + w) * P], bank[:, 0:w * P], t, pT_free[par], loose=True)
                self.bank.read(bi, t)
            p_free[par] = c.last("pe")
            bi, bank, free = self.bank.take()
            for kk in range(10):
                t = self.mm(bank[:, 0:P], pT[par][:, kk * P:(kk + 1) * P], v[:, kk, h * P:(h + 1) * P], kk == 0, kk == 9,
                            c.last("dve"), c.last("act"), free, signal=(kk == 9))
            pT_free[par] = t
            o = oh[par]
            t = self.copy("dve", o, bank[:, 0:P], t, o_free[par])
            self.bank.read(bi, t)
            t = self.act(pbuf[par][0][:, 0:P], o, ACT.Square, t, p_free[par], accum=s_[:, 4:5])
            self.ts(s_[:, 4:5], s_[:, 4:5], 1.0 / P, 1e-5, ALU.mult, ALU.add, t)
            yd_t.append((h, i))
            t = self.act(s_[:, 4:5], s_[:, 4:5], ACT.Sqrt, c.last("dve"))
            self.recip(s_[:, 5:6], s_[:, 4:5], t)
            t = self.ts(o, o, s_[:, 5:6], 1.0 - LAM_INIT, ALU.mult, ALU.mult)
            bi, bank, free = self.bank.take()
            t = self.turn(bank[:, 0:P], o, self.ident, t, free, signal=True)
            o_free[par] = t
            t = self.ts(self.ydT[:, h, i * P:(i + 1) * P], bank[:, 0:P], self.col["subln_w"], None, ALU.mult,
                        ALU.bypass, t)
            self.bank.read(bi, t)
            p_free[par] = [p_free[par], c.last("act"), c.last("dve")]
        self.yd_dram = self.nc.dram_tensor("yd_spill", (P, 4, SEQ), F32).ap()
        self.yd_spilled = c.dma("act", "spill_yd", self.yd_dram, self.ydT, c.last("dve"))
        sb.at = self.yd_at
        self.c.new_phase()
        self.banks(8)

    def par_slice(self, name, n):
        return self.par_at[name][0][:, self.par_at[name][1]:self.par_at[name][1] + n]

    def rwkv_project(self):
        c, sb, io = self.c, self.sb, self.io
        c.new_phase()
        for e in ("pe", "dve", "act", "pool"):
            c.held[e].append(self.yd_spilled)
        self.r, self.k = sb.take(4 * ALL, j=4), sb.take(4 * ALL, j=4)
        self.vtok = sb.take(10 * RW, i=10)
        self.wa, self.gl = sb.take(ALL), sb.take(SEQ)
        self.rwkv_keep = sb.at
        vfeat = sb.take(ALL)
        raws = Ring([sb.take(ALL + 3) for _ in range(2)])
        pads = [self.fill(raw[:, n:n + 1], 0.0) for raw in raws.slots for n in (0, CTX + 1, ALL + 2)]
        spans = [(0, CTX), (CTX, CTX + 512), (CTX + 512, ALL)]
        where = [1, CTX + 2, CTX + 2 + 512]
        hT = lambda k_, a, b: self.hT[:, k_, a:b]
        rank = {}

        def evac(raw, free, m):
            def emit(s, bank, t):
                a, b = spans[s]
                return self.copy("act", raw[0:m, where[s]:where[s] + b - a], bank, t, free, loose=True)
            return emit

        def conv(dst, raw, taps, m, after, with_ctx=True):
            for at, n, to in ([(1, CTX, 0)] if with_ctx else []) + [(CTX + 2, SEQ, CTX if with_ctx else 0)]:
                out = dst[0:m, to:to + n]
                self.ts(out, raw[0:m, at:at + n], taps[1], None, ALU.mult, ALU.bypass, after, pads[-1])
                self.stt(out, raw[0:m, at - 1:at - 1 + n], taps[0], out, ALU.mult, ALU.add)
                t = self.stt(out, raw[0:m, at + 1:at + 1 + n], taps[2], out, ALU.mult, ALU.add)
            return t

        for part, dst in enumerate((self.r, self.k, None)):
            wi, w, got = self.w_block(io["w_in"][0], part * RW, RW)
            for j in range(4):
                ri, raw, free = raws.take()
                self.product(lambda kk: w[:, kk, j * P:(j + 1) * P], hT, spans, KD, P, [got, self.hT_ready],
                             evac(raw, free, P))
                taps = [self.col[f"rconv{t}"][:, part * 4 + j:part * 4 + j + 1] for t in range(3)]
                to = vfeat if dst is None else dst[:, j, :]
                t = conv(to, raw, taps, P, [c.last("act"), c.last("pe") if dst is None else None])
                raws.read(ri, t)
                if dst is None:
                    for g in range(0, 10, 4):
                        n = min(4, 10 - g)
                        bi, bank, free = self.bank.take()
                        for i in range(n):
                            tt = self.turn(bank[:, i * P:(i + 1) * P], vfeat[:, (g + i) * P:(g + i + 1) * P],
                                           self.ident, t, free, signal=(i == n - 1))
                        out = self.vtok[:, g:g + n, j * P:(j + 1) * P]
                        self.bank.read(bi, self.copy("act", out, bank[:, 0:n * P].rearrange("p (i f) -> p i f", f=P), tt, loose=True))
            self.weights.read(wi, c.last("pe"))
        wi, w, got = self.w_block(io["w_in"][0], 3 * RW, 2 * LORA + GATE)
        for c0, m, name, dst in ((0, 2 * LORA, "lconv", self.wa), (2 * LORA, GATE, "gconv", self.gl)):
            ri, raw, free = raws.take()
            self.product(lambda kk: w[:, kk, c0:c0 + m], hT, spans, KD, m, [got, self.hT_ready], evac(raw, free, m))
            taps = [self.col[f"{name}{t}"][0:m, 0:1] for t in range(3)]
            t = conv(dst, raw, taps, m, [c.last("act")], with_ctx=(dst is self.wa))
            raws.read(ri, t)
        self.weights.read(wi, c.last("pe"))
        self.act(self.wa[0:LORA, :], self.wa[0:LORA, :], ACT.Tanh, t)
        self.act(self.gl[0:GATE, :], self.gl[0:GATE, :], ACT.Sigmoid)

    def rwkv(self):
        c, sb, io = self.c, self.sb, self.io
        c.new_phase()
        sb.at = self.w_at
        kk = sb.take(ALL)
        yacc = sb.take(NT * RW, i=NT)
        sb_w_end = self.w_at + self.w_slots * SLOT
        lora = sb.take(2 * RW, d=2)
        g2 = sb.take(RW)
        reset = sb.take(ALL)
        S = [sb.take(P) for _ in range(2)]
        assert sb.at <= sb_w_end
        sb.at = self.hT_at
        lw, cc, t1, aa = (sb.take(ALL) for _ in range(4))
        kr = sb.take(2 * ALL).rearrange("p (n two t) -> p n two t", two=2, t=P)
        beta, key = sb.take(ALL, ch=10), sb.take(ALL, ch=10)
        assert sb.at <= self.hT_at + KD * ALL
        sb.at = self.rwkv_keep
        bonus = sb.take(NT * 8, i=NT)
        small = sb.take(64)
        cmid, clast, gain = small[:, 0:10], small[:, 10:20], small[:, 20:30]
        omka = sb.take(4)
        rk = sb.take(4)
        hsel = sb.take(2)

        loads = [c.dma("act", "lora", lora[0:LORA, d, :], io[f"w2_{n}"][0], c.everything()) for d, n in enumerate(("fwd", "bwd"))]
        loads += [c.dma("act", "lora", lora[LORA:2 * LORA, d, :], io[f"a2_{n}"][0]) for d, n in enumerate(("fwd", "bwd"))]
        loads += [c.dma("act", "lora", g2[0:GATE, :], io["g2"][0])]
        lora_ready = loads[-1]
        self.fill(reset, 1.0)
        self.fill(reset.rearrange("p (n t) -> p n t", t=P)[:, :, 0:1], 0.0)
        consts = self.copy("pool", hsel, self.heads.rearrange("p (two h) -> p two h", two=2)[:, :, 0])
        self.ts(omka, self.col["k_a"], -1.0, 1.0, ALU.mult, ALU.add, consts)
        self.ts(rk, self.col["r_k"], 0.5, None, ALU.mult, ALU.bypass)

        def unit_keys(j):
            t = self.ts(kk, self.k[:, j, :], self.col["k_k"][:, j:j + 1], None, ALU.mult, ALU.bypass)
            t = self.act(t1, kk, ACT.Square, t, c.last("dve"))
            for a, b in ((0, 512), (512, 1024), (1024, 1280)):
                bi, bank, free = self.bank.take()
                tt = self.mm(bank[:, 0:b - a], self.heads, t1[:, a:b], True, True, t, free, signal=True)
                tt = self.act(lw[:, a:b], bank[:, 0:b - a], ACT.Sqrt, tt)
                self.bank.read(bi, tt)
            self.ts(lw, lw, 1e-12, None, ALU.max, ALU.bypass, tt, c.last("pe"))
            self.recip(lw, lw)
            self.tt(kk, kk, lw, ALU.mult)

        def group_memory():
            g = {"agbh": sb.take(2048, u=4), "D": sb.take(512, u=4), "E": sb.take(512, u=4), "Y": sb.take(512, u=4)}
            g["X"] = sb.take(512)
            g["tok"] = sb.take(512)
            flat = lambda v: v.rearrange("p u t -> p (u t)")
            g["WU"] = flat(g["D"])
            g["M"], g["N"] = g["X"][:, 0:256], g["X"][:, 256:512]
            g["WT"], g["U"] = flat(g["Y"])[:, 0:256], flat(g["Y"])[:, 256:512]
            return g

        G = [group_memory() for _ in range(2)]
        ydone = []

        for j in range(4):
            unit_keys(j)
            for d in range(2):
                fwd = d == 0
                bias_w = self.col["w0_fwd" if fwd else "w0_bwd"][:, j:j + 1]
                bias_a = self.col["a0_fwd" if fwd else "a0_bwd"][:, j:j + 1]
                for a, b in ((0, 512), (512, 1024), (1024, 1280)):
                    for lo, dst, bias in ((0, lw, bias_w), (LORA, aa, bias_a)):
                        bi, bank, free = self.bank.take()
                        t = self.mm(bank[:, 0:b - a], lora[lo:lo + LORA, d, j * P:(j + 1) * P],
                                    self.wa[lo:lo + LORA, a:b], True, True, lora_ready, c.last("act"), free, signal=True)
                        t = self.act(dst[:, a:b], bank[:, 0:b - a], ACT.Sigmoid, t, c.last("dve"), bias=bias)
                        self.bank.read(bi, t)
                flip = (lambda ap: ap) if fwd else (lambda ap: ap[:, ::-1])
                t = c.put("dve", lambda e, o=flip(cc), x=flip(lw): e.tensor_tensor_scan(
                    o, reset, x, 0.0, ALU.mult, ALU.add), t, consts)
                c3 = cc.rearrange("p (n t) -> p n t", t=P)
                mid, end = P // 2, (P - 1 if fwd else 0)
                self.copy("dve", cmid, c3[:, :, mid])
                self.copy("dve", clast, c3[:, :, end])
                self.tt(c3, c3, cmid.unsqueeze(2).broadcast_to([P, 10, P]), ALU.subtract)
                self.tt(gain, clast, cmid, ALU.subtract)
                for to, frm in (((0, 9), (1, 10)),) if fwd else (((1, 2), (0, 1)), ((0, 1), (9, 10)), ((3, 10), (2, 9))):
                    self.tt(gain[:, to[0]:to[1]], gain[:, to[0]:to[1]], cmid[:, frm[0]:frm[1]], ALU.add)
                self.tt(lw, cc, lw, ALU.subtract)
                self.ts(t1, aa, self.col["k_a"][:, j:j + 1], omka[:, j:j + 1], ALU.mult, ALU.add)
                self.tt(t1, t1, self.k[:, j, :], ALU.mult)
                kt = self.tt(aa, aa, kk, ALU.mult)
                self.act(gain, gain, ACT.Exp, kt, scale=-DECAY)
                self.act(lw, lw, ACT.Exp, scale=-DECAY)
                krp = kr
                t = self.act(krp[:, :, 1, :], c3, ACT.Exp, scale=-DECAY)
                em = self.act(cc, cc, ACT.Exp, scale=DECAY)
                lw3, t13, aa3 = (x.rearrange("p (n t) -> p n t", t=P) for x in (lw, t1, aa))
                kk3, r3 = (x.rearrange("p (n t) -> p n t", t=P) for x in (kk, self.r[:, j, :]))
                self.tt(kr[:, :, 0, :], lw3, kk3, ALU.mult, em, c.last("pe"))
                self.tt(kr[:, :, 1, :], kr[:, :, 1, :], r3, ALU.mult)
                self.stt(lw[:, 0:SEQ], t1[:, CTX:], rk[:, j:j + 1], self.r[:, j, CTX:], ALU.mult, ALU.mult)
                self.tt(key, t13, c3, ALU.mult)
                stream = self.tt(beta, aa3, c3, ALU.mult)
                bi, bank, free = self.bank.take()
                for i in range(NT):
                    t = self.mm(bank[:, 2 * i:2 * i + 2], lw[:, i * P:(i + 1) * P], hsel, True, True, stream, free,
                                signal=(i == NT - 1))
                b2 = bank[:, 0:2 * NT].rearrange("p (i two) -> p i two", two=2)
                bout = bonus[:, :, 2 * j:2 * j + 2]
                if fwd:
                    t = self.copy("dve", bout, b2, t)
                else:
                    t = self.tt(bout, bout, b2, ALU.add, t)
                self.bank.read(bi, t)

                order = [0, 1, *range(2, 10)] if fwd else [1, 0, *range(9, 1, -1)]
                groups = [order[n:n + 2] for n in range(0, 10, 2)]
                si = 0
                first = True
                for gs in (groups[0:1], groups[1:3], groups[3:5]):
                    self.chunk_inverses(gs, G, kr, beta, key, fwd, j, stream)
                    for gi, chunks in enumerate(gs):
                        g = G[gi]
                        for ci, n in enumerate(chunks):
                            self.chunk_step(g, ci, n, kr, gain, S, si, first, j, fwd, yacc, n == order[-1])
                            first = False
                            si ^= 1
        self.rwkv_output(yacc, bonus, g2, lora_ready)

    def chunk_inverses(self, gs, G, kr, beta, key, fwd, j, stream):
        c = self.c
        order_mask = self.sb.t[:, self.before_at:self.before_at + 2 * P] if fwd else \
            self.sb.t[:, self.later_at:self.later_at + 2 * P]
        side, other = ("lower", "upper") if fwd else ("upper", "lower")
        free_g = [c.last("pe"), c.last("dve"), c.last("act")]
        four = lambda m: m.unsqueeze(1).broadcast_to([P, 4, P])
        as4 = lambda b: b.rearrange("p (u t) -> p u t", u=4)
        for gi, chunks in enumerate(gs):
            g = G[gi]
            for u in range(4):
                n, h = chunks[u // 2], u % 2
                rows = slice(h * HEAD, (h + 1) * HEAD)
                bi, bank, free = self.bank.take()
                self.mm(bank[:, 0:256], beta[rows, n, :], kr[rows, n, :, :], True, True, stream, free)
                t = self.mm(bank[:, 256:512], key[rows, n, :], kr[rows, n, :, :], True, True, signal=True)
                t = self.tt(g["agbh"][:, u, :].rearrange("p (two x) -> p two x", two=2), bank.rearrange("p (two x) -> p two x", two=2),
                            order_mask.unsqueeze(1).broadcast_to([P, 2, 2 * P]), ALU.mult, t, free_g, loose=True)
                self.bank.read(bi, t)
            for ci, n in enumerate(chunks):
                bi, bank, free = self.bank.take()
                self.turn(bank[:, 0:P], kr[:, n, 0, :], self.ident, free)
                self.turn(bank[:, P:2 * P], beta[:, n, :], self.ident)
                self.turn(bank[:, 2 * P:3 * P], key[:, n, :], self.ident)
                for h in range(2):
                    u = 2 * ci + h
                    tt = self.mm(bank[:, 3 * P + h * HEAD:3 * P + (h + 1) * HEAD], g["agbh"][:, u, 256:384],
                                 self.vtok[:, n, j * P + h * HEAD:j * P + (h + 1) * HEAD], True, True,
                                 t, signal=True)
                self.act(g["X"][:, ci * 256:ci * 256 + P], bank[:, 0:P], ACT.Copy, tt, free_g, loose=True)
                self.act(g["tok"][:, ci * 256:ci * 256 + 256], bank[:, P:3 * P], ACT.Copy, loose=True)
                t2 = self.act(g["X"][:, ci * 256 + P:ci * 256 + 256], bank[:, 3 * P:4 * P], ACT.Copy, scale=-1.0, loose=True)
                self.bank.read(bi, t2)
        for gi, chunks in enumerate(gs):
            g = G[gi]
            at = g["agbh"][:, :, 0:P]
            bi, bank, free = self.bank.take()
            for u in range(4):
                t = self.mm(bank[:, u * P:(u + 1) * P], at[:, u, :], self.ident, True, True, c.last("dve"), free, signal=(u == 3))
            self.tt(g["Y"], at, four(self.level[other][:, 0, :]), ALU.mult, t)
            self.tt(g["E"], four(self.ident), g["Y"], ALU.subtract)
            self.tt(g["Y"], as4(bank), four(self.level[side][:, 0, :]), ALU.mult, t)
            self.bank.read(bi, c.last("dve"))
            g["t"] = self.tt(g["D"], four(self.ident), g["Y"], ALU.subtract)
        for li, m in enumerate(LEVELS):
            if m == 1:
                continue
            for gi, chunks in enumerate(gs):
                g = G[gi]
                bi, bank, free = self.bank.take()
                for u in range(4):
                    t = self.mm(bank[:, u * P:(u + 1) * P], g["agbh"][:, u, 0:P], g["D"][:, u, :], True, True,
                                g["t"], free, signal=(u == 3))
                g["t"] = self.tt(g["Y"], as4(bank), four(self.level[side][:, li, :]), ALU.mult, t, loose=True)
                self.bank.read(bi, g["t"])
            for gi, chunks in enumerate(gs):
                g = G[gi]
                bi, bank, free = self.bank.take()
                for u in range(4):
                    t = self.mm(bank[:, u * P:(u + 1) * P], g["Y"][:, u, :], g["E"][:, u, :], True, True,
                                g["t"], free, signal=(u == 3))
                g["t"] = self.tt(g["E"], g["E"], as4(bank), ALU.subtract, t, loose=True)
                self.bank.read(bi, g["t"])
            if m == 64:
                break
            for gi, chunks in enumerate(gs):
                g = G[gi]
                bi, bank, free = self.bank.take()
                for u in range(4):
                    t = self.turn(bank[:, u * P:(u + 1) * P], g["E"][:, u, :], self.ident, g["t"], free, signal=(u == 3))
                g["t"] = self.act(g["D"], as4(bank), ACT.Copy, t, loose=True)
                self.bank.read(bi, g["t"])
        for gi, chunks in enumerate(gs):
            g = G[gi]
            x5 = g["X"].rearrange("p (c w h f) -> p c w h f", c=2, w=2, h=2)
            w5 = g["WU"].rearrange("p (c w h f) -> p c w h f", c=2, w=2, h=2)
            bi, bank, free = self.bank.take()
            b5 = bank.rearrange("p (c w h f) -> p c w h f", c=2, w=2, h=2)
            for u in range(4):
                ci, h = u // 2, u % 2
                t = self.mm(b5[:, ci, :, h, :], g["E"][:, u, :], x5[:, ci, :, h, :], True, True, g["t"], c.last("act"), free,
                            signal=(u == 3))
            t = self.copy("act", g["WU"], bank, t, free_g)
            self.bank.read(bi, t)
            bi, bank, free = self.bank.take()
            for ci, n in enumerate(chunks):
                wk, u0 = g["WU"][:, ci * 256:ci * 256 + P], g["WU"][:, ci * 256 + P:ci * 256 + 256]
                bt, kt = g["tok"][:, ci * 256:ci * 256 + P], g["tok"][:, ci * 256 + P:ci * 256 + 256]
                self.mm(bank[:, ci * P:(ci + 1) * P], wk, bt, True, True, t, free)
                self.mm(bank[:, 256 + ci * P:256 + (ci + 1) * P], kt, self.vtok[:, n, j * P:(j + 1) * P], True, False)
                tt = self.mm(bank[:, 256 + ci * P:256 + (ci + 1) * P], bt, u0, False, True, signal=True)
            two = lambda x: x.rearrange("p (c t) -> p c t", c=2)
            hb = self.heads.unsqueeze(1).broadcast_to([P, 2, P])
            ib = self.ident.unsqueeze(1).broadcast_to([P, 2, P])
            self.tt(two(g["M"]), two(bank[:, 0:256]), hb, ALU.mult, tt)
            self.tt(two(g["M"]), ib, two(g["M"]), ALU.subtract)
            t2 = self.tt(two(g["N"]), two(bank[:, 256:512]), hb, ALU.mult)
            self.bank.read(bi, t2)
            bi, bank, free = self.bank.take()
            for ci in range(2):
                tt = self.turn(bank[:, ci * P:(ci + 1) * P], g["WU"][:, ci * 256:ci * 256 + P], self.ident, t, free, signal=(ci == 1))
            self.bank.read(bi, self.copy("act", g["WT"], bank[:, 0:256], tt))

    def chunk_step(self, g, ci, n, kr, gain, S, si, first, j, fwd, yacc, final):
        c = self.c
        s, s_next = S[si], S[si ^ 1]
        M, N = g["M"][:, ci * P:(ci + 1) * P], g["N"][:, ci * P:(ci + 1) * P]
        col = gain[:, n:n + 1]
        out = n >= 2
        ready = [c.last("dve"), c.last("act")]
        if not final:
            if first:
                self.ts(s_next, N, col, None, ALU.mult, ALU.bypass, c.last("pe"))
            else:
                self.ts(N, N, col, None, ALU.mult, ALU.bypass)
                bi, bank, free = self.bank.take()
                t = self.mm(bank[:, 0:P], M, s, True, True, ready, free, signal=True)
                t = self.stt(s_next, bank[:, 0:P], col, N, ALU.mult, ALU.add, t)
                self.bank.read(bi, t)
        if out:
            bi, bank, free = self.bank.take()
            t = self.mm(bank[:, 0:P], g["WT"][:, ci * P:(ci + 1) * P], s, True, True, ready, free, signal=True)
            u = g["U"][:, ci * P:(ci + 1) * P]
            t = self.tt(u, g["WU"][:, ci * 256 + P:ci * 256 + 256], bank[:, 0:P], ALU.subtract, t)
            self.bank.read(bi, t)
            bi, bank, free = self.bank.take()
            self.mm(bank[:, 0:P], kr[:, n, 1, :], s, True, False, free)
            for h in range(2):
                uu = 2 * ci + h
                cols = slice(h * HEAD, (h + 1) * HEAD)
                self.mm(bank[:, cols], g["agbh"][:, uu, 384:512], self.vtok[:, n, j * P + h * HEAD:j * P + (h + 1) * HEAD],
                        False, False)
                y = self.mm(bank[:, cols], g["agbh"][:, uu, 128:256], u[:, cols], False, h == 1, t, signal=(h == 1))
            dst = yacc[:, n - 2, j * P:(j + 1) * P]
            if fwd:
                t = self.copy("act", dst, bank[:, 0:P], y)
            else:
                t = self.tt(dst, dst, bank[:, 0:P], ALU.add, y)
            self.bank.read(bi, t)

    def rwkv_output(self, yacc, bonus, g2, lora_ready):
        c, sb, io = self.c, self.sb, self.io
        c.new_phase()
        sb.at = self.hT_at
        yrT_at = sb.at
        self.yrT = sb.take(4 * SEQ, j=4)
        lnw, lnb = sb.take(RW), sb.take(RW)
        stat = sb.take(128)
        sq = self.sb.t[:, self.rwkv_keep + 200:self.rwkv_keep + 200 + 4096]
        got = [c.dma("act", "lnx", t, io[n].partition_broadcast(P)[:, 0, :], c.everything()) for n, t in (("ln_x_w", lnw), ("ln_x_b", lnb))]
        y = yacc.rearrange("p i (h f) -> p (i h) f", f=HEAD)
        s3 = sq.rearrange("p (g f) -> p g f", f=HEAD)
        mean, var = stat[:, 0:64], stat[:, 64:128]
        bc = lambda x: x.unsqueeze(2).broadcast_to([P, 64, HEAD])
        t = c.put("dve", lambda e: e.tensor_reduce(mean, y, AX.X, ALU.add))
        self.ts(mean, mean, 1.0 / HEAD, None, ALU.mult, ALU.bypass)
        t = self.tt(y, y, bc(mean), ALU.subtract)
        t = self.act(s3, y, ACT.Square, t)
        c.put("dve", lambda e: e.tensor_reduce(var, s3, AX.X, ALU.add), t)
        self.rstd(var, var, HEAD, 64e-5)
        self.tt(y, y, bc(var), ALU.mult)
        row = lambda x: x.unsqueeze(1).broadcast_to([P, NT, RW])
        self.tt(yacc, yacc, row(lnw), ALU.mult, got[-1])
        self.tt(yacc, yacc, row(lnb), ALU.add)
        v = self.vtok[:, 2:10, :]
        for i in range(NT):
            vi = self.vtok[:, 2 + i, :].rearrange("p (h f) -> p h f", f=HEAD)
            self.tt(s3[:, 8 * i:8 * i + 8, :], vi, bonus[:, i, :].unsqueeze(2).broadcast_to([P, 8, HEAD]), ALU.mult, eng="dve")
        self.tt(yacc, yacc, sq.rearrange("p (i f) -> p i f", f=RW), ALU.add)
        for i in range(NT):
            bi, bank, free = self.bank.take()
            t = self.mm(bank, self.gl[0:GATE, i * P:(i + 1) * P], g2[0:GATE, :], True, True, lora_ready, free, c.last("act"), signal=True)
            t = self.tt(yacc[:, i, :], yacc[:, i, :], bank, ALU.mult, t)
            self.bank.read(bi, t)
        for g in range(2):
            self.turn_rows(lambda i: yacc[:, i, :], range(4 * g, 4 * g + 4),
                           lambda j, bank, t_: self.copy("act" if j % 2 else "dve", self.yrT[:, j, g * 512:(g + 1) * 512], bank, t_, loose=True),
                           t, kt=4)
        self.yr_ready = [c.last("act"), c.last("dve")]

    def gate_row(self, out, col, gain):
        c = self.c
        for half in range(2):
            bi, bank, free = self.bank.take()
            for j in range(4):
                jj = 4 * half + j
                t = self.stt(self.diag[:, j * P:(j + 1) * P], self.ident, col[:, jj:jj + 1],
                             gain[:, jj:jj + 1].broadcast_to([P, P]), ALU.mult, ALU.mult, c.last("pe"), c.last("act"))
            t = self.mm(bank, self.ones, self.diag, True, True, t, free, signal=True)
            t = self.act(out[:, half * 512:(half + 1) * 512], bank, ACT.Copy, t)
            self.bank.read(bi, t)
        return t

    def rows_product(self, lhs, w_dram, tiles, evac, ready, rows=None):
        c = self.c
        for n in range(2):
            wi, w, got = self.w_block(w_dram, n * 512, 512)
            for i in range(tiles):
                m = P if rows is None else rows(i)
                bi, bank, free = self.bank.take()
                for k in range(KD):
                    t = self.mm(bank[0:m, :], lhs(k, i), w[:, k, :], k == 0, k == KD - 1, got, free, ready,
                                signal=(k == KD - 1))
                self.bank.read(bi, evac(n, i, bank, t))
            self.weights.read(wi, c.last("pe"))

    def post_norm(self, y, x, ssq, row, i, ready):
        self.stt(y[:, i, :], y[:, i, :], ssq[:, i:i + 1], row, ALU.mult, ALU.mult, ready)
        return self.tt(x[:, i, :], x[:, i, :], y[:, i, :], ALU.add)

    def mix_out(self):
        c, sb, io = self.c, self.sb, self.io
        c.new_phase()
        for i in range(self.w_slots):
            self.weights.read(i, *c.everything())
        self.yrT_keep = self.yrT
        sb.at = self.hT_at + 4 * SEQ
        ydT = sb.take(4 * SEQ, h=4)
        back = c.dma("act", "load_yd", ydT, self.yd_dram, c.everything(), self.yd_spilled)
        y, x = sb.take(NT * D, i=NT), sb.take(NT * D, i=NT)
        row1 = sb.take(D)
        self.diag = sb.take(512)
        ssq = sb.take(3 * NT)
        junk = sb.take(512)
        gotx = c.dma("act", "load_x", x, io["x"][0].rearrange("(i p) d -> p i d", p=P))
        self.mod_blocks(range(4, 12))
        self.gate_row(row1, self.mod[:, 16:24], self.col["g_post_mix"])

        def evac(n, i, bank, t):
            a = self.copy("dve", y[:, i, n * 512:(n + 1) * 512], bank, t, loose=True)
            b = self.act(junk, y[:, i, n * 512:(n + 1) * 512], ACT.Square, a, accum=ssq[:, n * NT + i:n * NT + i + 1])
            return a, b

        yT = lambda k, i: (self.yrT if k < 4 else ydT)[:, k % 4, i * P:(i + 1) * P]
        wrap = lambda n, i, bank, t: list(evac(n, i, bank, t))
        self.rows_product(yT, io["w_out"][0], NT, wrap, [self.yr_ready, back])
        total = ssq[:, 2 * NT:3 * NT]
        self.tt(total, ssq[:, 0:NT], ssq[:, NT:2 * NT], ALU.add, c.last("act"))
        self.rstd(total, total, D, 1e-6)
        for i in range(NT):
            t = self.post_norm(y, x, total, row1, i, [gotx])
            sq = self.act(y[:, i, :], x[:, i, :], ACT.Square, t, accum=ssq[:, i:i + 1])
        self.x1_dram = self.nc.dram_tensor("x1_spill", (P, NT, D), F32).ap()
        self.x1_spilled = c.dma("act", "spill_x1", self.x1_dram, x, t)
        r = self.rstd(ssq[:, 0:NT], ssq[:, 0:NT], D, 1e-6, sq)
        for i in range(NT):
            t = self.ts(y[:, i, :], x[:, i, :], ssq[:, i:i + 1], None, ALU.mult, ALU.bypass, r, loose=True)
        gs2 = sb.take(KD)
        self.stt(gs2, self.mod[:, 32:40], 1.0, self.col["g_pre_ffn"], ALU.add, ALU.mult)
        self.h2T = sb.view(self.hT_at, KD * SEQ, k=KD)
        sh2 = self.mod[:, 24:32]
        before = [c.last("pe"), c.last("dve")]
        for g in range(2):
            def emit(j, bank, t, g=g):
                out = self.h2T[:, j, g * 512:(g + 1) * 512]
                if j % 2:
                    return self.act(out, bank, ACT.Identity, t, before, scale=gs2[:, j:j + 1], bias=sh2[:, j:j + 1], loose=True)
                return self.ts(out, bank, gs2[:, j:j + 1], sh2[:, j:j + 1], ALU.mult, ALU.add, t, before, loose=True)
            self.turn_rows(lambda i: y[:, i, :], range(4 * g, 4 * g + 4), emit, t)
        self.h2_ready = [c.last("act"), c.last("dve")]

    def mlp(self):
        c, sb, io = self.c, self.sb, self.io
        c.new_phase()
        for e in ("pe", "dve", "act", "pool"):
            c.held[e].append(self.x1_spilled)
        sb.at = self.hT_at + KD * SEQ
        hid = sb.take(KF * SEQ, k=KF)
        raws = Ring([sb.take(SEQ + 2) for _ in range(2)])
        cv, cg = sb.take(SEQ), sb.take(SEQ)
        for raw in raws.slots:
            pads = [self.fill(raw[:, n:n + 1], 0.0) for n in (0, SEQ + 1)]
        h2T = lambda k, a, b: self.h2T[:, k, a:b]
        w_up = io["w_up"][0]

        def conv(out, raw, tile):
            taps = [self.col[f"fconv{t}"][:, tile:tile + 1] for t in range(3)]
            self.ts(out, raw[:, 1:1 + SEQ], taps[1], self.col["ffn_conv_b"][:, tile:tile + 1], ALU.mult, ALU.add,
                    c.last("act"), pads)
            self.stt(out, raw[:, 0:SEQ], taps[0], out, ALU.mult, ALU.add)
            return self.stt(out, raw[:, 2:2 + SEQ], taps[2], out, ALU.mult, ALU.add)

        for blk in range(KF // 2):
            def parts(slot, blk=blk):
                v = slot.rearrange("p (k n) -> p k n", n=512)
                src = lambda c0: w_up[:, c0:c0 + 256].rearrange("(k p) n -> p k n", p=P)
                yield v[:, :, 0:256], src(blk * 256)
                yield v[:, :, 256:512], src(FF + blk * 256)
            wi, slot, got = self.load_block(parts)
            w = slot.rearrange("p (k n) -> p k n", n=512)
            for half in range(2):
                tile = 2 * blk + half
                for gate, dst in ((0, cv), (1, cg)):
                    ri, raw, free = raws.take()
                    c0 = 256 * gate + P * half
                    self.product(lambda k: w[:, k, c0:c0 + P], h2T, [(0, 512), (512, 1024)], KD, P, [got, self.h2_ready],
                                 lambda s, bank, t: self.copy("act", raw[:, 1 + s * 512:1 + (s + 1) * 512], bank, t, free, loose=True))
                    t = conv(dst, raw, tile + gate * KF)
                    raws.read(ri, t)
                t = self.act(cg, cg, ACT.Silu, t)
                t = self.tt(hid[:, tile, :], cv, cg, ALU.mult, t)
            self.weights.read(wi, c.last("pe"))

        y = self.h2T_rows = sb.view(self.hT_at, NT * D, i=NT)
        ssq = cv[:, 0:3 * NT]
        junk = cg[:, 0:512]
        up_done = c.everything()
        for n in range(2):
            held = [self.bank.take() for _ in range(NT)]
            for k0 in range(0, KF, KD):
                kn = min(KD, KF - k0)
                wi, w, got = self.w_block(io["w_down"][0], n * 512, 512, k0=k0, k=kn)
                for i in range(NT):
                    bi, bank, free = held[i]
                    for k in range(kn):
                        t = self.mm(bank, hid[:, k0 + k, i * P:(i + 1) * P], w[:, k, :], k0 + k == 0, k0 + k == KF - 1,
                                    got, free, up_done, signal=(k == kn - 1))
                    if k0 + kn == KF:
                        a = self.copy("dve", y[:, i, n * 512:(n + 1) * 512], bank, t, loose=True)
                        b = self.act(junk, y[:, i, n * 512:(n + 1) * 512], ACT.Square, a, accum=ssq[:, n * NT + i:n * NT + i + 1])
                        self.bank.read(bi, a, b)
                self.weights.read(wi, c.last("pe"))
        c.new_phase()
        sb.at = self.hT_at + KD * SEQ
        x = sb.take(NT * D, i=NT)
        row2 = sb.take(D)
        self.diag = sb.take(512)
        hT2 = sb.take(KD * L2, k=KD)
        back = c.dma("act", "load_x1", x, self.x1_dram, c.everything())
        total = ssq[:, 2 * NT:3 * NT]
        self.tt(total, ssq[:, 0:NT], ssq[:, NT:2 * NT], ALU.add)
        self.rstd(total, total, D, 1e-6)
        self.gate_row(row2, self.mod[:, 40:48], self.col["g_post_ffn"])
        for i in range(NT):
            t = self.post_norm(y, x, total, row2, i, [back, c.last("act")])
        self.x2_dram = self.nc.dram_tensor("x2_spill", (P, NT, D), F32).ap()
        self.x2_spilled = c.dma("act", "spill_x2", self.x2_dram, x, t)
        meta = sb.take(D)
        gm = c.dma("act", "load_meta", meta[0:META, :], io["meta_2"], c.everything())
        self.hcT, self.hcT_ready = hT2, self.turn_both(hT2, x, meta, [t, gm])
        self.hcT_end = sb.at

    def turn_both(self, out, x, meta, ready):
        c = self.c
        for j in range(KD):
            if j % 4 == 0:
                bi, bank, free = self.bank.take()
            t = self.turn(bank[:, j % 4 * META:(j % 4 + 1) * META], meta[0:META, j * P:(j + 1) * P],
                          self.ident[0:META, 0:META], ready, free, signal=True)
            if j % 4 == 3:
                t = self.copy("dve", out[:, j - 3:j + 1, 0:META], bank[:, 0:4 * META].rearrange("p (k t) -> p k t", k=4), t)
                self.bank.read(bi, t)
        for g in range(2):
            self.turn_rows(lambda i: x[:, i, :], range(4 * g, 4 * g + 4),
                           lambda j, bank, t: self.copy("act" if j % 2 else "dve", out[:, j, META + g * 512:META + (g + 1) * 512],
                                                        bank, t, loose=True), ready)
        return [c.last("act"), c.last("dve")]

    def conformer(self):
        c, sb, io = self.c, self.sb, self.io
        SP = self.spans2 = [(0, 352), (352, 696), (696, L2)]
        lo = self.hT_at
        conv = sb.view(lo, KD * L2, k=KD)
        c.new_phase()
        for e in ("pe", "dve", "act", "pool"):
            c.held[e].append(self.x2_spilled)
        sb.at = self.hcT_end
        zs = sb.take(KD * L2, k=KD)
        sb.at = lo + KD * L2
        glus = Ring([sb.take(L2 + TAPS - 1) for _ in range(2)])
        sig = [sb.take(L2) for _ in range(2)]
        assert sb.at <= self.hT_at + 2 * KD * SEQ + D + 512
        for g in glus.slots:
            pad = self.fill(g[:, 0:TAPS - 1], 0.0)
        hT = lambda k, a, b: self.hcT[:, k, a:b]
        w_in = io["conv_w_in_2"][0]
        b_in = self.col["conv_b_in"]
        dw = lambda r: self.col["dw_a"][:, r:r + 1] if r < 124 else self.col["dw_b"][:, r - 124:r - 123]
        for j in range(KD):
            def parts(slot, j=j):
                v = slot[:, 0:KD * 384].rearrange("p (k n) -> p k n", n=384)
                for part in range(3):
                    c0 = (1, 0, 2)[part] * D + j * P
                    yield v[:, :, part * P:(part + 1) * P], w_in[:, c0:c0 + P].rearrange("(k p) n -> p k n", p=P)
            wi, slot, got = self.load_block(parts)
            w = slot[:, 0:KD * 384].rearrange("p (k n) -> p k n", n=384)
            s1 = sig[j % 2]
            gi, glu, gfree = glus.take()

            def gate(s, bank, t):
                a, b = SP[s]
                return self.act(s1[:, a:b], bank, ACT.Sigmoid, t, c.last("dve"), bias=b_in[:, 8 + j:9 + j])

            def value(s, bank, t):
                a, b = SP[s]
                return self.stt(glu[:, TAPS - 1 + a:TAPS - 1 + b], bank, b_in[:, j:j + 1], s1[:, a:b], ALU.add, ALU.mult, t,
                                c.last("act"), gfree, pad)

            def zgate(s, bank, t):
                a, b = SP[s]
                out = zs[:, j, a:b]
                t = self.act(out, bank, ACT.Sigmoid, t, bias=b_in[:, 16 + j:17 + j])
                return self.stt(out, bank, b_in[:, 16 + j:17 + j], out, ALU.add, ALU.mult, t)

            for part, emit in enumerate((gate, value, zgate)):
                self.product(lambda k: w[:, k, part * P:(part + 1) * P], hT, SP, KD, P, [got, self.hcT_ready], emit)
            self.weights.read(wi, c.last("pe"))
            o = conv[:, j, :]
            self.ts(o, glu[:, 0:L2], dw(j), self.col["conv_b_dw"][:, j:j + 1], ALU.mult, ALU.add)
            for tap in range(1, TAPS):
                t = self.stt(o, glu[:, tap:tap + L2], dw(tap * KD + j), o, ALU.mult, ALU.add)
            glus.read(gi, t)

        mean, sq = sig, glus.slots

        def channel_sum(src, out, ready_of):
            held = [self.bank.take() for _ in SP]
            for k in range(KD):
                r = ready_of(k)
                for (a, b), (bi, bank, free) in zip(SP, held):
                    t = self.mm(bank[:, 0:b - a], self.ones, src(k)[:, a:b], k == 0, k == KD - 1, r, free, signal=True)
                self.sum_read = t
            for (a, b), (bi, bank, free) in zip(SP, held):
                tt = self.act(out[:, a:b], bank[:, 0:b - a], ACT.Copy, t, scale=1.0 / D)
                self.bank.read(bi, tt)
            return tt

        t = c.last("dve")
        m_t = channel_sum(lambda k: conv[:, k, :], mean[0], lambda k: t)
        sqs = [None, None]

        def centred(k):
            o = conv[:, k, :]
            t = self.tt(o, o, mean[0], ALU.subtract, m_t, c.last("pe"))
            t = self.act(sq[k % 2][:, 0:L2], o, ACT.Square, t, sqs[k % 2], loose=True)
            sqs[(k + 1) % 2] = c.last("pe")
            return t

        v_t = channel_sum(lambda k: sq[k % 2][:, 0:L2], mean[1], centred)
        self.ts(mean[1], mean[1], 1e-5, None, ALU.add, ALU.bypass, v_t)
        self.act(mean[1], mean[1], ACT.Sqrt, c.last("dve"))
        self.recip(mean[1], mean[1], c.last("act"))
        for k in range(KD):
            o = conv[:, k, :]
            t = self.tt(o, o, mean[1], ALU.mult)
            self.act(o, o, ACT.Silu, t, scale=self.col["conv_norm_g"][:, k:k + 1], bias=self.col["conv_norm_b"][:, k:k + 1], loose=True)
        for k in range(KD):
            o = conv[:, k, :]
            ready = self.tt(o, o, zs[:, k, :], ALU.mult, c.last("act"))
        c.new_phase()
        sb.at = lo + KD * L2
        x = sb.take(NT * D, i=NT)
        meta, brow, grow, lrow = (sb.take(D) for _ in range(4))
        self.ln_stat = sb.take(64)
        self.h1T = sb.take(KD * L2, k=KD)
        self.h1T_end = sb.at
        e = c.everything()
        c.dma("act", "rows2", x, self.x2_dram, e)
        c.dma("act", "rows2", meta[0:META, :], io["meta_2"])
        c.dma("act", "rows2", brow, io["conv_b_out_2"].partition_broadcast(P)[:, 0, :])
        c.dma("act", "rows2", grow, io["post_ln_g_2"][0:1].partition_broadcast(P)[:, 0, :])
        got = c.dma("act", "rows2", lrow, io["post_ln_b_2"][0:1].partition_broadcast(P)[:, 0, :])
        for i in range(NT):
            self.stt(x[:, i, :], x[:, i, :], DN_ALPHA, brow, ALU.mult, ALU.add, got, loose=True)
        self.stt(meta[0:META, :], meta[0:META, :], DN_ALPHA, brow[0:META, :], ALU.mult, ALU.add, got)
        row = lambda i: x[:, i, :] if i < NT else meta[0:META, :]

        def evac(n, i, bank, t):
            r = row(i)[:, n * 512:(n + 1) * 512]
            return self.tt(r, r, bank[0:META, :] if i == NT else bank, ALU.add, t)

        self.rows_product(lambda k, i: conv[:, k, META + i * P:META + (i + 1) * P] if i < NT else conv[:, k, 0:META],
                          io["conv_w_out_2"][0], NT + 1, evac, [ready], rows=lambda i: P if i < NT else META)
        for i in range(NT + 1):
            t = self.layer_norm(row(i), grow, lrow, P if i < NT else META)
        self.h1_dram = self.nc.dram_tensor("h1_spill", (P, NT, D), F32).ap()
        self.h1_spilled = c.dma("act", "spill_h1", self.h1_dram, x, t)
        self.h1_ready = self.turn_both(self.h1T, x, meta, [t])

    def layer_norm(self, r, grow, lrow, m):
        c = self.c
        st = self.ln_stat[0:m]
        for n in range(2):
            c.put("dve", lambda e, n=n: e.bn_stats(st[:, 6 * n:6 * n + 6], r[:, n * 512:(n + 1) * 512]), c.last("act"))
        c.put("dve", lambda e: e.bn_aggr(st[:, 12:14], st[:, 0:12]))
        self.ts(st[:, 14:15], st[:, 13:14], 1e-5, None, ALU.add, ALU.bypass)
        t = self.act(st[:, 14:15], st[:, 14:15], ACT.Sqrt, c.last("dve"))
        self.recip(st[:, 15:16], st[:, 14:15], t)
        self.ts(r, r, st[:, 12:13], st[:, 15:16], ALU.subtract, ALU.mult)
        self.tt(r, r, grow[0:m, :], ALU.mult)
        return self.tt(r, r, lrow[0:m, :], ALU.add)

    def gla(self):
        c, sb, io = self.c, self.sb, self.io
        NCH = 9
        LP = NCH * P
        c.new_phase()
        for e in ("pe", "dve", "act", "pool"):
            c.held[e].append(self.h1_spilled)
        sb.at = self.hT_at
        limit = self.h1T_end - KD * L2
        q, k = sb.take(GH * LP, h=GH), sb.take(GH * LP, h=GH)
        v = sb.take(NCH * D, i=NCH)
        a1 = sb.take(L2)
        wa2 = sb.take(512)
        assert sb.at <= limit
        sb.at = self.h1T_end
        b = sb.take(GH * LP, h=GH)
        h1T = lambda kk, x, y: self.h1T[:, kk, x:y]
        for t in (q, k, b):
            pad = self.fill(t[:, :, L2:LP], 0.0)
        gw = c.dma("act", "gla_a2", wa2[0:16, :], io["gla_w_a2_2"][0], c.everything())
        w_in = io["gla_w_in_2"][0]
        SP = self.spans2
        for c0, dst, scale in ((0, q, GK ** -0.5), (512, k, 1.0)):
            self.dense(w_in, c0, 512, h1T, SP, lambda j, s, bank, t: self.act(
                dst[:, j, SP[s][0]:SP[s][1]], bank, ACT.Copy, t, scale=scale, loose=True), self.h1_ready)
        for n in range(2):
            wi, w, got = self.w_block(w_in, 1024 + n * 512, 512)
            for i in range(NCH):
                m = P if i < 8 else META
                bi, bank, free = self.bank.take()
                for kk in range(KD):
                    t = self.mm(bank[0:m, :], self.h1T[:, kk, i * P:i * P + m], w[:, kk, :], kk == 0, kk == KD - 1, got, free,
                                signal=(kk == KD - 1))
                self.bank.read(bi, self.copy("dve" if i % 2 else "act", v[0:m, i, n * 512:(n + 1) * 512], bank[0:m, :], t, loose=True))
            self.weights.read(wi, c.last("pe"))
        wi, w, got = self.w_block(w_in, 3072, 16)
        self.product(lambda kk: w[:, kk, 0:16], h1T, SP, KD, 16, [got], lambda s, bank, t: self.copy("act", a1[0:16, SP[s][0]:SP[s][1]], bank, t, loose=True))
        self.weights.read(wi, c.last("pe"))
        g0, g1 = sb.take(L2), a1
        c.new_phase()
        reset = sb.view(self.w_at + 3 * SLOT - 2 * LP, LP)
        A = sb.view(self.w_at + 3 * SLOT - LP, LP, i=NCH)
        g1 = sb.view(self.w_at, L2)
        self.fill(reset, 1.0)
        self.fill(reset.rearrange("p (n t) -> p n t", t=P)[:, :, 0:1], 0.0)
        pad = self.fill(A, 0.0)
        ba = self.col["gla_b_a"]
        for h in range(GH):
            for s, (x, y) in enumerate(SP):
                bi, bank, free = self.bank.take()
                bk = bank[:, 0:y - x]
                t = self.mm(bk, wa2[0:16, h * P:(h + 1) * P], a1[0:16, x:y], True, True, gw, c.last("act"), free, signal=True)
                t2 = self.ts(b[:, h, x:y], bk, ba[:, h:h + 1], 0.0, ALU.add, ALU.min, t)
                t = self.act(g0[:, x:y], bk, ACT.Abs, t, t2, c.last("dve"), bias=ba[:, h:h + 1])
                self.bank.read(bi, t, t2)
            self.act(g0, g0, ACT.Exp, scale=-1.0)
            t = self.act(g1, g0, ACT.Ln, c.last("dve"), bias=1.0)
            self.tt(b[:, h, 0:L2], b[:, h, 0:L2], g1, ALU.subtract, t)
            c.put("dve", lambda e, bb=b[:, h, :]: e.tensor_tensor_scan(bb, reset, bb, 0.0, ALU.mult, ALU.add), pad)
        sb2 = self.w_at
        c.new_phase()
        take = lambda n: sb.view(sb2, n)
        e_, qx = take(LP), sb.view(sb2 + LP, LP)
        kx, S = sb.view(sb2 + 2 * LP, LP), [sb.view(sb2 + 3 * LP + n * GV, GV) for n in range(2)]
        kd, kt = sb.view(sb2 + 3 * LP + 2 * GV, LP), sb.view(sb2 + 4 * LP + 2 * GV, LP, i=NCH)
        o = sb.view(sb2 + 5 * LP + 2 * GV, NCH * GV, i=NCH)
        st = sb.view(sb2 + 5 * LP + 2 * GV + NCH * GV, 64)
        junk = sb.view(sb2 + 5 * LP + 2 * GV + NCH * GV + 64, GV)
        assert 7 * LP + 3 * GV + NCH * GV + 64 <= self.w_slots * SLOT
        oT = lambda kk: (q if kk % 2 == 0 else k)[:, kk // 2, :]
        blocks = lambda x, m: x.rearrange("p (n j) -> p n j", j=2 * m)
        self.fill(qx, 0.0)
        pad = self.fill(kx, 0.0)
        chunks = lambda x: x.rearrange("p (n t) -> p n t", t=P)
        sets = ((0, 4), (4, 8), (8, 9))
        for h in range(GH):
            bh, qh, kh = b[:, h, :], q[:, h, :], k[:, h, :]
            for li, m in enumerate((0,) + LEVELS):
                if m:
                    ref = blocks(bh, m)[:, :, m - 1:m].broadcast_to([P, LP // (2 * m), m])
                    bb, ee = blocks(bh, m), blocks(e_, m)
                    self.tt(ee[:, :, m:], bb[:, :, m:], ref, ALU.subtract, c.last("act"))
                    t = self.tt(ee[:, :, 0:m], ref, bb[:, :, 0:m], ALU.subtract, loose=True)
                    t = self.act(e_, e_, ACT.Exp, t, scale=1.0 / 16)
                    self.tt(blocks(qx, m)[:, :, m:], blocks(qh, m)[:, :, m:], ee[:, :, m:], ALU.mult, t, pad, c.last("pe"))
                    t = self.tt(blocks(kx, m)[:, :, 0:m], blocks(kh, m)[:, :, 0:m], ee[:, :, 0:m], ALU.mult, loose=True)
                    lq, lk, mask = qx, kx, self.level["upper"][:, li - 1, :]
                else:
                    lq, lk, mask, t = qh, kh, self.ident, c.everything()
                for x, y in sets:
                    bi, bank, free = self.bank.take()
                    for n in range(x, y):
                        tt = self.mm(bank[:, (n - x) * P:(n - x + 1) * P], chunks(lk)[:, n, :], chunks(lq)[:, n, :], True, True,
                                     t, free, signal=(n == y - 1))
                    w_ = y - x
                    tt = c.put("dve", lambda e, out=A[:, x:y, :], mk=mask.bitcast(I32).unsqueeze(1).broadcast_to([P, w_, P]),
                               dat=bank[:, 0:w_ * P].rearrange("p (n t) -> p n t", t=P): e.copy_predicated(out, mk, dat), tt)
                    self.bank.read(bi, tt)
            last = chunks(bh)[:, :, P - 1:P]
            t = self.act(e_, bh, ACT.Exp, c.last("dve"), scale=1.0 / 16)
            self.tt(qx, qh, e_, ALU.mult, t, c.last("pe"))
            self.copy("dve", st[:, 0:NCH], e_.rearrange("p (n t) -> p n t", t=P)[:, :, P - 1])
            t = self.tt(chunks(e_), last.broadcast_to([P, NCH, P]), chunks(bh), ALU.subtract)
            t = self.act(e_, e_, ACT.Exp, t, scale=1.0 / 16)
            t = self.tt(kd, kh, e_, ALU.mult, t)
            for x, y in sets:
                bi, bank, free = self.bank.take()
                for n in range(x, y):
                    tt = self.turn(bank[:, (n - x) * P:(n - x + 1) * P], chunks(kd)[:, n, :], self.ident, t, free, signal=(n == y - 1))
                self.bank.read(bi, self.copy("act", kt[:, x:y, :], bank[:, 0:(y - x) * P].rearrange("p (n t) -> p n t", t=P), tt, loose=True))
            ready = [c.last("act"), c.last("dve")]
            for n in range(NCH):
                m = P if n < 8 else META
                vn = v[0:m, n, h * GV:(h + 1) * GV]
                bi, bank, free = self.bank.take()
                t = self.mm(bank[0:m, 0:GV], A[0:m, n, 0:m], vn, True, n == 0, ready, free, signal=True)
                if n:
                    t = self.mm(bank[0:m, 0:GV], chunks(qx)[:, n, 0:m], S[n % 2], False, True, c.last("dve"), signal=True)
                tt = self.act(o[0:m, n, :], bank[0:m, 0:GV], ACT.Copy, t, loose=True)
                t3 = self.act(junk[0:m, :], bank[0:m, 0:GV], ACT.Square, t, accum=st[0:m, 16 + n:17 + n])
                self.bank.read(bi, tt, t3)
                if n < NCH - 1:
                    bi, bank, free = self.bank.take()
                    t = self.mm(bank[:, 0:GV], kt[:, n, :], vn, True, True, ready, free, signal=True)
                    if n == 0:
                        t = self.copy("dve", S[1], bank[:, 0:GV], t)
                    else:
                        t = self.stt(S[(n + 1) % 2], S[n % 2], st[:, n:n + 1], bank[:, 0:GV], ALU.mult, ALU.add, t, c.last("pe"))
                    self.bank.read(bi, t)
            for m, x, y in ((P, 16, 24), (META, 24, 25)):
                sl = st[0:m, x:y]
                self.rstd(sl, sl, GV, 1e-6, t3)
            for n in range(NCH):
                m = P if n < 8 else META
                t = self.ts(o[0:m, n, :], o[0:m, n, :], st[0:m, 16 + n:17 + n], None, ALU.mult, ALU.bypass, loose=(n > 0))
            for half in range(2):
                for x, y in sets:
                    bi, bank, free = self.bank.take()
                    for n in range(x, y):
                        m = P if n < 8 else META
                        tt = self.turn(bank[:, (n - x) * P:(n - x) * P + m], o[0:m, n, half * P:(half + 1) * P], self.ident[0:m, 0:m],
                                       t, free, signal=(n == y - 1))
                    w_ = min(L2, y * P) - x * P
                    self.bank.read(bi, self.ts(oT(2 * h + half)[:, x * P:x * P + w_], bank[:, 0:w_], self.col["gla_norm_g"][:, half:half + 1],
                                               None, ALU.mult, ALU.bypass, tt, loose=True))
        c.new_phase()
        for i in range(self.w_slots):
            self.weights.read(i, *c.everything())
        sg = Ring([g0, a1])
        for blk in range(2):
            wi, w, got = self.w_block(w_in, 2048 + blk * 512, 512)
            for j in range(4):
                jj = 4 * blk + j
                gi, gbuf, gfree = sg.take()

                def emit(s, bank, t):
                    x, y = SP[s]
                    t = self.act(gbuf[:, x:y], bank, ACT.Silu, t, gfree, loose=True)
                    u = self.tt(oT(jj)[:, x:y], oT(jj)[:, x:y], gbuf[:, x:y], ALU.mult, t, loose=True)
                    sg.read(gi, u)
                    return t
                self.product(lambda kk: w[:, kk, j * P:(j + 1) * P], h1T, SP, KD, P, [got], emit)
            self.weights.read(wi, c.last("pe"))
        ready = c.last("dve")
        sb.at = self.hT_at + 2 * GH * LP
        x = sb.take(NT * D, i=NT)
        grow, lrow = sb.take(D), sb.take(D)
        self.ln_stat = sb.take(64)
        c.dma("act", "rows3", x, self.h1_dram, c.everything())
        c.dma("act", "rows3", grow, io["post_ln_g_2"][1:2].partition_broadcast(P)[:, 0, :])
        got = c.dma("act", "rows3", lrow, io["post_ln_b_2"][1:2].partition_broadcast(P)[:, 0, :])

        def evac(n, i, bank, t):
            r = x[:, i, n * 512:(n + 1) * 512]
            return self.stt(r, r, DN_ALPHA, bank, ALU.mult, ALU.add, t, got)

        self.rows_product(lambda kk, i: oT(kk)[:, META + i * P:META + (i + 1) * P], io["gla_w_out_2"][0], NT, evac, [ready])
        out = io["out"][0].rearrange("(i p) d -> p i d", p=P)
        for i in range(NT):
            t = self.layer_norm(x[:, i, :], grow, lrow, P)
            c.dma("sp", "out", out[:, i, :], x[:, i, :], t)

def build(nc, io):
    with ExitStack() as ctx:
        k = Kernel(nc, io, ctx)
        k.constants()
        k.open_weights()
        k.modulation()
        k.first_norm()
        k.attention()
        k.rwkv_project()
        k.rwkv()
        k.mix_out()
        k.mlp()
        k.conformer()
        k.gla()
        k.c.emit()


NAMES = ["x", "c", "ctx", "c_ctx", "w_mod", "b_mod", "g_pre_mix", "g_post_mix", "g_pre_ffn", "g_post_ffn", "w_in",
         "rwkv_conv", "w0_fwd", "w2_fwd", "a0_fwd", "a2_fwd", "w0_bwd", "w2_bwd", "a0_bwd", "a2_bwd", "g2", "k_k",
         "k_a", "r_k", "ln_x_w", "ln_x_b", "lam_q1", "lam_k1", "lam_q2", "lam_k2", "subln_w", "w_out", "w_up",
         "ffn_conv", "ffn_conv_b", "w_down", "meta_2", "conv_w_in_2", "conv_b_in_2", "conv_w_dw_2", "conv_b_dw_2",
         "conv_norm_g_2", "conv_norm_b_2", "conv_w_out_2", "conv_b_out_2", "gla_w_in_2", "gla_w_a2_2", "gla_b_a_2",
         "gla_norm_g_2", "gla_w_out_2", "post_ln_g_2", "post_ln_b_2"]


def rope_tables():
    import numpy as np
    pairs = HEAD // 4
    row = np.repeat(np.arange(SEQ // 64, dtype=np.float32), 64)
    col = np.tile(np.arange(64, dtype=np.float32), SEQ // 64)
    inv = (np.float32(10000.0) ** (-np.arange(pairs, dtype=np.float32) / np.float32(pairs))).astype(np.float32)
    ang = np.concatenate([row[:, None] * inv, col[:, None] * inv], axis=-1)
    turn = np.zeros((P, P), np.float32)
    for p in range(P):
        if p % HEAD < HEAD // 2:
            turn[p + HEAD // 2, p] = -1.0
        else:
            turn[p - HEAD // 2, p] = 1.0
    tile = lambda t: np.ascontiguousarray(np.tile(t.T, (4, 1)).astype(np.float32))
    return {"rope_cos": tile(np.cos(ang)), "rope_sin": tile(np.sin(ang)), "rope_turn": turn}


def kernel(**inputs):
    import numpy as np
    import concourse.bacc as bacc
    from concourse.bass_utils import run_bass_kernel_spmd

    nc = bacc.Bacc("TRN2", target_bir_lowering=False, num_devices=1)
    arrays, io = {}, {}
    given = {n: np.ascontiguousarray(inputs[n]) for n in NAMES}
    given.update(rope_tables())
    for name, a in given.items():
        arrays[f"in_{name}"] = a
        io[name] = nc.dram_tensor(f"in_{name}", a.shape, mybir.dt.from_np(a.dtype), kind="ExternalInput").ap()
    io["out"] = nc.dram_tensor("out_y", (1, SEQ, D), F32, kind="ExternalOutput").ap()
    build(nc, io)
    r = run_bass_kernel_spmd(nc, [arrays], core_ids=[0])
    return r.results[0]["out_y"]
```

```python
from contextlib import ExitStack

from concourse import mybir

F32 = mybir.dt.float32
F32R = mybir.dt.float32r
I32 = mybir.dt.int32
ALU = mybir.AluOpType
ACT = mybir.ActivationFunctionType
AX = mybir.AxisListType

P = 128
BANK = 512
D = 1024
KD = D // P
SEQ, CTX, META = 1024, 256, 16
RW, HEAD = 512, 64
LORA, GATE = 32, 96
DIFF = 512
RWKV_COLS = 3 * RW + 2 * LORA + GATE
FF = 2816
KF = FF // P
NT = SEQ // P
NC = CTX // P
ALL = CTX + SEQ
DECAY = 0.6065306597126334
LAM_INIT = 0.8 - 0.6
L2 = META + SEQ
DN_ALPHA = 4 ** 0.25
TAPS = 31
GK, GV = 128, 256
GH = 4
LEVELS = (1, 2, 4, 8, 16, 32, 64)
SLOT = KD * 512


class Core:

    NAMES = ("pe", "dve", "act", "pool", "sp")

    def __init__(self, nc, ctx):
        self.nc, self.ctx = nc, ctx
        self.queue = {e: [] for e in self.NAMES}
        self.done = {e: ctx.enter_context(nc.semaphore(f"done_{e}")) for e in self.NAMES}
        self.count = {e: 0 for e in self.NAMES}
        self.waited = {e: {} for e in self.NAMES}
        self.held = {e: [] for e in self.NAMES}
        self.dma_count = {}
        self.dma_sems = {}

    def last(self, eng):
        return (self.done[eng], self.count[eng]) if self.count[eng] else None

    def waits(self, eng, after):
        need = []
        for item in after:
            if item is None:
                continue
            if isinstance(item, list):
                need += self.waits(eng, item)
                continue
            sem, value = item
            if self.waited[eng].get(id(sem), 0) < value:
                self.waited[eng][id(sem)] = value
                need.append((sem, value))
        return need

    def put(self, eng, step, *after, signal=True, loose=False):
        own = [] if (loose or eng == "pe") else [self.last(eng)]
        need = self.waits(eng, [*after, *own, *self.held[eng]])
        self.held[eng] = []
        if signal:
            self.count[eng] += 1
        self.queue[eng].append((need, step, (self.done[eng], 1) if signal else None))
        return (self.done[eng], self.count[eng]) if signal else None

    def dma(self, eng, name, out, in_, *after):
        if name not in self.dma_sems:
            self.dma_sems[name] = self.ctx.enter_context(self.nc.semaphore(f"dma_{name}"))
            self.dma_count[name] = 0
        self.dma_count[name] += 16
        sem = self.dma_sems[name]
        need = self.waits(eng, [*after, *(self.held[eng] if eng != "sp" else [])])
        self.queue[eng].append((need, lambda e: e.dma_start(out, in_), (sem, 16)))
        return (sem, self.dma_count[name])

    def everything(self):
        return [self.last(e) for e in ("pe", "dve", "act", "pool")]

    def new_phase(self):
        for e in ("pe", "dve", "act", "pool"):
            self.held[e] = self.held[e] + self.everything()

    def emit(self):
        tail = [(self.dma_sems[n], v) for n, v in self.dma_count.items()]
        block = self.ctx.enter_context(self.nc.Block())

        def run(name, eng):
            for need, step, inc in self.queue[name]:
                for sem, value in need:
                    eng.wait_ge(sem, value)
                made = step(eng)
                if inc:
                    made.then_inc(*inc)

        block.tensor(lambda eng: run("pe", eng))
        block.vector(lambda eng: run("dve", eng))
        block.scalar(lambda eng: run("act", eng))
        block.gpsimd(lambda eng: run("pool", eng))

        @block.sync
        def _(eng):
            run("sp", eng)
            for sem, value in tail:
                eng.wait_ge(sem, value)


class Ring:

    def __init__(self, slots):
        self.slots, self.readers, self.at = slots, [[] for _ in slots], -1

    def take(self):
        self.at = (self.at + 1) % len(self.slots)
        return self.at, self.slots[self.at], list(self.readers[self.at])

    def read(self, index, *counts):
        self.readers[index] = list(counts)


class Arena:

    def __init__(self, tensor, cols):
        self.t, self.at, self.cols = tensor, 0, cols

    def take(self, n, **shape):
        n0, self.at = self.at, self.at + n
        assert self.at <= self.cols, (self.at, self.cols)
        return self.view(n0, n, **shape)

    def view(self, at, n, **shape):
        v = self.t[:, at:at + n]
        if shape:
            names = list(shape)
            v = v.rearrange("p (" + " ".join(names) + " rest) -> p " + " ".join(names) + " rest", **shape)
        return v


class Kernel:
    def __init__(self, nc, io, ctx):
        self.nc, self.io = nc, io
        self.c = Core(nc, ctx)
        self.ctx = ctx
        cols = 53200
        self.sb = Arena(ctx.enter_context(nc.sbuf_tensor("sbuf_all", [P, cols], F32)), cols)
        self.ps = ctx.enter_context(nc.psum_tensor("psum_all", [P, 8 * BANK], F32))
        self.banks(8)

    def banks(self, n, first=0):
        self.bank = Ring([self.ps[:, (first + i) * BANK:(first + i + 1) * BANK] for i in range(n)])
        for i in range(n):
            self.bank.readers[i] = self.c.everything()

    def mm(self, out, lhsT, rhs, start, stop, *after, signal=False):
        return self.c.put("pe", lambda e: e.matmul(out, lhsT, rhs, start=start, stop=stop, skip_group_check=True),
                          *after, signal=signal)

    def turn(self, out, in_, ident, *after, signal=False):
        return self.c.put("pe", lambda e: e.transpose(out, in_, ident), *after, signal=signal)

    def act(self, out, in_, func, *after, scale=1.0, bias=0.0, accum=None, loose=False):
        kw = {} if accum is None else {"accum_out": accum}
        return self.c.put("act", lambda e: e.activation(out, in_, func, bias=bias, scale=scale, **kw), *after,
                          loose=loose)

    def copy(self, eng, out, in_, *after, loose=False):
        if eng == "act":
            return self.act(out, in_, ACT.Copy, *after, loose=loose)
        return self.c.put(eng, lambda e: e.tensor_copy(out, in_), *after, loose=loose)

    def tt(self, out, a, b, op, *after, eng="dve", loose=False):
        return self.c.put(eng, lambda e: e.tensor_tensor(out, a, b, op), *after, loose=loose)

    def ts(self, out, a, s1, s2, op0, op1, *after, eng="dve", loose=False):
        if s2 is None:
            return self.c.put(eng, lambda e: e.tensor_scalar(out, a, s1, None, op0), *after, loose=loose)
        return self.c.put(eng, lambda e: e.tensor_scalar(out, a, s1, s2, op0, op1), *after, loose=loose)

    def stt(self, out, a, s, b, op0, op1, *after, loose=False):
        return self.c.put("dve", lambda e: e.scalar_tensor_tensor(out, a, s, b, op0, op1), *after, loose=loose)

    def recip(self, out, a, *after):
        return self.c.put("dve", lambda e: e.reciprocal(out, a), *after)

    def fill(self, ap, value, *after, eng="pool"):
        return self.c.put(eng, lambda e: e.memset(ap, value), *after)

    def constants(self):
        c, sb = self.c, self.sb
        self.ident = sb.take(P)
        self.ones = sb.take(P)
        self.zero = sb.view(42000, P)
        stage = Ring([sb.view(40000 + i * P, P) for i in range(7)])
        cleared = [self.fill(sb.view(40000, 7 * P), 0.0, eng="dve")]
        self.fill(self.zero, 0.0)
        self.fill(self.ones, 1.0)

        def select(out, in_, pattern, base, mult, op, fill=0.0):
            return c.put("pool", lambda e: e.affine_select(out=out, in_=in_, pattern=pattern, compare_op=op,
                                                           fill=fill, base=base, channel_multiplier=mult))

        select(self.ident, self.zero, [[-1, P]], 0, 1, ALU.not_equal, 1.0)
        self.ident_ready = c.last("pool")
        self.before_at = sb.at
        self.before, self.upto = sb.take(P), sb.take(P)
        self.later_at = sb.at
        self.later, self.from_ = sb.take(P), sb.take(P)
        select(self.before, self.ones, [[1, P]], 0, -1, ALU.is_gt)
        select(self.upto, self.ones, [[1, P]], 0, -1, ALU.is_ge)
        select(self.later, self.ones, [[-1, P]], 0, 1, ALU.is_gt)
        select(self.from_, self.ones, [[-1, P]], 0, 1, ALU.is_ge)
        self.level = {"upper": sb.take(P * 7, m=7), "lower": sb.take(P * 7, m=7)}
        same = {1: self.ident}
        spare = sb.view(42200, P * 7, m=7)
        for i, m in enumerate(LEVELS):
            n = 2 * m
            s = spare[:, i, :]
            if n == P:
                self.copy("pool", s, self.ones)
            else:
                v = s.rearrange("p (b j) -> p b j", j=n)
                one = self.ones.rearrange("p (b j) -> p b j", j=n)
                select(v, one, [[-n, P // n], [0, n]], 0, 1, ALU.is_ge)
                select(v, v, [[n, P // n], [0, n]], n - 1, -1, ALU.is_ge)
            same[n] = s
        for i, m in enumerate(LEVELS):
            for side, order in (("upper", self.before), ("lower", self.later)):
                out = self.level[side][:, i, :]
                self.tt(out, same[2 * m], same[m], ALU.subtract, eng="pool")
                self.tt(out, out, order, ALU.mult, eng="pool")
        self.heads = sb.take(P)
        self.copy("pool", self.heads, same[64])

        cols, rows = {}, []

        def vec(name, ap, n, width=P):
            rows.append((name, ap, n, width))

        io = self.io
        lines = lambda ap: ap.rearrange("(r f) -> r f", f=P)
        for name in ("g_pre_mix", "g_pre_ffn", "g_post_mix", "g_post_ffn"):
            vec(name, lines(io[name][0]), KD)
        vec("c", lines(io["c"][0]), KD)
        vec("c_ctx", lines(io["c_ctx"]), KD)
        vec("b_mod", lines(io["b_mod"][0]), 48)
        rows.append(None)
        for name in ("w0_fwd", "w0_bwd", "a0_fwd", "a0_bwd", "k_k", "k_a"):
            vec(name, lines(io[name][0]), 4)
        vec("r_k", io["r_k"][0].rearrange("h f -> (h f)").rearrange("(r f) -> r f", f=P), 4)
        for t in range(3):
            vec(f"rconv{t}", lines(io["rwkv_conv"][0, t, 0:3 * RW]), 12)
            vec(f"lconv{t}", io["rwkv_conv"][0, t:t + 1, 3 * RW:3 * RW + 2 * LORA], 1, 2 * LORA)
            vec(f"gconv{t}", io["rwkv_conv"][0, t:t + 1, 3 * RW + 2 * LORA:RWKV_COLS], 1, GATE)
        vec("subln_w", io["subln_w"], 1)
        for name in ("lam_q1", "lam_q2", "lam_k1", "lam_k2"):
            vec(name, io[name], 1, HEAD)
        rows.append(None)
        for t in range(2):
            vec(f"fconv{t}", lines(io["ffn_conv"][0, t]), 44)
        rows.append(None)
        vec("fconv2", lines(io["ffn_conv"][0, 2]), 44)
        vec("ffn_conv_b", lines(io["ffn_conv_b"][0]), 44)
        rows.append(None)
        dw = io["conv_w_dw_2"][0].rearrange("t (r f) -> (t r) f", f=P)
        vec("dw_a", dw[0:124], 124)
        rows.append(None)
        vec("dw_b", dw[124:248], 124)
        rows.append(None)
        vec("conv_b_in", lines(io["conv_b_in_2"][0]), 24)
        vec("conv_b_dw", lines(io["conv_b_dw_2"][0]), 8)
        vec("conv_norm_g", lines(io["conv_norm_g_2"][0]), 8)
        vec("conv_norm_b", lines(io["conv_norm_b_2"][0]), 8)
        vec("gla_b_a", lines(io["gla_b_a_2"][0]), 4)
        vec("gla_norm_g", lines(io["gla_norm_g_2"][0]), 2)
        rows.append(None)

        total = sum(r[2] for r in rows if r)
        self.par = sb.take(total)
        at = group = 0
        batch, self.late_params = [], []
        self.col, self.par_at = {}, {}
        for r in rows:
            if r is not None:
                batch.append(r)
                continue
            i, buf, _ = stage.take()
            n, loads = 0, []
            for name, ap, k, width in batch:
                loads = [c.dma("act", f"params{group}", buf[n:n + k, 0:width], ap, cleared)]
                self.col[name] = self.par[:, at + n:at + n + k]
                self.par_at[name] = (self.par, at + n)
                n += k
            step = (at, n, buf, loads[-1])
            if group:
                self.late_params.append(step)
            else:
                self.turn_params(*step)
                self.mod_blocks = [self.w_block(io["w_mod"][0], b * 512, 512) for b in range(self.w_slots)]
                self.load_rows()
            at += n
            group += 1
            batch = []

    def turn_params(self, at, n, buf, loaded):
        bi, bank, free = self.bank.take()
        t = self.turn(bank[:, 0:n], buf[0:n, :], self.ident[0:n, 0:n], loaded, self.ident_ready, free, signal=True)
        self.par_ready = self.copy("dve", self.par[:, at:at + n], bank[:, 0:n], t)
        self.bank.read(bi, self.par_ready)

    def open_weights(self, slots=3):
        self.w_at = self.sb.at
        self.w_slots = slots
        self.sb.take(slots * SLOT)
        self.weights = Ring([self.sb.view(self.w_at + i * SLOT, SLOT) for i in range(slots)])
        self.w_queue = []

    def load_block(self, parts):
        i, slot, free = self.weights.take()
        got = None
        for view, src in parts(slot):
            got = self.c.dma("sp", f"w{i}", view, src, free)
        return i, slot, got

    def w_block(self, w, c0, n, k0=0, k=KD):
        def parts(slot):
            view = slot[:, 0:k * n].rearrange("p (k n) -> p k n", n=n)
            yield view, w[k0 * P:(k0 + k) * P, c0:c0 + n].rearrange("(k p) n -> p k n", p=P)
        i, slot, got = self.load_block(parts)
        return i, slot[:, 0:k * n].rearrange("p (k n) -> p k n", n=n), got

    def modulation(self):
        c = self.c
        sc = self.sb.take(16).rearrange("p (k two) -> p k two", two=2)
        self.mod = self.sb.take(48)
        self.modc = self.sb.take(16)
        a = self.act(sc[:, :, 0], self.col["c"], ACT.Silu, self.par_ready)
        a = self.act(sc[:, :, 1], self.col["c_ctx"], ACT.Silu)
        self.silu_c, self.silu_ready = sc, a
        self.scale_rows()
        for tile in range(2 * KD):
            self.mod_column(tile)
        self.gs1, self.gs1c = self.sb.take(KD), self.sb.take(KD)
        self.stt(self.gs1, self.mod[:, 8:16], 1.0, self.col["g_pre_mix"], ALU.add, ALU.mult)
        self.mod_ready = self.stt(self.gs1c, self.modc[:, 8:16], 1.0, self.col["g_pre_mix"], ALU.add, ALU.mult)

    def mod_column(self, tile):
        if tile % 4 == 0:
            self.mod_w = self.mod_blocks.pop(0)
        wi, w, got = self.mod_w
        j = tile % 4
        bi, bank, free = self.bank.take()
        for k in range(KD):
            t = self.mm(bank[:, 0:2], w[:, k, j * P:(j + 1) * P], self.silu_c[:, k, :], k == 0, k == KD - 1, got, free,
                        self.silu_ready, signal=(k == KD - 1))
        if j == 3:
            self.weights.read(wi, t)
            if tile == 3:
                self.mod_blocks.append(self.w_block(self.io["w_mod"][0], self.w_slots * 512, 512))
        bm = self.col["b_mod"][:, tile:tile + 1]
        done = self.tt(self.mod[:, tile:tile + 1], bank[:, 0:1], bm, ALU.add, t, loose=True)
        if tile < 2 * KD:
            done = self.tt(self.modc[:, tile:tile + 1], bank[:, 1:2], bm, ALU.add, t, loose=True)
        self.bank.read(bi, done)
        return done

    def rstd(self, out, ssq, n, eps, *after):
        t = self.ts(out, ssq, 1.0 / n, eps, ALU.mult, ALU.add, *after)
        t = self.act(out, out, ACT.Sqrt, t)
        return self.recip(out, out, t)

    def turn_rows(self, rows, tiles, emit, after, kt=KD):
        for j in range(kt):
            bi, bank, free = self.bank.take()
            for n, i in enumerate(tiles):
                t = self.turn(bank[:, n * P:(n + 1) * P], rows(i)[:, j * P:(j + 1) * P], self.ident,
                              after, free, signal=(n == len(tiles) - 1))
            self.bank.read(bi, emit(j, bank[:, 0:len(tiles) * P], t))
        return t

    def load_rows(self):
        c, sb, io = self.c, self.sb, self.io
        self.raw_at = 26200
        self.raw = sb.view(self.raw_at, 3 * 4 * D).rearrange("p (g i d) -> p g i d", g=3, i=4)
        x = io["x"][0].rearrange("(i p) d -> p i d", p=P)
        cx = io["ctx"][0].rearrange("(i p) d -> p i d", p=P)
        self.groups = [(cx, 0, 2, 0), (x, 0, 4, CTX), (x, 4, 4, CTX + 512)]
        self.raw_got = [c.dma("act", f"rows{g}", self.raw[:, g, 0:n, :], src[:, i0:i0 + n, :])
                        for g, (src, i0, n, _) in enumerate(self.groups)]

    def scale_rows(self):
        sb, raw = self.sb, self.raw
        stat, junk = sb.view(38500, 10), sb.view(38520, D)
        self.rows_scaled = []
        tiles = [(g, i) for g, (_, _, n, _) in enumerate(self.groups) for i in range(n)]
        for s, (g, i) in enumerate(tiles):
            sq = self.act(junk, raw[:, g, i, :], ACT.Square, self.raw_got[g], accum=stat[:, s:s + 1])
            if (g, i) != tiles[-1] and tiles[s + 1][0] == g:
                continue
            s0 = s - i
            r = self.rstd(stat[:, s0:s + 1], stat[:, s0:s + 1], D, 1e-6, sq)
            for n in range(i + 1):
                t = self.ts(raw[:, g, n, :], raw[:, g, n, :], stat[:, s0 + n:s0 + n + 1], None, ALU.mult, ALU.bypass, r, loose=True)
            self.rows_scaled.append(t)

    def first_norm(self):
        c, sb = self.c, self.sb
        self.hT_at = sb.at
        self.hT = sb.take(KD * ALL, k=KD)
        assert sb.at <= self.raw_at
        for g, (_, _, n, col) in enumerate(self.groups):
            scale, shift = (self.gs1c, self.modc) if g == 0 else (self.gs1, self.mod)

            def emit(j, bank, t, col=col, n=n, scale=scale, shift=shift):
                out = self.hT[:, j, col:col + n * P]
                if j % 2:
                    return self.act(out, bank, ACT.Identity, t, self.mod_ready, scale=scale[:, j:j + 1],
                                    bias=shift[:, j:j + 1], loose=True)
                return self.ts(out, bank, scale[:, j:j + 1], shift[:, j:j + 1], ALU.mult, ALU.add, t,
                               self.mod_ready, loose=True)

            self.turn_rows(lambda i, g=g: self.raw[:, g, i, :], range(n), emit, self.rows_scaled[g])
        for step in self.late_params:
            self.turn_params(*step)
        self.hT_ready = [c.last("act"), c.last("dve")]

    def dense(self, w, c0, n, rhs, spans, emit, after, kt=KD):
        wi, wt, got = self.w_block(w, c0, n, k=kt)
        for j in range((n + P - 1) // P):
            m = min(P, n - j * P)
            self.product(lambda k: wt[:, k, j * P:j * P + m], rhs, spans, kt, m, [got, after],
                         lambda s, bank, t: emit(j, s, bank, t))
        self.weights.read(wi, self.c.last("pe"))

    def product(self, lhs, rhs, spans, kt, m, after, emit):
        for s, (a, b) in enumerate(spans):
            bi, bank, free = self.bank.take()
            for k in range(kt):
                t = self.mm(bank[0:m, 0:b - a], lhs(k), rhs(k, a, b), k == 0, k == kt - 1, after, free,
                            signal=(k == kt - 1))
            self.bank.read(bi, emit(s, bank[0:m, 0:b - a], t))

    def attention(self):
        c, sb, io = self.c, self.sb, self.io
        self.yd_at = sb.at
        self.ydT = sb.take(4 * SEQ, h=4)
        q, k = sb.take(4 * SEQ, h=4), sb.take(4 * ALL, h=4)
        v = sb.take(10 * DIFF, i=10)
        rope_at = sb.at
        cos, sin, turn = sb.take(SEQ), sb.take(SEQ), sb.take(P)
        tmp = [sb.take(BANK), sb.take(BANK)]
        c.new_phase()
        tables = [c.dma("act", "rope", t, io[n]) for n, t in (("rope_cos", cos), ("rope_sin", sin), ("rope_turn", turn))]
        hT = lambda k_, a, b: self.hT[:, k_, a:b]
        ready = self.hT_ready
        turn_ring = Ring(tmp)

        def moved(dst):
            return lambda j, s, bank, t: self.copy("act" if s % 2 else "dve", dst(j, s), bank, t, loose=True)

        def rope(x, first, h):
            for a in (0, 512):
                xs = x[:, h, first + a:first + a + 512]
                bi, bank, free = self.bank.take()
                t = self.mm(bank, turn, xs, True, True, qk_ready, free, tables[-1], signal=True)
                ti, rot, _ = turn_ring.take()
                t1 = self.tt(rot, bank, sin[:, a:a + 512], ALU.mult, t)
                self.bank.read(bi, t1)
                self.tt(xs, xs, cos[:, a:a + 512], ALU.mult, t)
                self.tt(xs, xs, rot, ALU.add)

        self.dense(io["w_in"][0], RWKV_COLS, DIFF, lambda k_, a, b: self.hT[:, k_, CTX + a:CTX + b], [(0, 512), (512, 1024)],
                   lambda j, s, bank, t: self.act(q[:, j, s * 512:(s + 1) * 512], bank, ACT.Copy, t, scale=HEAD ** -0.5, loose=True), ready)
        spans = [(0, 512), (512, 1024), (1024, 1280)]
        self.dense(io["w_in"][0], RWKV_COLS + DIFF, DIFF, hT, spans,
                   moved(lambda j, s: k[:, j, spans[s][0]:spans[s][1]]), ready)
        qk_ready = [c.last("act"), c.last("dve")]
        wi, wv, got = self.w_block(io["w_in"][0], RWKV_COLS + 2 * DIFF, DIFF)
        for i in range(10):
            bi, bank, free = self.bank.take()
            for kk in range(KD):
                t = self.mm(bank, self.hT[:, kk, i * P:(i + 1) * P], wv[:, kk, :], kk == 0, kk == KD - 1,
                            got, free, ready, signal=(kk == KD - 1))
            self.bank.read(bi, self.copy("act", v[:, i, :], bank, t, loose=True))
            if i < 8:
                rope(*((q, 0) if i < 4 else (k, CTX)), i % 4)
        self.weights.read(wi, c.last("pe"))

        c.new_phase()
        sb.at = rope_at
        lam = sb.take(8)
        prod = lam[:, 0:2]
        qcols = self.par_slice("lam_q1", 2)
        kcols = self.par_slice("lam_k1", 2)
        t = self.tt(prod, qcols, kcols, ALU.mult)
        bi, bank, free = self.bank.take()
        t = self.mm(bank[:, 0:2], self.ones, prod, True, True, t, free, signal=True)
        t = self.act(lam[:, 2:4], bank[:, 0:2], ACT.Exp, t)
        self.bank.read(bi, t)
        neg_lam = lam[:, 4:5]
        self.tt(neg_lam, lam[:, 3:4], lam[:, 2:3], ALU.subtract, t)
        lam_ready = self.ts(neg_lam, neg_lam, -LAM_INIT, None, ALU.add, ALU.bypass)

        pbuf = [[sb.take(ALL) for m in range(2)] for _ in range(2)]
        pT = [sb.take(ALL) for _ in range(2)]
        stats = sb.take(16)
        ssq = sb.take(32)
        o_rows = self.ydT.rearrange("p h (i e) -> p h i e", e=P)
        self.banks(2, first=6)
        scores = [self.ps[:, 0:ALL], self.ps[:, 3 * BANK:3 * BANK + ALL]]
        start = c.everything()
        exp_done = [start, start]
        a_done, pv_done, o_read = [None] * 2, [None] * 2, [None] * 2
        sums_read = [None] * 2
        work = [(h, i) for h in range(4) for i in range(NT)]
        turned = {}

        def score(n, m):
            h, i = work[n]
            par = n % 2
            s_ = stats[:, 8 * par:8 * par + 8]
            for a, b in spans:
                t = self.mm(scores[m][:, a:b], q[m * HEAD:(m + 1) * HEAD, h, i * P:(i + 1) * P],
                            k[m * HEAD:(m + 1) * HEAD, h, a:b], True, True, start, exp_done[m], signal=(b == ALL))
            t = c.put("dve", lambda e, o=s_[:, m:m + 1], x=scores[m]: e.tensor_reduce(o, x, AX.X, ALU.max, negate=True), t,
                      exp_done[m])
            exp_done[m] = self.act(pbuf[par][m], scores[m], ACT.Exp, t, a_done[par], pv_done[par], sums_read[par], bias=s_[:, m:m + 1],
                                   accum=s_[:, 2 + m:3 + m], loose=True)

        def combine(n):
            par = n % 2
            s_ = stats[:, 8 * par:8 * par + 8]
            self.recip(s_[:, 4:6], s_[:, 2:4], exp_done[0], exp_done[1], o_read[par])
            self.stt(s_[:, 6:7], s_[:, 5:6], neg_lam, s_[:, 2:3], ALU.mult, ALU.mult, lam_ready)
            a_done[par] = self.stt(pbuf[par][0], pbuf[par][1], s_[:, 6:7], pbuf[par][0], ALU.mult, ALU.add)
            sums_read[par] = a_done[par]

        def turns(n, g):
            par = n % 2
            w = min(4, 10 - g)
            bi, bank, free = self.bank.take()
            for kk in range(w):
                t = self.turn(bank[:, kk * P:(kk + 1) * P], pbuf[par][0][:, (g + kk) * P:(g + kk + 1) * P], self.ident,
                              a_done[par], free, signal=(kk == w - 1))
            if g == 8:
                a_done[par] = t
            t = self.copy("act" if g == 0 else "dve", pT[par][:, g * P:(g + w) * P], bank[:, 0:w * P], t, pv_done[par], loose=True)
            self.bank.read(bi, t)
            turned[g] = t

        def weigh(n):
            h, i = work[n]
            par = n % 2
            s_ = stats[:, 8 * par:8 * par + 8]
            bi, bank, free = self.bank.take()
            for kk in range(10):
                t = self.mm(bank[:, 0:P], pT[par][:, kk * P:(kk + 1) * P], v[:, kk, h * P:(h + 1) * P], kk == 0, kk == 9,
                            turned[kk // 4 * 4], free, signal=(kk == 9))
            pv_done[par] = t
            t = self.act(o_rows[:, h, i, :], bank[:, 0:P], ACT.Copy, t, scale=s_[:, 4:5], loose=True)
            self.bank.read(bi, t)
            o_read[par] = t
            self.act(junk, o_rows[:, h, i, :], ACT.Square, t, accum=ssq[:, h * NT + i:h * NT + i + 1])

        junk = sb.take(P)
        mod_acc = sb.take(512)
        mod_w, mod_read = {}, [None]

        def mod_rest(n):
            block, part = 4 + n // 4, n % 4
            acc = mod_acc
            if part == 0:
                mod_w[0] = self.w_block(io["w_mod"][0], block * 512, 512)
            wi, w, got = mod_w[0]
            for k in (2 * part, 2 * part + 1):
                ck = self.silu_c[:, k, 0:1]
                if k == 0:
                    t = self.ts(acc, w[:, k, :], ck, None, ALU.mult, ALU.bypass, got, mod_read[0])
                else:
                    t = self.stt(acc, w[:, k, :], ck, acc, ALU.mult, ALU.add)
            if part < 3:
                return
            self.weights.read(wi, t)
            mod_done.append((block, t))

        def mod_sum(block, t):
            bi, bank, free = self.bank.take()
            for j in range(4):
                tt = self.mm(bank[:, j:j + 1], mod_acc[:, j * P:(j + 1) * P], self.ones[:, 0:1], True, True, t, free,
                             signal=(j == 3))
            mod_read[0] = tt
            cols = slice(4 * block, 4 * block + 4)
            self.bank.read(bi, self.tt(self.mod[:, cols], bank[:, 0:4], self.col["b_mod"][:, cols], ALU.add, tt, loose=True))

        mod_done = []
        for n in range(len(work) + 1):
            if n < len(work):
                score(n, 0)
            if mod_done:
                mod_sum(*mod_done.pop())
            if n:
                turns(n - 1, 0)
                turns(n - 1, 4)
            if n < len(work):
                score(n, 1)
            if n:
                turns(n - 1, 8)
                weigh(n - 1)
            if n < len(work):
                combine(n)
                mod_rest(n)
        r = self.rstd(ssq, ssq, P, 1e-5, c.last("act"))
        self.banks(8)
        yT = q
        for h in range(4):
            for i in range(NT):
                o = o_rows[:, h, i, :]
                t = self.ts(o, o, ssq[:, h * NT + i:h * NT + i + 1], None, ALU.mult, ALU.bypass, r, loose=True)
            for g in range(2):
                bi, bank, free = self.bank.take()
                for i in range(4):
                    tt = self.turn(bank[:, i * P:(i + 1) * P], o_rows[:, h, 4 * g + i, :], self.ident, t, free, signal=(i == 3))
                t2 = self.ts(yT[:, h, g * 512:(g + 1) * 512], bank, self.col["subln_w"], 1.0 - LAM_INIT, ALU.mult,
                             ALU.mult, tt, loose=True)
                self.bank.read(bi, t2)
        self.yd_dram = self.nc.dram_tensor("yd_spill", (P, 4, SEQ), F32).ap()
        self.yd_spilled = c.dma("act", "spill_yd", self.yd_dram, yT, c.last("dve"))
        sb.at = self.yd_at
        self.c.new_phase()
        self.banks(8)

    def par_slice(self, name, n):
        return self.par_at[name][0][:, self.par_at[name][1]:self.par_at[name][1] + n]

    def rwkv_project(self):
        c, sb, io = self.c, self.sb, self.io
        c.new_phase()
        for e in ("pe", "dve", "act", "pool"):
            c.held[e].append(self.yd_spilled)
        self.vtok = sb.take(10 * RW, i=10)
        self.wa, self.gl = sb.take(ALL), sb.take(SEQ)
        rk = sb.take(8 * ALL, j=4, w=2)
        self.rk_pair = [rk[:, 0], rk[:, 1]]
        self.rwkv_keep = sb.at - 4 * ALL
        vfeats = rk[:, 2:4].rearrange("p j w t -> p (j w) t")
        raws = Ring([sb.take(ALL + 3) for _ in range(2)])
        pads = [self.fill(raw[:, n:n + 1], 0.0) for raw in raws.slots for n in (0, CTX + 1, ALL + 2)]
        spans = [(0, CTX), (CTX, CTX + 512), (CTX + 512, ALL)]
        where = [1, CTX + 2, CTX + 2 + 512]
        hT = lambda k_, a, b: self.hT[:, k_, a:b]
        rank = {}

        def evac(raw, free, m):
            def emit(s, bank, t):
                a, b = spans[s]
                return self.copy("act", raw[0:m, where[s]:where[s] + b - a], bank, t, free, loose=True)
            return emit

        def conv(dst, raw, taps, m, after, with_ctx=True):
            for at, n, to in ([(1, CTX, 0)] if with_ctx else []) + [(CTX + 2, SEQ, CTX if with_ctx else 0)]:
                out = dst[0:m, to:to + n]
                self.ts(out, raw[0:m, at:at + n], taps[1], None, ALU.mult, ALU.bypass, after, pads[-1])
                self.stt(out, raw[0:m, at - 1:at - 1 + n], taps[0], out, ALU.mult, ALU.add)
                t = self.stt(out, raw[0:m, at + 1:at + 1 + n], taps[2], out, ALU.mult, ALU.add)
            return t

        late = []

        def turn_values(j, vfeat, t):
            for g in range(0, 10, 4):
                n = min(4, 10 - g)
                bi, bank, free = self.bank.take()
                for i in range(n):
                    tt = self.turn(bank[:, i * P:(i + 1) * P], vfeat[:, (g + i) * P:(g + i + 1) * P], self.ident, t, free, signal=(i == n - 1))
                out = self.vtok[:, g:g + n, j * P:(j + 1) * P]
                self.bank.read(bi, self.copy("act", out, bank[:, 0:n * P].rearrange("p (i f) -> p i f", f=P), tt, loose=True))

        for part, dst in enumerate((rk[:, :, 0], rk[:, :, 1], None)):
            wi, w, got = self.w_block(io["w_in"][0], part * RW, RW)
            for j in range(4):
                ri, raw, free = raws.take()
                self.product(lambda kk: w[:, kk, j * P:(j + 1) * P], hT, spans, KD, P, [got, self.hT_ready],
                             evac(raw, free, P))
                taps = [self.col[f"rconv{t}"][:, part * 4 + j:part * 4 + j + 1] for t in range(3)]
                if dst is None:
                    vfeat = vfeats[:, j, :]
                t = conv(vfeat if dst is None else dst[:, j, :], raw, taps, P,
                         [c.last("act"), self.rk_spilled if dst is None else None])
                raws.read(ri, t)
                if dst is None:
                    late.append((j, vfeat, t))
                    if len(late) > 1:
                        turn_values(*late.pop(0))
            self.weights.read(wi, c.last("pe"))
            if part == 1:
                self.rk_dram = self.nc.dram_tensor("rk_spill", (P, 2, 2, ALL), F32).ap()
                self.rk_spilled = c.dma("act", "spill_rk", self.rk_dram, rk[:, 2:4], t)
        wi, w, got = self.w_block(io["w_in"][0], 3 * RW, 2 * LORA + GATE)
        for c0, m, name, dst in ((0, 2 * LORA, "lconv", self.wa), (2 * LORA, GATE, "gconv", self.gl)):
            ri, raw, free = raws.take()
            self.product(lambda kk: w[:, kk, c0:c0 + m], hT, spans, KD, m, [got, self.hT_ready], evac(raw, free, m))
            taps = [self.col[f"{name}{t}"][0:m, 0:1] for t in range(3)]
            t = conv(dst, raw, taps, m, [c.last("act")], with_ctx=(dst is self.wa))
            raws.read(ri, t)
            if late:
                turn_values(*late.pop(0))
        self.weights.read(wi, c.last("pe"))
        self.act(self.wa[0:LORA, :], self.wa[0:LORA, :], ACT.Tanh, t)
        self.wa_ready = self.act(self.gl[0:GATE, :], self.gl[0:GATE, :], ACT.Sigmoid)

    STREAMS = [(j, d) for j in range(4) for d in range(2)]
    SLOTS = 3

    def rwkv(self):
        c, sb, io = self.c, self.sb, self.io
        c.new_phase()
        for e in ("pe", "dve", "act", "pool"):
            c.held[e].append(self.rk_spilled)
        sb.at = self.w_at
        self.yacc = yacc = sb.take(NT * RW, i=NT)
        self.kk = sb.take(ALL)
        self.lora = sb.take(2 * RW, d=2)
        g2 = sb.take(RW)
        S = [sb.take(P) for _ in range(2)]
        self.bonus = bonus = sb.take(NT * 8, i=NT)
        self.omka, self.rk, self.hsel = sb.take(4), sb.take(4), sb.take(2)
        self.gains = [sb.take(32) for _ in range(2)]

        def group_memory(n):
            take = sb.take
            g = {"agbh": take(2048, u=4), "D": take(512, u=4), "E": take(512, u=4), "Y": take(512, u=4)}
            g["X"] = take(512)
            flat = lambda v: v.rearrange("p u t -> p (u t)")
            g["WU"] = flat(g["D"])
            g["M"], g["N"] = g["X"][:, 0:256], g["X"][:, 256:512]
            g["WT"], g["U"] = flat(g["Y"])[:, 0:256], flat(g["Y"])[:, 256:512]
            g["free"] = c.everything()
            return g

        G = [group_memory(0)]
        assert sb.at <= self.w_at + self.w_slots * SLOT
        sb.at = self.hT_at
        self.work = [sb.take(ALL) for _ in range(4)]
        factors = [(sb.take(2 * ALL).rearrange("p (n two t) -> p n two t", two=2, t=P),
                    sb.take(ALL, ch=10), sb.take(ALL, ch=10))]
        assert sb.at <= self.hT_at + KD * ALL
        sb.at = self.rwkv_keep
        factors.append((sb.take(2 * ALL).rearrange("p (n two t) -> p n two t", two=2, t=P),
                        sb.take(ALL, ch=10), sb.take(ALL, ch=10)))
        while len(G) < self.SLOTS:
            G.append(group_memory(len(G)))

        for d, n in enumerate(("fwd", "bwd")):
            c.dma("act", "lora", self.lora[0:LORA, d, :], io[f"w2_{n}"][0], c.everything())
            c.dma("act", "lora", self.lora[LORA:2 * LORA, d, :], io[f"a2_{n}"][0])
        self.lora_ready = c.dma("act", "lora", g2[0:GATE, :], io["g2"][0])
        self.copy("pool", self.hsel, self.heads.rearrange("p (two h) -> p two h", two=2)[:, :, 0])
        self.ts(self.omka, self.col["k_a"], -1.0, 1.0, ALU.mult, ALU.add, c.last("pool"))
        self.ts(self.rk, self.col["r_k"], 0.5, None, ALU.mult, ALU.bypass)

        streams = [{"ready": None, "gone": None, "buf": factors[n % 2], "gain": self.gains[n % 2]}
                   for n in range(len(self.STREAMS))]
        groups = [{"stream": s, "n": n, "ready": None} for s in range(len(streams)) for n in range(5)]
        loads = {}
        gone = [0]

        def prepare():
            for s, (j, d) in enumerate(self.STREAMS):
                if d == 0:
                    self.rk_ready = loads.get(j)
                    yield from self.unit_keys(j)
                while s >= 2 and streams[s - 2]["gone"] is None:
                    yield
                yield from self.factors(j, d, streams[s], streams[s - 2]["gone"] if s >= 2 else None)
                if d == 1 and j < 2:
                    loads[j + 2] = c.dma("sp", f"load_rk{j}", self.rk_pair[j], self.rk_dram[:, j], c.last("dve"), self.rk_spilled)

        def invert(slot):
            for gi in range(slot, len(groups), self.SLOTS):
                gr = groups[gi]
                st = streams[gr["stream"]]
                while st["ready"] is None or gone[0] < gi - self.SLOTS + 1:
                    yield
                j, d = self.STREAMS[gr["stream"]]
                order = [0, 1, *range(2, 10)] if d == 0 else [1, 0, *range(9, 1, -1)]
                yield from self.invert(G[slot], order[2 * gr["n"]:2 * gr["n"] + 2], st, d == 0, j)
                gr["ready"] = True

        def recur():
            si = 0
            for gi, gr in enumerate(groups):
                while gr["ready"] is None:
                    yield
                st, g = streams[gr["stream"]], G[gi % self.SLOTS]
                j, d = self.STREAMS[gr["stream"]]
                order = [0, 1, *range(2, 10)] if d == 0 else [1, 0, *range(9, 1, -1)]
                for ci in range(2):
                    n = order[2 * gr["n"] + ci]
                    yield from self.chunk_step(g, ci, n, st, S, si, gr["n"] == 0 and ci == 0, j, d == 0, n == order[-1])
                    si ^= 1
                g["free"] = [c.last("pe"), c.last("dve"), c.last("act")]
                gone[0] += 1
                if gr["n"] == 4:
                    st["gone"] = g["free"]

        self.state_at, self.y_read, self.bonus_read, self.t1_read = None, None, None, None
        live = [recur(), *(invert(slot) for slot in range(self.SLOTS)), prepare()]
        while live:
            for gen in list(live):
                try:
                    next(gen)
                except StopIteration:
                    live.remove(gen)
        self.rwkv_output(yacc, bonus, g2, self.lora_ready)

    SPANS = ((0, 512), (512, 1024), (1024, 1280))

    def unit_keys(self, j):
        lw, cc, t1, aa = self.work
        c = self.c
        t = self.ts(self.kk, self.rk_pair[j % 2][:, 1], self.col["k_k"][:, j:j + 1], None, ALU.mult, ALU.bypass, self.rk_ready)
        tq = self.act(t1, self.kk, ACT.Square, t)
        roots = []
        for a, b in self.SPANS:
            bi, bank, free = self.bank.take()
            tt = self.mm(bank[:, 0:b - a], self.heads, t1[:, a:b], True, True, tq, free, signal=True)
            roots.append(self.act(lw[:, a:b], bank[:, 0:b - a], ACT.Sqrt, tt, self.bonus_read))
            self.bank.read(bi, roots[-1])
        yield
        self.ts(lw, lw, 1e-12, None, ALU.max, ALU.bypass, roots[-1])
        yield
        for a in range(0, ALL, 256):
            self.recip(lw[:, a:a + 256], lw[:, a:a + 256])
            yield
        self.tt(self.kk, self.kk, lw, ALU.mult)
        self.t1_read = tt

    def factors(self, j, d, st, free_f):
        c = self.c
        lw, cc, t1, aa = self.work
        kr, beta, key = st["buf"]
        cmid, clast, gain = st["gain"][:, 0:10], st["gain"][:, 10:20], st["gain"][:, 20:30]
        fwd = d == 0
        free_d = c.last("dve")
        for lo, dst, bias in ((0, lw, self.col["w0_fwd" if fwd else "w0_bwd"]), (LORA, aa, self.col["a0_fwd" if fwd else "a0_bwd"])):
            for a, b in self.SPANS:
                bi, bank, free = self.bank.take()
                t = self.mm(bank[:, 0:b - a], self.lora[lo:lo + LORA, d, j * P:(j + 1) * P],
                            self.wa[lo:lo + LORA, a:b], True, True, self.lora_ready, self.wa_ready, free, signal=True)
                t = self.act(dst[:, a:b], bank[:, 0:b - a], ACT.Sigmoid, t, free_d, self.bonus_read, bias=bias[:, j:j + 1])
                self.bank.read(bi, t)
            if lo == 0:
                t_w = t
        yield
        c3 = cc.rearrange("p (n t) -> p n t", t=P)
        lw3, t13, aa3 = (x.rearrange("p (n t) -> p n t", t=P) for x in (lw, t1, aa))
        kk3, r3 = (x.rearrange("p (n t) -> p n t", t=P) for x in (self.kk, self.rk_pair[j % 2][:, 0]))
        flip = (lambda ap: ap) if fwd else (lambda ap: ap[:, ::-1])
        for n in range(10):
            c.put("dve", lambda e, o=flip(c3[:, n, :]), x=flip(lw3[:, n, :]): e.tensor_tensor_scan(
                o, self.ones, x, 0.0, ALU.mult, ALU.add), t_w, free_f, loose=n > 0)
            if n % 4 == 3:
                yield
        mid, end = P // 2, (P - 1 if fwd else 0)
        self.copy("dve", cmid, c3[:, :, mid])
        self.copy("dve", clast, c3[:, :, end])
        t_c = self.tt(c3, c3, cmid.unsqueeze(2).broadcast_to([P, 10, P]), ALU.subtract)
        self.tt(gain, clast, cmid, ALU.subtract)
        for to, frm in (((0, 9), (1, 10)),) if fwd else (((1, 2), (0, 1)), ((0, 1), (9, 10)), ((3, 10), (2, 9))):
            t_g = self.tt(gain[:, to[0]:to[1]], gain[:, to[0]:to[1]], cmid[:, frm[0]:frm[1]], ALU.add)
        t_p = self.tt(lw, cc, lw, ALU.subtract)
        self.act(kr[:, :, 1, :], c3, ACT.Exp, t_c, free_f, scale=-DECAY)
        e_c = self.act(cc, cc, ACT.Exp, t_p, scale=DECAY)
        e_p = self.act(lw, lw, ACT.Exp, t_p, scale=-DECAY)
        e_g = self.act(gain, gain, ACT.Exp, t_g, scale=-DECAY)
        yield
        self.ts(t1, aa, self.col["k_a"][:, j:j + 1], self.omka[:, j:j + 1], ALU.mult, ALU.add, t, self.t1_read, free_d, eng="pool")
        t_k = self.tt(t1, t1, self.rk_pair[j % 2][:, 1], ALU.mult, eng="pool")
        yield
        t_a = self.tt(aa, aa, self.kk, ALU.mult, eng="pool")
        self.tt(kr[:, :, 1, :], kr[:, :, 1, :], r3, ALU.mult, e_c)
        yield
        self.tt(beta, aa3, c3, ALU.mult, free_f, t_a)
        self.tt(key, t13, c3, ALU.mult, t_k)
        yield
        self.tt(kr[:, :, 0, :], lw3, kk3, ALU.mult, e_p)
        st["ready"] = [c.last("dve"), e_g]
        t = self.stt(lw[:, 0:SEQ], t1[:, CTX:], self.rk[:, j:j + 1], self.rk_pair[j % 2][:, 0, CTX:], ALU.mult, ALU.mult)
        yield
        bi, bank, free = self.bank.take()
        for i in range(NT):
            t2 = self.mm(bank[:, 2 * i:2 * i + 2], lw[:, i * P:(i + 1) * P], self.hsel, True, True, t, free, signal=(i == NT - 1))
        self.bonus_read = t2
        b2 = bank[:, 0:2 * NT].rearrange("p (i two) -> p i two", two=2)
        bout = self.bonus[:, :, 2 * j:2 * j + 2]
        if fwd:
            t = self.copy("dve", bout, b2, t2)
        else:
            t = self.tt(bout, bout, b2, ALU.add, t2)
        self.bank.read(bi, t)
        yield

    def invert(self, g, chunks, st, fwd, j):
        c = self.c
        kr, beta, key = st["buf"]
        stream, free_g = st["ready"], g["free"]
        at0 = self.before_at if fwd else self.later_at
        order_mask = self.sb.t[:, at0:at0 + 2 * P]
        side, other = ("lower", "upper") if fwd else ("upper", "lower")
        four = lambda m: m.unsqueeze(1).broadcast_to([P, 4, P])
        as4 = lambda b: b.rearrange("p (u t) -> p u t", u=4)
        ctx_only = chunks[0] < 2
        for u in range(4):
            n, h = chunks[u // 2], u % 2
            rows = slice(h * HEAD, (h + 1) * HEAD)
            bi, bank, free = self.bank.take()
            if ctx_only:
                self.mm(bank[:, 0:P], beta[rows, n, :], kr[rows, n, 0, :], True, True, stream, free)
                t = self.mm(bank[:, P:2 * P], key[rows, n, :], kr[rows, n, 0, :], True, True, signal=True)
                t = self.tt(g["agbh"][:, u, :].rearrange("p (two x) -> p two x", two=2)[:, :, 0:P],
                            bank[:, 0:2 * P].rearrange("p (two x) -> p two x", two=2),
                            order_mask[:, 0:P].unsqueeze(1).broadcast_to([P, 2, P]), ALU.mult, t, free_g, loose=True)
            else:
                self.mm(bank[:, 0:256], beta[rows, n, :], kr[rows, n, :, :], True, True, stream, free)
                t = self.mm(bank[:, 256:512], key[rows, n, :], kr[rows, n, :, :], True, True, signal=True)
                t = self.tt(g["agbh"][:, u, :].rearrange("p (two x) -> p two x", two=2), bank.rearrange("p (two x) -> p two x", two=2),
                            order_mask.unsqueeze(1).broadcast_to([P, 2, 2 * P]), ALU.mult, t, free_g, loose=True)
            self.bank.read(bi, t)
            if u % 2:
                yield
        at = g["agbh"][:, :, 0:P]
        bi, bank, free = self.bank.take()
        for u in range(4):
            ta = self.turn(bank[:, u * P:(u + 1) * P], at[:, u, :], self.ident, t, free, signal=(u == 3))
        self.tt(g["Y"], at, four(self.level[other][:, 0, :]), ALU.mult, t)
        self.tt(g["E"], four(self.ident), g["Y"], ALU.subtract)
        self.tt(g["Y"], as4(bank), four(self.level[side][:, 0, :]), ALU.mult, ta)
        self.bank.read(bi, c.last("dve"))
        gt = self.tt(g["D"], four(self.ident), g["Y"], ALU.subtract)
        yield
        for ci, n in enumerate(chunks):
            bi, bank, free = self.bank.take()
            self.turn(bank[:, 0:P], kr[:, n, 0, :], self.ident, free, stream)
            self.turn(bank[:, P:2 * P], beta[:, n, :], self.ident)
            self.turn(bank[:, 2 * P:3 * P], key[:, n, :], self.ident)
            for h in range(2):
                u = 2 * ci + h
                tt = self.mm(bank[:, 3 * P + h * HEAD:3 * P + (h + 1) * HEAD], g["agbh"][:, u, 256:384],
                             self.vtok[:, n, j * P + h * HEAD:j * P + (h + 1) * HEAD], True, True, t, signal=True)
            self.act(g["X"][:, ci * 256:ci * 256 + P], bank[:, 0:P], ACT.Copy, tt, free_g, loose=True)
            self.act(g["agbh"][:, 2 * ci:2 * ci + 2, 256:384], bank[:, P:3 * P].rearrange("p (w t) -> p w t", w=2), ACT.Copy, loose=True)
            t2 = self.act(g["X"][:, ci * 256 + P:ci * 256 + 256], bank[:, 3 * P:4 * P], ACT.Copy, scale=-1.0, loose=True)
            self.bank.read(bi, t2)
            yield
        t_x = t2
        for li, m in enumerate(LEVELS):
            if m == 1:
                continue
            bi, bank, free = self.bank.take()
            for u in range(4):
                t = self.mm(bank[:, u * P:(u + 1) * P], g["agbh"][:, u, 0:P], g["D"][:, u, :], True, True, gt, free, signal=(u == 3))
            gt = self.tt(g["Y"], as4(bank), four(self.level[side][:, li, :]), ALU.mult, t, loose=True)
            self.bank.read(bi, gt)
            yield
            bi, bank, free = self.bank.take()
            for u in range(4):
                t = self.mm(bank[:, u * P:(u + 1) * P], g["Y"][:, u, :], g["E"][:, u, :], True, True, gt, free, signal=(u == 3))
            gt = self.tt(g["E"], g["E"], as4(bank), ALU.subtract, t, loose=True)
            self.bank.read(bi, gt)
            yield
            if m == 64:
                break
            bi, bank, free = self.bank.take()
            for u in range(4):
                t = self.turn(bank[:, u * P:(u + 1) * P], g["E"][:, u, :], self.ident, gt, free, signal=(u == 3))
            gt = self.act(g["D"], as4(bank), ACT.Copy, t, loose=True)
            self.bank.read(bi, gt)
            yield
        x5 = g["X"].rearrange("p (c w h f) -> p c w h f", c=2, w=2, h=2)
        bi, bank, free = self.bank.take()
        b5 = bank.rearrange("p (c w h f) -> p c w h f", c=2, w=2, h=2)
        for u in range(4):
            ci, h = u // 2, u % 2
            t = self.mm(b5[:, ci, :, h, :], g["E"][:, u, :], x5[:, ci, :, h, :], True, True, gt, t_x, free, signal=(u == 3))
        t = self.copy("act", g["WU"], bank, t, loose=True)
        self.bank.read(bi, t)
        yield
        bi, bank, free = self.bank.take()
        for ci, n in enumerate(chunks):
            wk, u0 = g["WU"][:, ci * 256:ci * 256 + P], g["WU"][:, ci * 256 + P:ci * 256 + 256]
            bt, kt = g["agbh"][:, 2 * ci, 256:384], g["agbh"][:, 2 * ci + 1, 256:384]
            self.mm(bank[:, ci * P:(ci + 1) * P], wk, bt, True, True, t, free)
            self.mm(bank[:, 256 + ci * P:256 + (ci + 1) * P], kt, self.vtok[:, n, j * P:(j + 1) * P], True, False)
            tt = self.mm(bank[:, 256 + ci * P:256 + (ci + 1) * P], bt, u0, False, True, signal=True)
        two = lambda x: x.rearrange("p (c t) -> p c t", c=2)
        hb = self.heads.unsqueeze(1).broadcast_to([P, 2, P])
        ib = self.ident.unsqueeze(1).broadcast_to([P, 2, P])
        self.tt(two(g["M"]), two(bank[:, 0:256]), hb, ALU.mult, tt)
        t2 = self.tt(two(g["N"]), two(bank[:, 256:512]), hb, ALU.mult, loose=True)
        self.bank.read(bi, t2)
        self.tt(two(g["M"]), ib, two(g["M"]), ALU.subtract)
        for ci, n in enumerate(chunks):
            N = g["N"][:, ci * P:(ci + 1) * P]
            gm = self.ts(N, N, st["gain"][:, 20 + n:21 + n], None, ALU.mult, ALU.bypass, stream)
        if not ctx_only:
            bi, bank, free = self.bank.take()
            for ci in range(2):
                tt = self.turn(bank[:, ci * P:(ci + 1) * P], g["WU"][:, ci * 256:ci * 256 + P], self.ident, t, free, signal=(ci == 1))
            gw = self.copy("act", g["WT"], bank[:, 0:256], tt, loose=True)
            self.bank.read(bi, gw)
            gm = [gm, gw]
        g["t"] = gm
        yield

    def chunk_step(self, g, ci, n, st, S, si, first, j, fwd, final):
        c = self.c
        s, s_next = S[si], S[si ^ 1]
        kr = st["buf"][0]
        M, N = g["M"][:, ci * P:(ci + 1) * P], g["N"][:, ci * P:(ci + 1) * P]
        ready = [g["t"], self.state_at]
        if not final:
            if first:
                new = self.copy("dve", s_next, N, g["t"], c.last("pe"))
            else:
                bi, bank, free = self.bank.take()
                t = self.mm(bank[:, 0:P], M, s, True, True, ready, free, signal=True)
                new = self.stt(s_next, bank[:, 0:P], st["gain"][:, 20 + n:21 + n], N, ALU.mult, ALU.add, t, self.y_read)
                self.bank.read(bi, new)
        if n >= 2:
            bi, bank, free = self.bank.take()
            t = self.mm(bank[:, 0:P], g["WT"][:, ci * P:(ci + 1) * P], s, True, True, ready, free, signal=True)
            u = g["U"][:, ci * P:(ci + 1) * P]
            t = self.tt(u, g["WU"][:, ci * 256 + P:ci * 256 + 256], bank[:, 0:P], ALU.subtract, t)
            self.bank.read(bi, t)
            yield
            bi, bank, free = self.bank.take()
            self.y_read = self.mm(bank[:, 0:P], kr[:, n, 1, :], s, True, False, free, signal=True)
            for h in range(2):
                uu = 2 * ci + h
                cols = slice(h * HEAD, (h + 1) * HEAD)
                self.mm(bank[:, cols], g["agbh"][:, uu, 384:512], self.vtok[:, n, j * P + h * HEAD:j * P + (h + 1) * HEAD],
                        False, False)
                y = self.mm(bank[:, cols], g["agbh"][:, uu, 128:256], u[:, cols], False, h == 1, t, signal=(h == 1))
            dst = self.yacc[:, n - 2, j * P:(j + 1) * P]
            if fwd:
                t = self.copy("act", dst, bank[:, 0:P], y)
            else:
                t = self.tt(dst, dst, bank[:, 0:P], ALU.add, y)
            self.bank.read(bi, t)
        if not final:
            self.state_at = new
        yield

    def rwkv_output(self, yacc, bonus, g2, lora_ready):
        c, sb, io = self.c, self.sb, self.io
        c.new_phase()
        sb.at = self.hT_at
        yrT_at = sb.at
        self.yrT = sb.take(4 * SEQ, j=4)
        lnw, lnb = sb.take(RW), sb.take(RW)
        stat = sb.take(128)
        bv = sb.take(NT * RW)
        sq = self.sb.t[:, self.rwkv_keep + 200:self.rwkv_keep + 200 + 4096]
        got = [c.dma("act", "lnx", t, io[n].partition_broadcast(P)[:, 0, :], c.everything()) for n, t in (("ln_x_w", lnw), ("ln_x_b", lnb))]
        y = yacc.rearrange("p i (h f) -> p (i h) f", f=HEAD)
        s3 = sq.rearrange("p (g f) -> p g f", f=HEAD)
        mean, var = stat[:, 0:64], stat[:, 64:128]
        bc = lambda x: x.unsqueeze(2).broadcast_to([P, 64, HEAD])
        for i in range(NT):
            b_t = self.tt(bv[:, i * RW:(i + 1) * RW].rearrange("p (h f) -> p h f", f=HEAD),
                          self.vtok[:, 2 + i, :].rearrange("p (h f) -> p h f", f=HEAD),
                          bonus[:, i, :].unsqueeze(2).broadcast_to([P, 8, HEAD]), ALU.mult, eng="pool", loose=(i > 0))
        t = c.put("dve", lambda e: e.tensor_reduce(mean, y, AX.X, ALU.add))
        self.ts(mean, mean, 1.0 / HEAD, None, ALU.mult, ALU.bypass)
        t = self.tt(y, y, bc(mean), ALU.subtract)
        t = self.act(s3, y, ACT.Square, t)
        c.put("dve", lambda e: e.tensor_reduce(var, s3, AX.X, ALU.add), t)
        self.rstd(var, var, HEAD, 64e-5)
        self.tt(y, y, bc(var), ALU.mult)
        row = lambda x: x.unsqueeze(1).broadcast_to([P, NT, RW])
        self.tt(yacc, yacc, row(lnw), ALU.mult, got[-1])
        self.tt(yacc, yacc, row(lnb), ALU.add)
        self.tt(yacc, yacc, bv.rearrange("p (i f) -> p i f", f=RW), ALU.add, b_t)
        for i in range(NT):
            bi, bank, free = self.bank.take()
            t = self.mm(bank, self.gl[0:GATE, i * P:(i + 1) * P], g2[0:GATE, :], True, True, lora_ready, free, signal=True)
            gated = self.tt(yacc[:, i, :], yacc[:, i, :], bank, ALU.mult, t)
            self.bank.read(bi, gated)
            if i % 4 == 3:
                g = i // 4
                self.turn_rows(lambda i: yacc[:, i, :], range(4 * g, 4 * g + 4),
                               lambda j, bank, t_: self.copy("act", self.yrT[:, j, g * 512:(g + 1) * 512], bank, t_, loose=True),
                               gated, kt=4)
        self.yr_ready = [c.last("act"), c.last("dve")]

    def gate_row(self, out, col, gain):
        c = self.c
        for half in range(2):
            bi, bank, free = self.bank.take()
            for j in range(4):
                jj = 4 * half + j
                t = self.stt(self.diag[:, j * P:(j + 1) * P], self.ident, col[:, jj:jj + 1],
                             gain[:, jj:jj + 1].broadcast_to([P, P]), ALU.mult, ALU.mult, c.last("pe"), c.last("act"))
            t = self.mm(bank, self.ones, self.diag, True, True, t, free, signal=True)
            t = self.act(out[:, half * 512:(half + 1) * 512], bank, ACT.Copy, t)
            self.bank.read(bi, t)
        return t

    def rows_product(self, lhs, w_dram, tiles, evac, finish, ready, rows=None):
        c = self.c
        halves = [self.w_block(w_dram, n * 512, 512) for n in range(2)]
        for i in range(tiles):
            m = P if rows is None else rows(i)
            for n, (wi, w, got) in enumerate(halves):
                bi, bank, free = self.bank.take()
                for k in range(KD):
                    t = self.mm(bank[0:m, :], lhs(k, i), w[:, k, :], k == 0, k == KD - 1, got, free, ready(i),
                                signal=(k == KD - 1))
                self.bank.read(bi, evac(n, i, bank[0:m, :], t))
            finish(i)
        for wi, _, _ in halves:
            self.weights.read(wi, c.last("pe"))

    def post_norm(self, y, x, ssq, row, i, ready):
        self.stt(y[:, i, :], y[:, i, :], ssq[:, i:i + 1], row, ALU.mult, ALU.mult, ready)
        return self.tt(x[:, i, :], x[:, i, :], y[:, i, :], ALU.add)

    def mix_out(self):
        c, sb, io = self.c, self.sb, self.io
        c.new_phase()
        for i in range(self.w_slots):
            self.weights.read(i, *c.everything())
        sb.at = self.hT_at + 4 * SEQ
        ydT = sb.take(4 * SEQ, h=4)
        back = c.dma("act", "load_yd", ydT, self.yd_dram, c.everything(), self.yd_spilled)
        self.h2T_at = self.hT_at + KF * L2
        y = sb.take(NT * D, i=NT)
        row1 = sb.take(D)
        self.diag = sb.take(512)
        ssq = sb.take(3 * NT)
        junk = sb.take(512)
        gs2 = sb.take(KD)
        xs = Ring([sb.take(D) for _ in range(3)])
        assert sb.at <= self.h2T_at
        x_dram = io["x"][0].rearrange("(i p) d -> p i d", p=P)
        loaded = {}

        def load(i):
            xi, xr, free = xs.take()
            loaded[i] = xi, xr, c.dma("act", f"load_x{xi}", xr, x_dram[:, i, :], free)

        for i in range(3):
            load(i)
        row_t = self.gate_row(row1, self.mod[:, 16:24], self.col["g_post_mix"])

        self.stt(gs2, self.mod[:, 32:40], 1.0, self.col["g_pre_ffn"], ALU.add, ALU.mult)
        sh2 = self.mod[:, 24:32]
        self.h2T = sb.view(self.h2T_at, KD * SEQ, k=KD)
        self.x1_dram = self.nc.dram_tensor("x1_spill", (P, NT, D), F32).ap()

        def evac(n, i, bank, t):
            a = self.copy("dve", y[:, i, n * 512:(n + 1) * 512], bank, t, loose=True)
            self.act(junk, y[:, i, n * 512:(n + 1) * 512], ACT.Square, a, accum=ssq[:, n * NT + i:n * NT + i + 1])
            return a

        def finish(i):
            r = ssq[:, 2 * NT + i:2 * NT + i + 1]
            self.tt(r, ssq[:, i:i + 1], ssq[:, NT + i:NT + i + 1], ALU.add, c.last("act"))
            self.rstd(r, r, D, 1e-6)
            self.stt(y[:, i, :], y[:, i, :], r, row1, ALU.mult, ALU.mult, row_t)
            xi, x, gotx = loaded[i]
            t = self.tt(x, x, y[:, i, :], ALU.add, gotx)
            self.x1_spilled = c.dma("sp", "spill_x1", self.x1_dram[:, i, :], x, t)
            t = self.act(y[:, i, :], x, ACT.Square, t, accum=r)
            self.rstd(r, r, D, 1e-6, t)
            t = self.ts(y[:, i, :], x, r, None, ALU.mult, ALU.bypass)
            xs.read(xi, t, self.x1_spilled)
            if i + 3 < NT:
                load(i + 3)
            if i % 4 != 3:
                return
            g = i // 4

            def emit(j, bank, t):
                out = self.h2T[:, j, g * 512:(g + 1) * 512]
                if j % 2:
                    return self.act(out, bank, ACT.Identity, t, scale=gs2[:, j:j + 1], bias=sh2[:, j:j + 1], loose=True)
                return self.ts(out, bank, gs2[:, j:j + 1], sh2[:, j:j + 1], ALU.mult, ALU.add, t, loose=True)
            self.turn_rows(lambda n: y[:, n, :], range(4 * g, 4 * g + 4), emit, t)

        yT = lambda k, i: (self.yrT if k < 4 else ydT)[:, k % 4, i * P:(i + 1) * P]
        self.rows_product(yT, io["w_out"][0], NT, evac, finish, lambda i: [self.yr_ready, back])
        self.h2_ready = [c.last("act"), c.last("dve")]

    def mlp(self):
        c, sb, io = self.c, self.sb, self.io
        c.new_phase()
        sb.at = self.hT_at
        hid = sb.take(KF * L2, k=KF)
        assert sb.at <= self.h2T_at
        sb.at = self.h2T_at + KD * SEQ
        raws = Ring([sb.take(SEQ + 2) for _ in range(2)])
        cv, cg = sb.take(SEQ), sb.take(SEQ)
        for raw in raws.slots:
            pads = [self.fill(raw[:, n:n + 1], 0.0) for n in (0, SEQ + 1)]
        h2T = lambda k, a, b: self.h2T[:, k, a:b]
        w_up = io["w_up"][0]

        def conv(out, raw, tile):
            taps = [self.col[f"fconv{t}"][:, tile:tile + 1] for t in range(3)]
            self.ts(out, raw[:, 1:1 + SEQ], taps[1], self.col["ffn_conv_b"][:, tile:tile + 1], ALU.mult, ALU.add,
                    c.last("act"), pads)
            self.stt(out, raw[:, 0:SEQ], taps[0], out, ALU.mult, ALU.add)
            return self.stt(out, raw[:, 2:2 + SEQ], taps[2], out, ALU.mult, ALU.add)

        for blk in range(KF // 2):
            def parts(slot, blk=blk):
                v = slot.rearrange("p (k n) -> p k n", n=512)
                src = lambda c0: w_up[:, c0:c0 + 256].rearrange("(k p) n -> p k n", p=P)
                yield v[:, :, 0:256], src(blk * 256)
                yield v[:, :, 256:512], src(FF + blk * 256)
            wi, slot, got = self.load_block(parts)
            w = slot.rearrange("p (k n) -> p k n", n=512)
            for half in range(2):
                tile = 2 * blk + half
                for gate, dst in ((0, cv), (1, cg)):
                    ri, raw, free = raws.take()
                    c0 = 256 * gate + P * half
                    self.product(lambda k: w[:, k, c0:c0 + P], h2T, [(0, 512), (512, 1024)], KD, P, [got, self.h2_ready],
                                 lambda s, bank, t: self.copy("act", raw[:, 1 + s * 512:1 + (s + 1) * 512], bank, t, free, loose=True))
                    t = conv(dst, raw, tile + gate * KF)
                    raws.read(ri, t)
                t = self.act(cg, cg, ACT.Silu, t)
                t = self.tt(hid[:, tile, META:L2], cv, cg, ALU.mult, t)
            self.weights.read(wi, c.last("pe"))

        y = sb.view(self.h2T_at, NT * D, i=NT)
        up_done = c.everything()
        c.new_phase()
        sb.at = self.h2T_at + KD * SEQ
        xt = Ring([sb.take(D) for _ in range(2)])
        row2, small = sb.take(D), sb.take(D)
        ssq, junk = small[:, 0:3 * NT], small[:, 32:32 + 512]
        self.diag = xt.slots[0][:, 0:512]
        meta = xt.slots[1]
        row_t = self.gate_row(row2, self.mod[:, 40:48], self.col["g_post_ffn"])
        xt.read(0, c.last("pe"))
        self.hcT = hid[:, 0:KD, :]
        self.x2_dram = self.nc.dram_tensor("x2_spill", (P, NT, D), F32).ap()

        def evac(n, i, bank, t):
            a = self.copy("dve", y[:, i, n * 512:(n + 1) * 512], bank, t, loose=True)
            self.act(junk, y[:, i, n * 512:(n + 1) * 512], ACT.Square, a, accum=ssq[:, n * NT + i:n * NT + i + 1])
            return a

        def load(i):
            xi, x, free = xt.take()
            return xi, x, c.dma("sp", f"load_x1_{xi}", x, self.x1_dram[:, i, :], free, self.x1_spilled, up_done)

        held = [self.bank.take() for _ in range(NT)]
        for k0 in range(0, KF, KD):
            kn = min(KD, KF - k0)
            wi, w, got = self.w_block(io["w_down"][0], 0, 512, k0=k0, k=kn)
            for i in range(NT):
                bi, bank, free = held[i]
                for k in range(kn):
                    t = self.mm(bank, hid[:, k0 + k, META + i * P:META + (i + 1) * P], w[:, k, :], k0 + k == 0, k0 + k == KF - 1,
                                got, free, signal=(k == kn - 1))
                if k0 + kn == KF:
                    self.bank.read(bi, evac(0, i, bank, t))
            self.weights.read(wi, c.last("pe"))
        blocks = [(k0, *self.w_block(io["w_down"][0], 512, 512, k0=k0, k=min(KD, KF - k0))) for k0 in range(0, KF, KD)]
        gm = c.dma("sp", "load_meta", meta[0:META, :], io["meta_2"], up_done)
        pend = None

        def finish(i, xi, x, back):
            r = ssq[:, 2 * NT + i:2 * NT + i + 1]
            self.tt(r, ssq[:, i:i + 1], ssq[:, NT + i:NT + i + 1], ALU.add, c.last("act"))
            self.rstd(r, r, D, 1e-6)
            self.stt(y[:, i, :], y[:, i, :], r, row2, ALU.mult, ALU.mult, row_t)
            t = self.tt(x, x, y[:, i, :], ALU.add, back)
            self.x2_spilled = c.dma("sp", "spill_x2", self.x2_dram[:, i, :], x, t)
            return t

        def turn_tile(i, xi, x, t):
            self.turn_tile(self.hcT, META + i * P, x, P, t, down[i])
            xt.read(xi, c.last("pe"), self.x2_spilled)

        down = {}
        t_meta = None
        for i in range(NT):
            bi, bank, free = self.bank.take()
            for k0, wi, w, got in blocks:
                for k in range(w.shape[1]):
                    t = self.mm(bank, hid[:, k0 + k, META + i * P:META + (i + 1) * P], w[:, k, :], k0 + k == 0, k0 + k == KF - 1,
                                got, free, signal=(k0 + k == KF - 1))
            down[i] = t
            self.bank.read(bi, evac(1, i, bank, t))
            if i == 0:
                self.turn_tile(self.hcT, 0, meta, META, gm, None)
                xt.read(1, c.last("pe"))
            if pend:
                turn_tile(*pend)
            xi, x, back = load(i)
            pend = (i, xi, x, finish(i, xi, x, back))
        turn_tile(*pend)
        for _, wi, _, _ in blocks:
            self.weights.read(wi, down[NT - 1])
        self.hcT_ready = [c.last("act"), c.last("dve")]

    def turn_tile(self, out, col, rows, m, *after):
        for half in range(2):
            bi, bank, free = self.bank.take()
            for j in range(4):
                t = self.turn(bank[:, j * m:(j + 1) * m], rows[0:m, (4 * half + j) * P:(4 * half + j + 1) * P],
                              self.ident[0:m, 0:m], free, *after, signal=(j == 3))
            self.bank.read(bi, self.copy("act" if half else "dve", out[:, 4 * half:4 * half + 4, col:col + m],
                                         bank[:, 0:4 * m].rearrange("p (k t) -> p k t", k=4), t, *after, loose=True))


    def conformer(self):
        c, sb, io = self.c, self.sb, self.io
        SP = self.spans2 = [(0, 352), (352, 696), (696, L2)]
        c.new_phase()
        for e in ("pe", "dve", "act", "pool"):
            c.held[e].append(self.x2_spilled)
        before = [*c.everything(), self.x2_spilled]
        sb.at = self.hT_at + KD * L2
        conv, zs = sb.take(KD * L2, k=KD), sb.take(KD * L2, k=KD)
        glu_at = sb.at
        glus = Ring([sb.take(L2 + TAPS - 1) for _ in range(3)])
        sig = Ring([sb.take(L2) for _ in range(2)])
        xs = Ring([sb.take(D) for _ in range(3)])
        brow, grow, lrow = (sb.take(D) for _ in range(3))
        self.ln_stat = sb.take(64)
        x2_row = lambda i: (io["meta_2"], META) if i == NT else (self.x2_dram[:, i, :], P)
        loaded = {}

        def load(i, *after):
            xi, x, free = xs.take()
            src, m = x2_row(i)
            loaded[i] = xi, x, c.dma("act", f"load_x2_{xi}", x[0:m, :], src, free, *after)

        c.dma("act", "rows2", brow, io["conv_b_out_2"].partition_broadcast(P)[:, 0, :], before)
        c.dma("act", "rows2", grow, io["post_ln_g_2"][0:1].partition_broadcast(P)[:, 0, :])
        rows_got = c.dma("act", "rows2", lrow, io["post_ln_b_2"][0:1].partition_broadcast(P)[:, 0, :])
        for i in range(3):
            load(i, before)
        for g in glus.slots:
            pad = self.fill(g[:, 0:TAPS - 1], 0.0)
        hT = lambda k, a, b: self.hcT[:, k, a:b]
        w_in = io["conv_w_in_2"][0]
        b_in = self.col["conv_b_in"]
        dw = lambda r: self.col["dw_a"][:, r:r + 1] if r < 124 else self.col["dw_b"][:, r - 124:r - 123]
        self.banks(5)
        held = [self.ps[:, (5 + s) * BANK:(5 + s) * BANK + b - a] for s, (a, b) in enumerate(SP)]

        conv_done = {}

        def channel_sum(k):
            for s, (a, b) in enumerate(SP):
                t = self.mm(held[s], self.ones, conv[:, k, a:b], k == 0, k == KD - 1, conv_done[k], signal=True)
            return t

        def glu_conv(j):
            def parts(slot):
                v = slot[:, 0:KD * 256].rearrange("p (k n) -> p k n", n=256)
                for part in range(2):
                    c0 = (1 - part) * D + j * P
                    yield v[:, :, part * P:(part + 1) * P], w_in[:, c0:c0 + P].rearrange("(k p) n -> p k n", p=P)
            wi, slot, got = self.load_block(parts)
            w = slot[:, 0:KD * 256].rearrange("p (k n) -> p k n", n=256)
            si, s1, sfree = sig.take()
            gi, glu, gfree = glus.take()

            def gate(s, bank, t):
                a, b = SP[s]
                return self.act(s1[:, a:b], bank, ACT.Sigmoid, t, sfree, bias=b_in[:, 8 + j:9 + j])

            def value(s, bank, t):
                a, b = SP[s]
                t = self.stt(glu[:, TAPS - 1 + a:TAPS - 1 + b], bank, b_in[:, j:j + 1], s1[:, a:b], ALU.add, ALU.mult, t,
                             c.last("act"), gfree, pad, loose=True)
                sig.read(si, t)
                return t

            for part, emit in enumerate((gate, value)):
                self.product(lambda k: w[:, k, part * P:(part + 1) * P], hT, SP, KD, P, [got, self.hcT_ready], emit)
            self.weights.read(wi, c.last("pe"))
            o = conv[:, j, :]
            self.ts(o, glu[:, 0:L2], dw(j), self.col["conv_b_dw"][:, j:j + 1], ALU.mult, ALU.add)
            for tap in range(1, TAPS):
                t = self.stt(o, glu[:, tap:tap + L2], dw(tap * KD + j), o, ALU.mult, ALU.add)
            glus.read(gi, t)
            conv_done[j] = t

        zw = {}

        def z_gate(j):
            if j % 2 == 0:
                zw[0] = self.w_block(w_in, 2 * D + j * P, 256)
            wi, w, got = zw[0]

            def zgate(s, bank, t):
                a, b = SP[s]
                return self.act(zs[:, j, a:b], bank, ACT.Silu, t, bias=b_in[:, 16 + j:17 + j], loose=True)

            self.product(lambda k: w[:, k, (j % 2) * P:(j % 2 + 1) * P], hT, SP, KD, P, [got], zgate)
            if j % 2:
                self.weights.read(wi, c.last("pe"))

        for j in range(KD):
            glu_conv(j)
            if 2 <= j < 7:
                z_gate(j - 2)
            if j > 2:
                channel_sum(j - 3)
        for j in range(5, KD):
            z_gate(j)
        for k in range(5, KD):
            mean_done = channel_sum(k)

        mean, rs = sig.slots
        sq = sb.view(glu_at, KD * 352, k=KD)
        h_done = c.last("pe")
        span_ready = []
        wide = lambda row, a, b: row[:, a:b].unsqueeze(1).broadcast_to([P, KD, b - a])
        squared = {}

        def centre(s):
            a, b = SP[s]
            o = conv[:, :, a:b]
            t = self.act(mean[:, a:b], held[s], ACT.Copy, mean_done, taps_done, scale=1.0 / D, loose=True)
            t = self.tt(o, o, wide(mean, a, b), ALU.subtract, t)
            t = self.act(sq[:, :, 0:b - a], o, ACT.Square, t, squared.get(s - 1), taps_done, loose=True)
            for k in range(KD):
                squared[s] = self.mm(held[s], self.ones, sq[:, k, 0:b - a], k == 0, k == KD - 1, t, signal=(k == KD - 1))

        def scale(s):
            a, b = SP[s]
            self.ts(rs[:, a:b], held[s], 1.0 / D, 1e-5, ALU.mult, ALU.add, squared[s])
            t = self.act(rs[:, a:b], rs[:, a:b], ACT.Sqrt, c.last("dve"))
            self.recip(rs[:, a:b], rs[:, a:b], t)
            o = conv[:, :, a:b]
            t = self.tt(o, o, wide(rs, a, b), ALU.mult)
            for k in range(KD):
                t = self.act(conv[:, k, a:b], conv[:, k, a:b], ACT.Silu, t, scale=self.col["conv_norm_g"][:, k:k + 1],
                             bias=self.col["conv_norm_b"][:, k:k + 1], loose=True)
            return t

        def gated(s, t):
            a, b = SP[s]
            o = conv[:, :, a:b]
            span_ready.append(self.tt(o, o, zs[:, :, a:b], ALU.mult, t))

        taps_done = c.last("dve")
        for s in range(3):
            centre(s)
        scaled = [scale(0), scale(1)]
        gated(0, scaled[0])
        scaled.append(scale(2))
        gated(1, scaled[1])
        gated(2, scaled[2])

        self.h1T = sb.view(self.hT_at, KD * L2, k=KD)
        self.h1_dram = self.nc.dram_tensor("h1_spill", (P, NT, D), F32).ap()
        pend = []

        def evac(n, i, bank, t):
            xi, x, gotx = loaded[i]
            r = x[0:bank.shape[0], n * 512:(n + 1) * 512]
            self.stt(r, r, DN_ALPHA, brow[0:bank.shape[0], n * 512:(n + 1) * 512], ALU.mult, ALU.add, gotx, rows_got)
            return self.tt(r, r, bank, ALU.add, t)

        def turn_last():
            i, xi, x, t = pend.pop()
            m = META if i == NT else P
            self.turn_tile(self.h1T, 0 if i == NT else META + i * P, x, m, t, h_done)
            xs.read(xi, c.last("pe"), self.h1_spilled if i < NT else None)
            if i + 3 <= NT:
                load(i + 3)

        def finish(i):
            xi, x, _ = loaded[i]
            m = META if i == NT else P
            t = self.layer_norm(x[0:m, :], grow, lrow, m)
            if i < NT:
                self.h1_spilled = c.dma("sp", "spill_h1", self.h1_dram[:, i, :], x, t)
            if pend:
                turn_last()
            pend.append((i, xi, x, t))

        self.rows_product(lambda k, i: conv[:, k, META + i * P:META + (i + 1) * P] if i < NT else conv[:, k, 0:META],
                          io["conv_w_out_2"][0], NT + 1, evac, finish,
                          lambda i: [span_ready[0 if i == NT else next(s for s, (a, b) in enumerate(SP) if b >= META + (i + 1) * P)]],
                          rows=lambda i: P if i < NT else META)
        turn_last()
        self.h1_ready = [c.last("act"), c.last("dve")]
        self.banks(8)

    def layer_norm(self, r, grow, lrow, m, *rows_ready):
        c = self.c
        st = self.ln_stat[0:m]
        for n in range(2):
            c.put("dve", lambda e, n=n: e.bn_stats(st[:, 6 * n:6 * n + 6], r[:, n * 512:(n + 1) * 512]), c.last("act"))
        c.put("dve", lambda e: e.bn_aggr(st[:, 12:14], st[:, 0:12]))
        self.ts(st[:, 14:15], st[:, 13:14], 1e-5, None, ALU.add, ALU.bypass)
        t = self.act(st[:, 14:15], st[:, 14:15], ACT.Sqrt, c.last("dve"))
        self.recip(st[:, 15:16], st[:, 14:15], t)
        self.ts(r, r, st[:, 12:13], st[:, 15:16], ALU.subtract, ALU.mult)
        self.tt(r, r, grow[0:m, :], ALU.mult, *rows_ready)
        return self.tt(r, r, lrow[0:m, :], ALU.add)

    def gla(self):
        c, sb, io = self.c, self.sb, self.io
        NCH = (L2 + P - 1) // P
        LP = NCH * P
        HALF = KD * 256
        c.new_phase()
        for e in ("pe", "dve", "act", "pool"):
            c.held[e].append(self.h1_spilled)
        start = c.everything()
        slots = [sb.view(self.w_at + i * HALF, HALF) for i in range(4)]
        self.weights = Ring(slots)
        for i in range(4):
            self.weights.read(i, *start)
        sb.at = self.w_at + 4 * HALF
        a1, wa2, junk, soft = sb.take(L2), sb.take(GH * P), sb.take(GV), sb.take(L2)
        assert sb.at <= self.w_at + self.w_slots * SLOT
        sb.at = self.hT_at + KD * L2
        q, k = sb.take(GH * LP, h=GH), sb.take(GH * LP, h=GH)
        oT = lambda kk: (q if kk % 2 == 0 else k)[:, kk // 2, :]
        rows_at = sb.at
        e_, qx, kx = sb.take(LP), sb.take(LP), sb.take(LP)
        norm_at = sb.at
        b = [sb.take(LP) for _ in range(2)]
        qd, kt = sb.take(LP), sb.take(LP, i=NCH)
        A = [sb.take(LP, i=NCH) for _ in range(2)]
        v = [sb.take(NCH * GV, i=NCH) for _ in range(2)]
        o = sb.take(NCH * GV, i=NCH)
        S = [sb.take(GV) for _ in range(2)]
        last_b = [sb.take(NCH) for _ in range(2)]
        st = sb.take(NCH)
        gate_r = [sb.take(L2) for _ in range(2)]
        chunks = lambda x: x.rearrange("p (n t) -> p n t", t=P)
        blocks = lambda x, m: x.rearrange("p (n j) -> p n j", j=2 * m)
        sets = ((0, 4), (4, 8), (8, 9))
        SP = self.spans2
        h1T = lambda kk, x, y: self.h1T[:, kk, x:y]
        w_in = io["gla_w_in_2"][0]
        rows_of = lambda n: P if (n + 1) * P <= L2 else L2 - n * P
        for t in (q, k):
            self.fill(t[:, :, L2:LP], 0.0)
        for t in (b[0], b[1]):
            self.fill(t[:, L2:LP], 0.0)
        for t in (A[0], A[1], qx, kx):
            padded = self.fill(t, 0.0)
        gw = c.dma("act", "gla_a2", wa2[0:16, :], io["gla_w_a2_2"][0], start)

        def qk_steps(h):
            def parts(slot):
                s = slot.rearrange("p (k n) -> p k n", n=256)
                for part in range(2):
                    c0 = part * 512 + h * P
                    yield s[:, :, part * P:(part + 1) * P], w_in[:, c0:c0 + P].rearrange("(k p) n -> p k n", p=P)
            wi, slot, got = self.load_block(parts)
            w = slot.rearrange("p (k n) -> p k n", n=256)

            def step(part, s):
                dst, scale = ((q, GK ** -0.5), (k, 1.0))[part]
                self.product(lambda kk: w[:, kk, part * P:(part + 1) * P], h1T, [SP[s]], KD, P, [got, self.h1_ready],
                             lambda _, bank, t: self.act(dst[:, h, SP[s][0]:SP[s][1]], bank, ACT.Copy, t, scale=scale, loose=True))
                if (part, s) == (1, 2):
                    self.weights.read(wi, c.last("pe"))
                    q_ready[h] = c.last("act")
            return [lambda part=part, s=s: step(part, s) for part in range(2) for s in range(3)]

        def v_steps(h):
            wi, w, got = self.w_block(w_in, 1024 + h * GV, GV)

            def step(i):
                m = rows_of(i)
                bi, bank, free = self.bank.take()
                for kk in range(KD):
                    t = self.mm(bank[0:m, 0:GV], self.h1T[:, kk, i * P:i * P + m], w[:, kk, :], kk == 0, kk == KD - 1, got, free,
                                signal=(kk == KD - 1))
                v_ready[h] = self.copy("dve" if i % 2 else "act", v[h % 2][0:m, i, :], bank[0:m, 0:GV], t, o_done.get(h - 2), loose=True)
                self.bank.read(bi, v_ready[h])
                if i == NCH - 1:
                    v_ready[h] = [c.last("act"), c.last("dve")]
                    self.weights.read(wi, c.last("pe"))
            return [lambda i=i: step(i) for i in range(NCH)]

        def r_steps(h):
            wi, w, got = self.w_block(w_in, 2048 + h * GV, GV)

            def step(j, s):
                x, y = SP[s]
                self.product(lambda kk: w[:, kk, j * P:(j + 1) * P], h1T, [(x, y)], KD, P, [got],
                             lambda _, bank, t: self.act(gate_r[j][:, x:y], bank, ACT.Silu, t, gated.get(h - 1), loose=True))
                if (j, s) == (1, 2):
                    self.weights.read(wi, c.last("pe"))
                    r_ready[h] = c.last("act")
            return [lambda j=j, s=s: step(j, s) for j in range(2) for s in range(3)]

        def gate_step(h):
            bh, ba = b[h % 2], self.col["gla_b_a"][:, h:h + 1]
            for x, y in SP:
                bi, bank, free = self.bank.take()
                bk = bank[:, 0:y - x]
                t = self.mm(bk, wa2[0:16, h * P:(h + 1) * P], a1[0:16, x:y], True, True, gw, a1_ready, free, signal=True)
                t2 = self.ts(bh[:, x:y], bk, ba, 0.0, ALU.add, ALU.min, t)
                t = self.act(soft[:, x:y], bk, ACT.Abs, t, t2, bias=ba)
                self.bank.read(bi, t, t2)
            self.act(soft, soft, ACT.Exp, scale=-1.0)
            t = self.act(soft, soft, ACT.Ln, bias=1.0)
            self.tt(bh[:, 0:L2], bh[:, 0:L2], soft, ALU.subtract, t)
            for n in range(NCH):
                t = c.put("dve", lambda e, x=chunks(bh)[:, n, :]: e.tensor_tensor_scan(x, self.ones, x, 0.0, ALU.mult, ALU.add),
                          padded, loose=(n > 0))
            b_ready[h] = t

        def factors(h, li):
            bh, qh, kh, m = b[h % 2], q[:, h, :], k[:, h, :], LEVELS[li - 1]
            ref = blocks(bh, m)[:, :, m - 1:m].broadcast_to([P, LP // (2 * m), m])
            bb, ee = blocks(bh, m), blocks(e_, m)
            self.tt(ee[:, :, m:], bb[:, :, m:], ref, ALU.subtract, e_read[0])
            t = self.tt(ee[:, :, 0:m], ref, bb[:, :, 0:m], ALU.subtract, loose=True)
            t = self.act(e_, e_, ACT.Exp, t, scale=1.0 / 16)
            self.tt(blocks(qx, m)[:, :, m:], blocks(qh, m)[:, :, m:], ee[:, :, m:], ALU.mult, t, padded, x_read[0], q_ready[h], loose=True)
            return self.tt(blocks(kx, m)[:, :, 0:m], blocks(kh, m)[:, :, 0:m], ee[:, :, 0:m], ALU.mult, loose=True)

        def level(h, li):
            Ah = A[h % 2]
            if li:
                lq, lk, mask, t = qx, kx, self.level["upper"][:, li - 1, :], x_ready[0]
            else:
                lq, lk, mask, t = q[:, h, :], k[:, h, :], self.ident, [q_ready[h], padded]
            held = []
            for x, y in sets:
                bi, bank, free = self.bank.take()
                for n in range(x, y):
                    tt = self.mm(bank[:, (n - x) * P:(n - x + 1) * P], chunks(lk)[:, n, :], chunks(lq)[:, n, :], True, True,
                                 t, free, signal=(n == y - 1))
                held.append((x, y, bi, bank, tt))
            x_read[0] = tt
            if li < len(LEVELS):
                x_ready[0] = factors(h, li + 1)
            for x, y, bi, bank, tt in held:
                w_ = y - x
                tt = c.put("dve", lambda e, out=Ah[:, x:y, :], mk=mask.bitcast(I32).unsqueeze(1).broadcast_to([P, w_, P]),
                           dat=bank[:, 0:w_ * P].rearrange("p (n t) -> p n t", t=P): e.copy_predicated(out, mk, dat), tt,
                           o_done.get(h - 2), padded)
                self.bank.read(bi, tt)
            A_ready[h] = tt

        def decays(h):
            bh, qh, kh = b[h % 2], q[:, h, :], k[:, h, :]
            last = chunks(bh)[:, :, P - 1:P]
            t = self.act(e_, bh, ACT.Exp, c.last("dve"), scale=1.0 / 16)
            self.tt(qd, qh, e_, ALU.mult, t, o_done.get(h - 1))
            self.copy("dve", last_b[h % 2], chunks(e_)[:, :, P - 1], loose=True)
            t = self.tt(chunks(e_), last.broadcast_to([P, NCH, P]), chunks(bh), ALU.subtract)
            t = self.act(e_, e_, ACT.Exp, t, scale=1.0 / 16)
            decayed[h] = e_read[0] = self.tt(kx, kh, e_, ALU.mult, t, x_read[0])

        def keys_step(h):
            for x, y in sets:
                bi, bank, free = self.bank.take()
                for n in range(x, y):
                    t = self.turn(bank[:, (n - x) * P:(n - x + 1) * P], chunks(kx)[:, n, :], self.ident, decayed[h], free, signal=(n == y - 1))
                x_read[0] = t
                kt_ready[h] = self.copy("act", kt[:, x:y, :], bank[:, 0:(y - x) * P].rearrange("p (n t) -> p n t", t=P), t,
                                        o_done.get(h - 1), loose=True)
                self.bank.read(bi, kt_ready[h])

        def chunk_step(h, n):
            m = rows_of(n)
            vn = v[h % 2][0:m, n, :]
            bi, bank, free = self.bank.take()
            t = self.mm(bank[0:m, 0:GV], A[h % 2][0:m, n, 0:m], vn, True, n == 0, A_ready[h], v_ready[h], free, signal=True)
            if n:
                t = self.mm(bank[0:m, 0:GV], chunks(qd)[:, n, 0:m], S[n % 2], False, True, decayed[h], state[0], signal=True)
            o_done[h] = t
            tt = self.act(o[0:m, n, :], bank[0:m, 0:GV], ACT.Copy, t, o_turned.get(h - 1), loose=True)
            ssq_ready[0] = self.act(junk[0:m, :], bank[0:m, 0:GV], ACT.Square, t, o_scaled.get(h - 1), accum=st[0:m, n:n + 1])
            self.bank.read(bi, tt, ssq_ready[0])
            if n < NCH - 1:
                bi, bank, free = self.bank.take()
                t = self.mm(bank[:, 0:GV], kt[:, n, :], vn, True, True, kt_ready[h], free, signal=True)
                if n == 0:
                    state[0] = self.copy("dve", S[1], bank[:, 0:GV], t, loose=True)
                else:
                    state[0] = self.stt(S[(n + 1) % 2], S[n % 2], last_b[h % 2][:, n:n + 1], bank[:, 0:GV], ALU.mult, ALU.add, t,
                                        o_done[h])
                self.bank.read(bi, state[0])

        def norm_step(h):
            for m, x, y in ((P, 0, NCH - 1), (rows_of(NCH - 1), NCH - 1, NCH)):
                self.rstd(st[0:m, x:y], st[0:m, x:y], GV, 1e-6, ssq_ready[0])
            for n in range(NCH):
                m = rows_of(n)
                o_scaled[h] = self.ts(o[0:m, n, :], o[0:m, n, :], st[0:m, n:n + 1], None, ALU.mult, ALU.bypass, loose=(n > 0))

        def turn_step(h, half):
            out = oT(2 * h + half)
            for x, y in sets:
                bi, bank, free = self.bank.take()
                for n in range(x, y):
                    m = rows_of(n)
                    t = self.turn(bank[:, (n - x) * P:(n - x) * P + m], o[0:m, n, half * P:(half + 1) * P], self.ident[0:m, 0:m],
                                  o_scaled[h], free, signal=(n == y - 1))
                o_turned[h] = t
                a, z = x * P, min(L2, y * P)
                gated[h] = self.stt(out[:, a:z], bank[:, 0:z - a], self.col["gla_norm_g"][:, half:half + 1], gate_r[half][:, a:z],
                                    ALU.mult, ALU.mult, t, r_ready[h], loose=True)
                self.bank.read(bi, gated[h])

        xs = Ring([sb.view(rows_at + i * D, D) for i in range(3)])
        grow, lrow = sb.view(norm_at, D), sb.view(norm_at + D, D)
        loaded = {}

        def load(i, *after):
            xi, x, free = xs.take()
            loaded[i] = xi, x, c.dma("act", f"load_h1_{xi}", x, self.h1_dram[:, i, :], free, *after)

        def last_rows():
            free_now = c.everything()
            c.dma("act", "rows3", grow, io["post_ln_g_2"][1:2].partition_broadcast(P)[:, 0, :], free_now)
            loaded["norm"] = c.dma("act", "rows3", lrow, io["post_ln_b_2"][1:2].partition_broadcast(P)[:, 0, :])
            for i in range(3):
                load(i, free_now)

        q_ready, v_ready, r_ready, b_ready, kt_ready, decayed = {}, {}, {}, {}, {}, {}
        A_ready, o_done, o_scaled, o_turned, gated = {}, {}, {}, {}, {}
        e_read, x_read, x_ready, state, ssq_ready = [None], [None], [None], [None], [None]

        wi, w, got = self.w_block(w_in, 3072, 16)
        first = qk_steps(0)
        self.product(lambda kk: w[:, kk, 0:16], h1T, SP, KD, 16, [got, self.h1_ready],
                     lambda s, bank, t: self.copy("act", a1[0:16, SP[s][0]:SP[s][1]], bank, t, loose=True))
        self.weights.read(wi, c.last("pe"))
        a1_ready = c.last("act")
        gate_step(0)
        for step in first:
            step()
        for h in range(GH + 1):
            critical, filler = [], []
            if h < GH:
                filler += v_steps(h)
            if h + 1 < GH:
                filler += qk_steps(h + 1)
            if h:
                filler += r_steps(h - 1)
                critical.append(lambda: keys_step(h - 1))
            for n in range(NCH):
                if h < GH and n <= len(LEVELS):
                    critical.append(lambda n=n: level(h, n))
                if h:
                    critical.append(lambda n=n: chunk_step(h - 1, n))
                if n == 3 and h + 1 < GH:
                    critical.append(lambda: gate_step(h + 1))
            if h:
                critical.append(lambda: norm_step(h - 1))
            if h < GH:
                critical.append(lambda: decays(h))
            if h == GH:
                critical.insert(1, last_rows)
            spread = max(0, len(filler) - 3)
            done = 0
            for i, step in enumerate(critical):
                step()
                while done < spread * (i + 1) // len(critical):
                    filler[done]()
                    done += 1
            for step in filler[done:]:
                step()
            if h:
                for half in range(2):
                    turn_step(h - 1, half)
        ready = gated[GH - 1]

        readers = [t for r in self.weights.readers for t in r]
        self.weights = Ring([sb.view(self.w_at + i * SLOT, SLOT) for i in range(2)])
        for i in range(2):
            self.weights.read(i, *readers)
        def evac(n, i, bank, t):
            xi, x, got = loaded[i]
            r = x[:, n * 512:(n + 1) * 512]
            return self.stt(r, r, DN_ALPHA, bank, ALU.mult, ALU.add, t, got)

        out = io["out"][0].rearrange("(i p) d -> p i d", p=P)

        def finish(i):
            xi, x, _ = loaded[i]
            t = self.layer_norm(x, grow, lrow, P, loaded["norm"])
            xs.read(xi, c.dma("sp", f"out{xi}", out[:, i, :], x, t))
            if i + 3 < NT:
                load(i + 3)

        self.rows_product(lambda kk, i: oT(kk)[:, META + i * P:META + (i + 1) * P], io["gla_w_out_2"][0], NT, evac, finish,
                          lambda i: [ready])

def build(nc, io):
    with ExitStack() as ctx:
        k = Kernel(nc, io, ctx)
        k.open_weights()
        k.constants()
        k.modulation()
        k.first_norm()
        k.attention()
        k.rwkv_project()
        k.rwkv()
        k.mix_out()
        k.mlp()
        k.conformer()
        k.gla()
        k.c.emit()


NAMES = ["x", "c", "ctx", "c_ctx", "w_mod", "b_mod", "g_pre_mix", "g_post_mix", "g_pre_ffn", "g_post_ffn", "w_in",
         "rwkv_conv", "w0_fwd", "w2_fwd", "a0_fwd", "a2_fwd", "w0_bwd", "w2_bwd", "a0_bwd", "a2_bwd", "g2", "k_k",
         "k_a", "r_k", "ln_x_w", "ln_x_b", "lam_q1", "lam_k1", "lam_q2", "lam_k2", "subln_w", "w_out", "w_up",
         "ffn_conv", "ffn_conv_b", "w_down", "meta_2", "conv_w_in_2", "conv_b_in_2", "conv_w_dw_2", "conv_b_dw_2",
         "conv_norm_g_2", "conv_norm_b_2", "conv_w_out_2", "conv_b_out_2", "gla_w_in_2", "gla_w_a2_2", "gla_b_a_2",
         "gla_norm_g_2", "gla_w_out_2", "post_ln_g_2", "post_ln_b_2"]


def rope_tables():
    import numpy as np
    pairs = HEAD // 4
    row = np.repeat(np.arange(SEQ // 64, dtype=np.float32), 64)
    col = np.tile(np.arange(64, dtype=np.float32), SEQ // 64)
    inv = (np.float32(10000.0) ** (-np.arange(pairs, dtype=np.float32) / np.float32(pairs))).astype(np.float32)
    ang = np.concatenate([row[:, None] * inv, col[:, None] * inv], axis=-1)
    turn = np.zeros((P, P), np.float32)
    for p in range(P):
        if p % HEAD < HEAD // 2:
            turn[p + HEAD // 2, p] = -1.0
        else:
            turn[p - HEAD // 2, p] = 1.0
    tile = lambda t: np.ascontiguousarray(np.tile(t.T, (4, 1)).astype(np.float32))
    return {"rope_cos": tile(np.cos(ang)), "rope_sin": tile(np.sin(ang)), "rope_turn": turn}


def kernel(**inputs):
    import numpy as np
    import concourse.bacc as bacc
    from concourse.bass_utils import run_bass_kernel_spmd

    nc = bacc.Bacc("TRN2", target_bir_lowering=False, num_devices=1)
    arrays, io = {}, {}
    given = {n: np.ascontiguousarray(inputs[n]) for n in NAMES}
    given.update(rope_tables())
    for name, a in given.items():
        arrays[f"in_{name}"] = a
        io[name] = nc.dram_tensor(f"in_{name}", a.shape, mybir.dt.from_np(a.dtype), kind="ExternalInput").ap()
    io["out"] = nc.dram_tensor("out_y", (1, SEQ, D), F32, kind="ExternalOutput").ap()
    build(nc, io)
    r = run_bass_kernel_spmd(nc, [arrays], core_ids=[0])
    return r.results[0]["out_y"]
```
